# Optimizing a Trainium2 kernel written in Bass

```python
import math
import jax, jax.numpy as jnp
from jax import lax
import numpy as np

D_MODEL = 1024
BATCH = 1
SEQ = 128
DEPTH = 2
DEC_BATCH = 1
DEC_SEQ = 1024
PAST_LEN = 128

GRID_W = 64
N_RET_LAYERS = (DEPTH + 1) // 2
N_ATT_LAYERS = DEPTH // 2
HY_W = D_MODEL // 2
HY_EMB = 33
HY_BANDS = (HY_EMB - 1) // 2
HY_FF = 64
HY_TARGET = 1e-2
HY_FAST = 0.3
HY_SLOW = 1.5
RET_W = D_MODEL // 2
RET_HEADS = 4
RET_HEAD_DIM = RET_W // RET_HEADS
RET_CHUNK = 128
DIFF_HEADS = 8
DIFF_HEAD_DIM = D_MODEL // (2 * DIFF_HEADS)
Q_BLOCK = 128
ROPE_BASE = 10000.0
N_EXPERTS = 16
EC_FACTOR = 2
EXPERT_FF = 1024
EVEN_IN = 3 * HY_W + 4 * RET_W
EPS = 1e-6

kernel_name = "hyena_retnet_diffattn_ec_diffusion_step"

def rms_norm(x, g):
    xf = x.astype(jnp.float32)
    y = xf * lax.rsqrt(jnp.mean(xf * xf, axis=-1, keepdims=True) + EPS)
    return (y * g).astype(x.dtype)

def ada_modulation(cond, w, b):
    m = jax.nn.silu(cond) @ w + b
    m = m.reshape(cond.shape[:-1] + (1, 6, D_MODEL))
    return [m[..., i, :] for i in range(6)]

def short_conv3(x, w, b):
    xp = jnp.pad(x, ((0, 0), (1, 1), (0, 0)))
    return xp[:, :-2] * w[0] + xp[:, 1:-1] * w[1] + xp[:, 2:] * w[2] + b

def hyena_filters(L, f1w, f1b, fr1, f2w, f2b, fr2, f3w):
    pos = jnp.arange(L, dtype=jnp.float32)
    t = pos / (L - 1)
    w = 2.0 * math.pi * pos / L
    f = jnp.linspace(1e-4, HY_BANDS - 1, HY_BANDS, dtype=jnp.float32)
    wf = w[:, None] * f[None, :]
    feat = jnp.concatenate([t[:, None], jnp.cos(wf), -jnp.sin(wf)], axis=-1)
    h = jnp.sin(fr1 * (feat @ f1w + f1b))
    h = jnp.sin(fr2 * (h @ f2w + f2b))
    h = (h @ f3w).astype(jnp.float32).reshape(L, 2, 2, HY_W)
    deltas = jnp.linspace(math.log(HY_TARGET) / HY_SLOW, math.log(HY_TARGET) / HY_FAST, HY_W, dtype=jnp.float32)
    window = jnp.exp(-t[:, None] * jnp.abs(deltas)[None, :])
    h = h * window[:, None, None, :]
    h = h / (jnp.sum(jnp.abs(h), axis=(0, 2), keepdims=True) + EPS)
    fwd, bwd = h[:, :, 0], h[:, :, 1]
    kern = jnp.concatenate([fwd, jnp.zeros((1, 2, HY_W), jnp.float32), bwd[1:][::-1]], axis=0)
    return jnp.transpose(kern, (1, 0, 2))

def long_conv(z, kern, bias):
    L = z.shape[1]
    zf = z.astype(jnp.float32)
    Z = jnp.fft.rfft(zf, n=2 * L, axis=1)
    K = jnp.fft.rfft(kern, n=2 * L, axis=0)
    y = jnp.fft.irfft(Z * K[None], n=2 * L, axis=1)[:, :L]
    return (y + zf * bias).astype(z.dtype)

def hyena(u, short_w, short_b, f1w, f1b, fr1, f2w, f2b, fr2, f3w, hbias):
    L = u.shape[1]
    u = short_conv3(u, short_w, short_b)
    v, x1, x2 = jnp.split(u, 3, axis=-1)
    kern = hyena_filters(L, f1w, f1b, fr1, f2w, f2b, fr2, f3w)
    z = long_conv(v, kern[0], hbias[0]) * x1
    z = long_conv(z, kern[1], hbias[1]) * x2
    return z

def retention_chunked(q, k, v, log_g, s0):
    B, L, H, _ = q.shape
    nc = L // RET_CHUNK

    def to_chunks(t):
        return t.reshape(B, nc, RET_CHUNK, H, t.shape[-1]).transpose(1, 0, 3, 2, 4)

    qc, kc, vc = to_chunks(q), to_chunks(k), to_chunks(v)
    i = jnp.arange(RET_CHUNK, dtype=jnp.float32)
    diff = i[:, None] - i[None, :]
    decay_mask = jnp.where(diff[None] >= 0, jnp.exp(log_g[:, None, None] * jnp.maximum(diff, 0.0)[None]), 0.0)
    q_decay = jnp.exp(log_g[:, None] * (i + 1.0))[..., None]
    k_decay = jnp.exp(log_g[:, None] * (RET_CHUNK - 1.0 - i))[..., None]
    chunk_decay = jnp.exp(log_g * RET_CHUNK)[:, None, None]

    def step(s, qkv):
        qi, ki, vi = qkv
        scores = jnp.einsum("bhid,bhjd->bhij", qi, ki) * decay_mask
        inner = jnp.einsum("bhij,bhjv->bhiv", scores, vi)
        cross = jnp.einsum("bhid,bhdv->bhiv", qi * q_decay, s)
        s_new = s * chunk_decay + jnp.einsum("bhjd,bhjv->bhdv", ki * k_decay, vi)
        return s_new, inner + cross

    s_fin, out = lax.scan(step, s0, (qc, kc, vc))
    out = out.transpose(1, 0, 3, 2, 4).reshape(B, L, H, -1)
    return out, s_fin

def head_group_norm(o):
    mu = jnp.mean(o, axis=-1, keepdims=True)
    var = jnp.mean(jnp.square(o - mu), axis=-1, keepdims=True)
    return (o - mu) * lax.rsqrt(var + EPS)

def even_mixer(h, s0, w_in, short_w, short_b, f1w, f1b, fr1, f2w, f2b, fr2, f3w, hbias, decay_logit, w_out):
    B, L, _ = h.shape
    proj = h @ w_in
    hy_in, q, k, v, g = jnp.split(proj, [3 * HY_W, 3 * HY_W + RET_W, 3 * HY_W + 2 * RET_W, 3 * HY_W + 3 * RET_W], axis=-1)
    y_hy = hyena(hy_in, short_w, short_b, f1w, f1b, fr1, f2w, f2b, fr2, f3w, hbias)

    def heads(t):
        return t.reshape(B, L, RET_HEADS, RET_HEAD_DIM).astype(jnp.float32)

    q, k, v = heads(q), heads(k) * (RET_HEAD_DIM ** -0.5), heads(v)
    log_g = jax.nn.log_sigmoid(decay_logit.astype(jnp.float32))
    o_f, s_f = retention_chunked(q, k, v, log_g[0], s0[:, 0])
    o_b, s_b = retention_chunked(q[:, ::-1], k[:, ::-1], v[:, ::-1], log_g[1], s0[:, 1])
    o = head_group_norm(o_f + o_b[:, ::-1])
    y_ret = (jax.nn.silu(g.astype(jnp.float32)) * o.reshape(B, L, RET_W)).astype(h.dtype)
    y = jnp.concatenate([y_hy, y_ret], axis=-1) @ w_out
    return y, jnp.stack([s_f, s_b], axis=1)

def axial_rope(x):
    L = x.shape[1]
    rows = L // GRID_W
    row = jnp.repeat(jnp.arange(rows, dtype=jnp.float32), GRID_W)
    col = jnp.tile(jnp.arange(GRID_W, dtype=jnp.float32), rows)
    half = x.shape[-1] // 2
    quarter = half // 2
    freqs = ROPE_BASE ** (-jnp.arange(quarter, dtype=jnp.float32) / quarter)

    def rot(xh, p):
        ang = p[:, None] * freqs[None, :]
        cos = jnp.cos(ang)[None, :, None, None, :]
        sin = jnp.sin(ang)[None, :, None, None, :]
        a, b = xh[..., :quarter].astype(jnp.float32), xh[..., quarter:].astype(jnp.float32)
        return jnp.concatenate([a * cos - b * sin, a * sin + b * cos], axis=-1)

    return jnp.concatenate([rot(x[..., :half], row), rot(x[..., half:], col)], axis=-1).astype(x.dtype)

def diff_project(h, w_in):
    B, L, _ = h.shape
    q, k, v = jnp.split(h @ w_in, 3, axis=-1)
    return (q.reshape(B, L, DIFF_HEADS, 2, DIFF_HEAD_DIM),
            k.reshape(B, L, DIFF_HEADS, 2, DIFF_HEAD_DIM),
            v.reshape(B, L, DIFF_HEADS, 2 * DIFF_HEAD_DIM))

def diff_attention(q, k, v, lam):
    B, Lq, H, _, d = q.shape
    nb = Lq // Q_BLOCK
    qb = q.reshape(B, nb, Q_BLOCK, H, 2, d).transpose(1, 0, 2, 3, 4, 5)
    scale = d ** -0.5

    def block(qi):
        s = jnp.einsum("bqhmd,bkhmd->bhmqk", qi, k).astype(jnp.float32) * scale
        p = jax.nn.softmax(s, axis=-1)
        a = p[:, :, 0] - lam * p[:, :, 1]
        return jnp.einsum("bhqk,bkhe->bqhe", a.astype(v.dtype), v)

    o = lax.map(block, qb)
    return o.transpose(1, 0, 2, 3, 4).reshape(B, Lq, H, 2 * d)

def diff_lambda(lq1, lk1, lq2, lk2, lam_init):
    return (jnp.exp(jnp.sum(lq1 * lk1).astype(jnp.float32))
            - jnp.exp(jnp.sum(lq2 * lk2).astype(jnp.float32)) + lam_init)

def diff_output(o, subln_g, lam_init, w_out):
    B, L = o.shape[:2]
    o = rms_norm(o, subln_g) * (1.0 - lam_init)
    return o.reshape(B, L, D_MODEL).astype(w_out.dtype) @ w_out

def odd_context(h, w_in, lam, lam_init, subln_g, w_out):
    B, L, _ = h.shape
    q, k, v = diff_project(h, w_in)
    o = diff_attention(q, k, v, lam)
    return diff_output(o, subln_g, lam_init, w_out), k.reshape(B, L, DIFF_HEADS, 2 * DIFF_HEAD_DIM), v

def odd_latent(h, ck, cv, w_in, lam, lam_init, subln_g, w_out):
    q, k, v = diff_project(h, w_in)
    q, k = axial_rope(q), axial_rope(k)
    B, Lc = ck.shape[:2]
    keys = jnp.concatenate([ck.reshape(B, Lc, DIFF_HEADS, 2, DIFF_HEAD_DIM).astype(k.dtype), k], axis=1)
    vals = jnp.concatenate([cv.astype(v.dtype), v], axis=1)
    o = diff_attention(q, keys, vals, lam)
    return diff_output(o, subln_g, lam_init, w_out)

def expert_choice_ffn(h, w_router, wg, wu, wd):
    N, D = h.shape
    cap = EC_FACTOR * N // N_EXPERTS
    aff = jax.nn.softmax((h @ w_router).astype(jnp.float32), axis=-1)
    gate, idx = lax.top_k(aff.T, cap)
    xs = h[idx]
    hid = jax.nn.silu(jnp.einsum("ecd,edf->ecf", xs, wg)) * jnp.einsum("ecd,edf->ecf", xs, wu)
    out = jnp.einsum("ecf,efd->ecd", hid, wd) * gate[..., None].astype(h.dtype)
    return jnp.zeros_like(h).at[idx.reshape(-1)].add(out.reshape(-1, D))

def setup_inputs(seed: int = 0) -> dict:
    key = jax.random.key(seed)
    ks = iter(jax.random.split(key, 48))

    def nrm(shape, scale):
        return jax.random.normal(next(ks), shape, jnp.float32) * scale

    D, R, A = D_MODEL, N_RET_LAYERS, N_ATT_LAYERS
    base_logit = jnp.asarray(np.log(2.0 ** (5 + np.arange(RET_HEADS)) - 1.0), jnp.float32)
    return {
        "x_prompt": nrm((BATCH, SEQ, D), 1.0),
        "x_sample": nrm((DEC_BATCH, DEC_SEQ, D), 1.0),
        "state_ret": nrm((DEC_BATCH, R, 2, RET_HEADS, RET_HEAD_DIM, RET_HEAD_DIM), 1.0),
        "cache_k": nrm((DEC_BATCH, A, PAST_LEN, DIFF_HEADS, 2 * DIFF_HEAD_DIM), 1.0),
        "cache_v": nrm((DEC_BATCH, A, PAST_LEN, DIFF_HEADS, 2 * DIFF_HEAD_DIM), 1.0),
        "c": nrm((DEC_BATCH, D), 1.0),
        "c_ctx": nrm((D,), 1.0),
        "w_mod": nrm((DEPTH, D, 6 * D), D ** -0.5),
        "b_mod": nrm((DEPTH, 6 * D), 0.01),
        "norm1_g": 1.0 + nrm((DEPTH, D), 0.05),
        "norm2_g": 1.0 + nrm((DEPTH, D), 0.05),
        "w_in_even": nrm((R, D, EVEN_IN), D ** -0.5),
        "hy_short_w": nrm((R, 3, 3 * HY_W), 3 ** -0.5),
        "hy_short_b": nrm((R, 3 * HY_W), 0.01),
        "hy_f1_w": nrm((R, HY_EMB, HY_FF), HY_EMB ** -0.5),
        "hy_f1_b": nrm((R, HY_FF), 0.01),
        "hy_freq1": 1.0 + nrm((R, HY_FF), 0.1),
        "hy_f2_w": nrm((R, HY_FF, HY_FF), HY_FF ** -0.5),
        "hy_f2_b": nrm((R, HY_FF), 0.01),
        "hy_freq2": 1.0 + nrm((R, HY_FF), 0.1),
        "hy_f3_w": nrm((R, HY_FF, 4 * HY_W), HY_FF ** -0.5),
        "hy_bias": nrm((R, 2, HY_W), 0.1),
        "ret_decay": base_logit + nrm((R, 2, RET_HEADS), 0.1),
        "w_out_even": nrm((R, D, D), D ** -0.5),
        "w_in_odd": nrm((A, D, 3 * D), D ** -0.5),
        "lam_q1": nrm((A, DIFF_HEAD_DIM), 0.1),
        "lam_k1": nrm((A, DIFF_HEAD_DIM), 0.1),
        "lam_q2": nrm((A, DIFF_HEAD_DIM), 0.1),
        "lam_k2": nrm((A, DIFF_HEAD_DIM), 0.1),
        "subln_g": 1.0 + nrm((A, 2 * DIFF_HEAD_DIM), 0.05),
        "w_out_odd": nrm((A, D, D), D ** -0.5),
        "moe_router": nrm((DEPTH, D, N_EXPERTS), D ** -0.5),
        "moe_wg": nrm((DEPTH, N_EXPERTS, D, EXPERT_FF), D ** -0.5),
        "moe_wu": nrm((DEPTH, N_EXPERTS, D, EXPERT_FF), D ** -0.5),
        "moe_wd": nrm((DEPTH, N_EXPERTS, EXPERT_FF, D), EXPERT_FF ** -0.5),
        "final_g": 1.0 + nrm((D,), 0.05),
    }

def reference(x_prompt, x_sample, state_ret, cache_k, cache_v, c, c_ctx, w_mod, b_mod, norm1_g, norm2_g,
              w_in_even, hy_short_w, hy_short_b, hy_f1_w, hy_f1_b, hy_freq1, hy_f2_w, hy_f2_b, hy_freq2,
              hy_f3_w, hy_bias, ret_decay, w_out_even, w_in_odd, lam_q1, lam_k1, lam_q2, lam_k2, subln_g,
              w_out_odd, moe_router, moe_wg, moe_wu, moe_wd, final_g):
    xp, xs = x_prompt, x_sample
    Bp, Lp, _ = xp.shape
    Bs, Ls, _ = xs.shape
    new_ret, new_k, new_v = [], [], []
    for l in range(DEPTH):
        sh1p, sc1p, g1p, sh2p, sc2p, g2p = ada_modulation(c_ctx, w_mod[l], b_mod[l])
        sh1s, sc1s, g1s, sh2s, sc2s, g2s = ada_modulation(c, w_mod[l], b_mod[l])
        hp = rms_norm(xp, norm1_g[l]) * (1.0 + sc1p) + sh1p
        hs = rms_norm(xs, norm1_g[l]) * (1.0 + sc1s) + sh1s
        i = l // 2
        if l % 2 == 0:
            params = (w_in_even[i], hy_short_w[i], hy_short_b[i], hy_f1_w[i], hy_f1_b[i], hy_freq1[i],
                      hy_f2_w[i], hy_f2_b[i], hy_freq2[i], hy_f3_w[i], hy_bias[i], ret_decay[i], w_out_even[i])
            s0 = jnp.zeros((Bp, 2, RET_HEADS, RET_HEAD_DIM, RET_HEAD_DIM), jnp.float32)
            yp, st = even_mixer(hp, s0, *params)
            ys, _ = even_mixer(hs, state_ret[:, i].astype(jnp.float32), *params)
            new_ret.append(st)
        else:
            lam_init = 0.8 - 0.6 * math.exp(-0.3 * l)
            lam = diff_lambda(lam_q1[i], lam_k1[i], lam_q2[i], lam_k2[i], lam_init)
            yp, kc, vc = odd_context(hp, w_in_odd[i], lam, lam_init, subln_g[i], w_out_odd[i])
            ys = odd_latent(hs, cache_k[:, i], cache_v[:, i], w_in_odd[i], lam, lam_init, subln_g[i], w_out_odd[i])
            new_k.append(kc)
            new_v.append(vc)
        xp = xp + g1p * yp
        xs = xs + g1s * ys
        hp = rms_norm(xp, norm2_g[l]) * (1.0 + sc2p) + sh2p
        hs = rms_norm(xs, norm2_g[l]) * (1.0 + sc2s) + sh2s
        fp = expert_choice_ffn(hp.reshape(Bp * Lp, D_MODEL), moe_router[l], moe_wg[l], moe_wu[l], moe_wd[l])
        fs = expert_choice_ffn(hs.reshape(Bs * Ls, D_MODEL), moe_router[l], moe_wg[l], moe_wu[l], moe_wd[l])
        xp = xp + g2p * fp.reshape(Bp, Lp, D_MODEL)
        xs = xs + g2s * fs.reshape(Bs, Ls, D_MODEL)
    y_prompt = rms_norm(xp, final_g)
    y_sample = rms_norm(xs, final_g)
    new_state_ret = jnp.stack(new_ret, axis=1)
    new_cache_k = jnp.stack(new_k, axis=1)
    new_cache_v = jnp.stack(new_v, axis=1)
    return (y_prompt, y_sample, new_state_ret, new_cache_k, new_cache_v)


_drawn_inputs = setup_inputs


def setup_inputs(seed=0):
    import zlib

    import numpy as np

    out = dict(_drawn_inputs(seed))
    spreads = {}
    factors = {'hy_short_b': 32.587,
     'hy_f1_b': 18.616,
     'hy_freq1': 2.994,
     'hy_f2_b': 33.571,
     'hy_freq2': 12.779,
     'lam_k1': 8.0,
     'subln_g': 2.736}
    for name, (base, spread) in spreads.items():
        noise = np.random.default_rng([zlib.crc32(name.encode()), seed]).standard_normal(out[name].shape)
        drawn = base * np.exp(spread * noise) if base else spread * noise
        out[name] = __import__('jax').numpy.asarray(drawn.astype(out[name].dtype))
    for name, factor in factors.items():
        out[name] = (out[name] * factor).astype(out[name].dtype)
    return out
```

```python
from contextlib import ExitStack
import math

import numpy as np

import concourse.bass as bass
from concourse import mybir

ALU = mybir.AluOpType
ACT = mybir.ActivationFunctionType
AX = mybir.AxisListType
F32 = mybir.dt.float32
I32 = mybir.dt.int32
U32 = mybir.dt.uint32

P = 128
D = 1024
DK = D // P
LAT, CTX = 1024, 128
NT = LAT + CTX
T = NT // P
HW = 512
RH = 4
AH = 8
NE = 16
CAPL, CAPC = 2 * LAT // NE, 2 * CTX // NE
CAP = CAPL + CAPC
EPS = 1e-6
NS = 4
U = 4096
LAM_INIT = 0.8 - 0.6 * math.exp(-0.3)
SCRATCH = 2048
MAGIC = 12582912.0


def tables():
    def order(L):
        return np.concatenate([np.arange(0, L, 2), np.arange(1, L, 2)])
    t = {}
    n = order(LAT).astype(np.float64)
    w = 2 * np.pi * (np.arange(512) + 0.5) / (2 * LAT)
    for name, f in (("cos", np.cos), ("sin", np.sin)):
        m = f(n[:, None] * w[None, :])
        t["fwd_" + name] = m.reshape(8, P, 512).transpose(1, 0, 2)
        t["inv_" + name] = (m.T / LAT).reshape(4, P, LAT).transpose(1, 0, 2)
    nc_ = np.arange(CTX, dtype=np.float64)
    wc = 2 * np.pi * (np.arange(CTX) + 0.5) / (2 * CTX)
    a = nc_[:, None] * wc[None, :]
    t["ctx_dft"] = np.stack([np.cos(a), np.sin(a), np.cos(a).T / CTX, np.sin(a).T / CTX], 1)

    feats, wins = [], []
    for L in (LAT, CTX):
        pos = np.arange(L, dtype=np.float32)
        tt = pos / np.float32(L - 1)
        ww = np.float32(2.0 * math.pi) * pos / np.float32(L)
        f = np.linspace(1e-4, 15, 16, dtype=np.float32)
        wf = ww[:, None] * f[None, :]
        ft = np.concatenate([tt[:, None], np.cos(wf), -np.sin(wf)], -1)
        dl = np.linspace(math.log(1e-2) / 1.5, math.log(1e-2) / 0.3, HW, dtype=np.float32)
        wn = np.exp(-tt[:, None] * np.abs(dl)[None, :])
        o = order(L) if L == LAT else np.arange(L)
        feats.append(ft[o])
        wins.append(wn[o])
    t["feat"] = np.concatenate(feats, 0).T
    t["window"] = np.concatenate(wins, 0).reshape(T, P, HW).transpose(1, 0, 2)

    i = np.arange(P, dtype=np.float64)
    dji = i[None, :] - i[:, None]
    t["decay"] = np.stack([np.maximum(dji, 0), np.maximum(-dji, 0), dji >= 0, dji <= 0,
                           np.broadcast_to(i[None, :] + 1, (P, P)), np.broadcast_to(P - i[None, :], (P, P))], 1)
    small = np.zeros((P, 16))
    small[:, 0] = P - 1 - i
    small[:, 1] = i
    small[:, 2:11] = i[:, None] + P * np.arange(T)[None, :]
    t["small"] = small
    t["ident"] = np.eye(P)
    t["lower"] = (dji < 0)
    t["iota"] = np.broadcast_to(i[None, :], (P, P))

    fr = (10000.0 ** (-np.arange(16, dtype=np.float32) / np.float32(16))).astype(np.float32)
    tok = np.arange(LAT)
    d = np.arange(P) % 64
    where = np.where((d // 32)[:, None] == 0, (tok // 64)[None, :], (tok % 64)[None, :]).astype(np.float32)
    ang = where * fr[d % 16][:, None]
    sign = np.where((d % 32) < 16, -1.0, 1.0)[:, None]
    t["rope"] = np.stack([np.cos(ang), np.sin(ang) * sign], 1)
    return {k: np.ascontiguousarray(v.astype(np.float32)) for k, v in t.items()}


def build(nc, a, out, tab):
    with ExitStack() as ctx:
        def sb(name, shape, dt=F32):
            return ctx.enter_context(nc.sbuf_tensor(name, shape, dt))

        made = {}

        shared = {"n10.": ("n.", 0), "n20.": ("n.", 1), "n11.": ("n.", 2), "n21.": ("n.", 3), "z.": ("n.", 4),
                  "o0.": ("o.", 0), "o1.": ("o.", 1), "e0.": ("e.", 0), "e1.": ("e.", 1),
                  "m0.": ("m.", 0), "m1.": ("m.", 1)}
        adds = {"n.ssq": T, "n.var": 1, "n.std": 1, "n.xn": T, "n.tA": T, "n.tD": T, "n.evA": T, "n.evD": T,
                "n.y": 0, "n.g": 0,
                "o.g": 1, "o.gev": 4, "o.mm": 2 * T, "o.x": 2 * T, "o.x_out": 16 * T, "o.xn_out": 16 * T,
                "m.big_free": 1,
                "e.tab": 48, "e.lg": 1, "e.sub": 1, "e.exp": 1, "e.aff": 1, "e.at": 3, "e.affT": 3,
                "e.aft_out": 16, "e.bc0": 8 * NE, "e.bc1": 8 * NE, "e.oh": NE, "e.ranked": NE, "e.ix": NE,
                "e.idx": 2 * NE, "e.xs0": 16 * NE, "e.xs1": 16 * NE, "e.ti": 3 * NE, "e.te": 3 * NE,
                "e.gu": 8 * NE, "e.sg": 8 * NE, "e.hid": 8 * NE, "e.d": 8 * NE, "e.dn": 8 * NE,
                "e.to": 2 * NE, "e.rows": 2 * NE, "e.added": 32 * NE, "e.scattered": NE}

        def common(name):
            head, _, tail = name.partition(".")
            pre, k = shared.get(head + ".", (head + ".", 0))
            return (pre + tail if _ else name), k

        def s(name):
            name = common(name)[0]
            if name not in made:
                made[name] = ctx.enter_context(nc.semaphore(name))
            return made[name]

        ahead = {"e.dn": 1, "e.to": 1, "e.rows": 1, "e.hid": 1, "e.scattered": 1}

        def at(name, value):
            base, k = common(name)
            value = value + (k * adds[base] if k else 0)
            return s(name), (value + ahead[base] if base in ahead else value)

        ring = sb("ring", [P, NS, U])
        hT = sb("hT", [P, DK * NT])
        yT = sb("yT", [P, DK * NT])
        big = sb("big", [P, 2 * T * D])
        misc = sb("misc", [P, 2048])
        ident = sb("ident_sb", [P, P])
        colA = sb("colA", [P, P])
        colB = sb("colB", [P, 80])
        modc = sb("modc", [P, 2, 48, 2])
        amul = sb("amul", [P, 2, 2, 8, 2])
        scond = sb("scond", [P, 8, 2])
        tmp16 = sb("tmp16", [P, 8, 2])
        small = sb("small_sb", [P, 16])
        stat = sb("stat", [P, 3, T])
        cdft = sb("cdft", [P, 4, P])
        fcol = sb("fcol", [64, 4])
        dk = sb("dk", [P, 5, 8])
        kdec = sb("kdec", [P, 2, 4])
        cdec = sb("cdec", [P, 8])
        gst = sb("gst", [P, 3, T * 8])
        lamc = sb("lamc", [P, 8])
        gstf = gst[:, :, :].rearrange("p a t -> p (a t)")
        ones = gstf[:, 0:P]
        gmv = gstf[:, 0:72].rearrange("p (j c) -> p j c", c=2)
        ps = ctx.enter_context(nc.psum_tensor("ps", [P, 8, 512], F32))

        def bank(b, n=1):
            return ps[:, b:b + n, :].rearrange("p b n -> p (b n)")

        xd = nc.dram_tensor("x_res", [NT, D], F32, kind="Internal").ap()
        xn_d = nc.dram_tensor("x_normed", [NT, D], F32, kind="Internal").ap()
        ud = nc.dram_tensor("hy_u", [12, P, NT], F32, kind="Internal").ap()
        kd = nc.dram_tensor("hy_spec", [2, 2, P, U], F32, kind="Internal").ap()
        kcd = nc.dram_tensor("hy_spec_ctx", [P, 2, 2, HW], F32, kind="Internal").ap()
        aftd = nc.dram_tensor("aff_t", [NE, NT], F32, kind="Internal").ap()

        units = []

        def unit(src, ready=None):
            units.append((src, ready))
            return len(units) - 1

        def w_units(w, cols):
            return [unit(w[:, c:c + 512].rearrange("(k p) n -> p k n", p=P)) for c in cols]

        mod_units = {0: w_units(a["w_mod"][0], range(0, 6144, 512))}
        even_units = w_units(a["w_in_even"][0], [1536, 2048, 2560, 3072, 0, 512, 1024])
        hy_units = []
        for o in range(2):
            hy_units.append([unit(tab["fwd_cos"]), unit(tab["fwd_sin"]),
                             unit(kd[o, 0], ("f.spec_out", 16 * 4 * (o + 1))), unit(kd[o, 1], None),
                             unit(tab["inv_cos"]), unit(tab["inv_sin"])])
        oute_units = w_units(a["w_out_even"][0], [0, 512])
        exp_units = {}

        def expert_src(l, e, j):
            w = a[("moe_wg", "moe_wu", "moe_wg", "moe_wu", "moe_wd", "moe_wd")[j]]
            c = (0, 0, 512, 512, 0, 512)[j]
            return w[l, e, :, c:c + 512]

        exp_units[0] = len(units)
        units += [None] * (6 * NE)
        mod_units[1] = w_units(a["w_mod"][1], range(0, 6144, 512))
        odd_units = w_units(a["w_in_odd"][0], range(0, 3072, 512))
        outo_units = w_units(a["w_out_odd"][0], [0, 512])
        exp_units[1] = len(units)
        units += [None] * (6 * NE)

        def slot(n):
            return ring[:, n % NS, :]

        def landed(eng, n, more=0):
            eng.wait_ge(*at(f"slot{n % NS}_landed", 16 * (n // NS + 1) + more))

        def free(ins, n):
            ins.then_inc(s(f"slot{n % NS}_free"), 1)

        hTv = hT[:, :].rearrange("p (k t) -> p k t", k=DK)
        yTv = yT[:, :].rearrange("p (k t) -> p k t", k=DK)
        X = big[:, 0:T * D].rearrange("p (t d) -> p t d", t=T)
        XN = big[:, T * D:2 * T * D].rearrange("p (t d) -> p t d", t=T)
        FH = big[:, 0:9216].rearrange("p (t d c) -> p t d c", t=T, d=2)
        FS = big[:, 9216:18432].rearrange("p (t d c) -> p t d c", t=T, d=2)
        fwd_c = hT[:, 0:4096].rearrange("p (t k) -> p t k", t=8)
        fwd_s = hT[:, 4096:8192].rearrange("p (t k) -> p t k", t=8)
        facc = hT[:, 8192:9216].rearrange("p (g c) -> p g c", g=2)
        win = yT[:, 0:4608].rearrange("p (t c) -> p t c", t=T)
        featT = yT[0:33, 4608:4608 + NT]
        harg = yT[0:64, 5760:5760 + NT]
        hrnd = yT[0:64, 6912:6912 + NT]
        h2T = yT[0:64, 8064:8064 + NT]
        f1w = big[0:33, 256:320]
        f2w = big[0:64, 320:384]
        fstage = big[:, 0:4096].rearrange("p (b f c) -> p b f c", b=2, f=4)
        fstagec = big[:, 4096:5120].rearrange("p (f c) -> p f c", f=2)
        ftmp = big[:, 5120:7168].rearrange("p (f c) -> p f c", f=4)
        f3w = misc[0:64, :]
        hrow = big[:, 9216:9728]
        qT = big[:, 0:4608].rearrange("p (h t) -> p h t", h=4)
        kT = big[:, 4608:9216].rearrange("p (h t) -> p h t", h=4)
        vtok = big[:, 9216:13824].rearrange("p (t c) -> p t c", t=T)
        gtok = big[:, 13824:18432].rearrange("p (t c) -> p t c", t=T)
        ktok = hT[:, 0:4608].rearrange("p (t c) -> p t c", t=T)
        sbwd = hT[:, 4608:8704].rearrange("p (c n) -> p c n", c=8)
        sfwd = hT[:, 8704:9216]
        raw = [yT[:, i * NT:(i + 1) * NT] for i in range(2)]
        ubuf = [yT[:, (2 + i) * NT:(3 + i) * NT] for i in range(2)]
        rtab = yT[:, 4608:5376].rearrange("p (a n) -> p a n", a=6)
        lamv = yT[:, 5376:5632].rearrange("p (a n) -> p a n", a=4)
        rarg = yT[:, 5632:6144]
        rmask = misc[:, 0:512]
        qdec = misc[:, 512:1536].rearrange("p (d n) -> p d n", d=2)
        sm = [yT[:, i * 512:(i + 1) * 512] for i in range(2)]
        qfb = yT[:, 1024:2048].rearrange("p (d n) -> p d n", d=2)
        vdec = yT[:, 2048:3072].rearrange("p (d n) -> p d n", d=2)
        sctx = yT[:, 3072:4096].rearrange("p (d n) -> p d n", d=2)
        bnb = yT[:, 4096:4312].rearrange("p (j c) -> p j c", c=6)
        zT = [big[:, i * 4608:(i + 1) * 4608].rearrange("p (c t) -> p c t", c=4) for i in range(3)]
        vt = big[:, 13824:18432].rearrange("p (t c) -> p t c", t=T)
        spec = hT[:, 0:8192].rearrange("p (k f c) -> p k f c", k=4, f=4)
        specc = hT[:, 8192:9216].rearrange("p (f c) -> p f c", f=2)
        xh = yT[:, 0:2048].rearrange("p (f c) -> p f c", f=4)
        xq = yT[:, 2048:4096].rearrange("p (f c) -> p f c", f=4)
        ht = yT[:, 4096:4608]
        kctx = misc[:, :].rearrange("p (o f c) -> p o f c", o=2, f=2)
        grow = misc[:, :].rearrange("p (g d) -> p g d", g=2)
        kTa = big[:, 0:9216].rearrange("p (h t) -> p h t", h=AH)
        va = big[:, 9216:18432].rearrange("p (t d) -> p t d", t=T)
        qTa = yTv
        cosT = misc[:, 0:1024]
        sinT = misc[:, 1024:2048]
        eb = hT[:, 0:4608].rearrange("p (b m k) -> p b m k", b=2, m=2)
        aT = hT[:, 4608:5760]
        oh = hT[:, 5760:6912].rearrange("p (t d) -> p t d", t=T)
        cv = hT[:, 6912:7936]
        ckT = hT[:, 7936:8960].rearrange("p (h t) -> p h t", h=AH)
        junk2 = misc[:, 0:P]
        xs = [big[:, i * D:(i + 1) * D] for i in range(2)]
        xsc = [big[0:CAPC, (2 + i) * D:(3 + i) * D] for i in range(2)]
        xsT = [big[:, 4096 + i * 1152:4096 + (i + 1) * 1152].rearrange("p (k c) -> p k c", k=8) for i in range(2)]
        hid = big[:, 6400:7552].rearrange("p (k c) -> p k c", k=8)
        sg = [big[:, 7552 + i * CAP:7552 + (i + 1) * CAP] for i in range(3)]
        outT = big[:, 8064:9216].rearrange("p (k c) -> p k c", k=8)
        orow = [big[:, 9216 + i * D:9216 + (i + 1) * D] for i in range(2)]
        orowc = [big[0:CAPC, 11264 + i * D:11264 + (i + 1) * D] for i in range(2)]
        bc = [big[:, 13312 + i * NT:13312 + (i + 1) * NT] for i in range(2)]
        onehot = big[:, 15616:16768].rearrange("p (t n) -> p t n", t=T)
        junk = big[:, 16768:17792]
        aff = yT[:, 0:144].rearrange("p (t e) -> p t e", t=T)
        affm = yT[:, 144:288].rearrange("p (t e) -> p t e", t=T)
        affT = yT[0:NE, 512:512 + NT]
        tg = yT[:, 1664:1664 + 36].rearrange("p (b t c) -> p b t c", b=2, t=T)
        cnt = yT[:, 1700:1727].rearrange("p (t c) -> p t c", t=T)
        rank = yT[:, 1727:1736]
        rowmax = yT[:, 1736:1754].rearrange("p (c t) -> p c t", c=2)
        gate = yT[:, 1754:1762].rearrange("p (b c) -> p b c", b=2)
        idx = yT[:, 1762:1770].bitcast(U32).rearrange("p (b c) -> p b c", b=2)
        lower = yT[:, 1792:1920]
        iota = yT[:, 1920:2048]
        rw = yT[:, 2048:2176].rearrange("p (k e) -> p k e", k=8)

        block = ctx.enter_context(nc.Block())

        class Chain:

            def __init__(self, eng, name):
                self.eng, self.sem, self.n, self.off = eng, s(name), 0, 0

            def __call__(self, ins):
                ins.then_inc(self.sem, 1)
                self.n += 1
                self.eng.wait_ge(self.sem, self.off + self.n)

        def each_expert_pair(eng, chains, per, body):
            start = [c.n for c in chains]
            with eng.Fori(0, 7) as i:
                for c, n in zip(chains, per):
                    c.off = i * n
                body(i, False)
            for c, n, n0 in zip(chains, per, start):
                assert c.n - n0 == n, (c.n - n0, n)
                c.off, c.n = 0, n0 + 7 * n
            body(7, True)

        @block.sync
        def _(sp):
            def load(n):
                src, ready = units[n]
                if ready:
                    sp.wait_ge(*at(ready[0], ready[1]))
                if n >= NS:
                    sp.wait_ge(*at(f"slot{n % NS}_free", n // NS))
                dst = slot(n) if len(src.shape) == 2 else slot(n).rearrange("p (k n) -> p k n", k=src.shape[1])
                sp.dma_start(dst, src).then_inc(s(f"slot{n % NS}_landed"), 16)

            def experts(l):
                base = exp_units[l]

                def pair(i, last):
                    for ee in range(2):
                        for j in range(6):
                            n = base + 6 * ee + j
                            sp.wait_ge(*at(f"slot{n % NS}_free", n // NS + 3 * i))
                            sp.dma_start(slot(n).rearrange("p (k n) -> p k n", k=DK),
                                         expert_src(l, 2 * i + ee, j).rearrange("(k p) n -> p k n", p=P)
                                         ).then_inc(s(f"slot{n % NS}_landed"), 16)
                each_expert_pair(sp, [], [], pair)

            for n in range(exp_units[0]):
                load(n)
            experts(0)
            for n in range(exp_units[0] + 6 * NE, exp_units[1]):
                load(n)
            experts(1)

        @block.gpsimd
        def _(pool):
            def ld(dst, src, name):
                pool.dma_start(dst, src).then_inc(s(name), 16)

            pool.sem_inc(s("e.scattered"), ahead["e.scattered"])
            r0 = 0
            for name, n in (("b_mod", 96), ("norm1_g", 16), ("norm2_g", 16)):
                v = a[name].rearrange("l (r c) -> (l r) c", c=P)
                ld(big[r0:r0 + n, 0:P], v, "c.rows")
                r0 += n
            r0 = 0
            for v, n in ((a["hy_short_w"][0].rearrange("s (r c) -> (s r) c", c=P), 36),
                         (a["hy_short_b"][0].rearrange("(r c) -> r c", c=P), 12),
                         (a["hy_bias"][0].rearrange("o (r c) -> (o r) c", c=P), 8),
                         (a["subln_g"], 1),
                         (a["c"].rearrange("o (r c) -> (o r) c", c=P), 8),
                         (a["c_ctx"].rearrange("(r c) -> r c", c=P), 8)):
                ld(big[r0:r0 + n, P:2 * P], v, "c.rows")
                r0 += n
            ld(ident[:, :], tab["ident"], "c.ident")
            ld(small[:, :], tab["small"], "c.small")
            ld(cdft[:, :, :], tab["ctx_dft"], "c.small")
            ld(featT, tab["feat"], "f.in")
            for i, name in enumerate(("hy_f1_b", "hy_freq1", "hy_f2_b", "hy_freq2")):
                ld(fcol[:, i:i + 1], a[name][0].rearrange("(p o) -> p o", o=1), "f.in")
            ld(big[0:33, 256:320], a["hy_f1_w"][0], "f.in")
            ld(big[0:64, 320:384], a["hy_f2_w"][0], "f.in")
            ld(f3w, a["hy_f3_w"][0], "f.in")
            ld(win, tab["window"], "f.in")
            ld(fwd_c, tab["fwd_cos"], "f.dft")
            ld(fwd_s, tab["fwd_sin"], "f.dft")

            def load_x(src_l, src_c, k):
                for t in range(T):
                    src = src_l[t * P:(t + 1) * P, :] if t < 8 else src_c
                    ld(X[:, t, :], src, f"x{t}.landed")

            for o in range(2):
                for kt in range(4):
                    pool.wait_ge(*at("f.spec", 4 * o + kt + 1 + o))
                    pool.dma_start(kd[o, kt // 2, :, (kt % 2) * 2048:(kt % 2 + 1) * 2048],
                                   fstage[:, kt % 2].rearrange("p f c -> p (f c)")).then_inc(s("f.spec_out"), 16)
                    pool.wait_ge(*at("f.spec_out", 16 * (4 * o + kt + 1)))
                pool.wait_ge(*at("f.spec", 5 * (o + 1)))
                pool.dma_start(kcd[:, o, :, :], fstagec).then_inc(s("f.specc_out"), 16)
                pool.wait_ge(*at("f.specc_out", 16 * (o + 1)))

            load_x(a["x_sample"][0], a["x_prompt"][0], 0)
            ld(rtab, tab["decay"], "r.tab")
            ld(dk[:, 0:1, :], a["ret_decay"].rearrange("o d h -> o (d h)").partition_broadcast(P), "r.tab")
            for i, name in enumerate(("lam_q1", "lam_k1", "lam_q2", "lam_k2")):
                ld(lamv[:, i:i + 1, :], a[name].partition_broadcast(P), "r.tab")
            for j in range(12):
                pool.wait_ge(*at("p.u", j + 1))
                pool.dma_start(ud[j], ubuf[j % 2]).then_inc(s(f"p.u_out{j % 2}"), 16)
            for b in range(2):
                pool.wait_ge(*at(f"p.u_out{b}", 16 * 6))
            pool.wait_ge(*at("p.ev", 4 + 4 + 9 + 9 + 12))
            pool.wait_ge(*at("p.mm", 4 + 4 + 9 + 9 + 12))
            for d, dst in ((0, sfwd), (1, sbwd[:, 7, :])):
                ld(dst.rearrange("p (h n) -> p h n", h=RH),
                   a["state_ret"][0, 0, d].rearrange("h p n -> p h n"), "r.s0")
            pool.wait_ge(*at("r.st", 9))
            for d in range(2):
                pool.dma_start(out[2][0, 0, d].rearrange("h p n -> p h n"),
                               sctx[:, d, :].rearrange("p (h n) -> p h n", h=RH)).then_inc(s("r.sctx_out"), 16)
            pool.wait_ge(*at("r.otev", T))
            for i in range(3):
                ld(zT[i], ud[4 * i:4 * i + 4].rearrange("c p t -> p c t"), f"h.u{i}")
            ld(kctx, kcd, "h.kctx")

            def after_mixer(l):
                pool.wait_ge(*at(f"m{l}.big_free", 1))
                if l == 0:
                    load_x(a["x_sample"][0], a["x_prompt"][0], 0)
                else:
                    load_x(xd, xd[LAT:NT, :], 0)
                for t in range(T):
                    pool.wait_ge(*at(f"o{l}.x", 2 * (t + 1)))
                    pool.dma_start(xd[t * P:(t + 1) * P, :], X[:, t, :]).then_inc(s(f"o{l}.x_out"), 16)
                for t in range(T):
                    pool.wait_ge(*at(f"n2{l}.xn", t + 1))
                    pool.dma_start(xn_d[t * P:(t + 1) * P, :], XN[:, t, :]).then_inc(s(f"o{l}.xn_out"), 16)

            def experts(l):
                m = f"e{l}."
                pool.wait_ge(*at(f"o{l}.mm", 18))
                ld(rw, a["moe_router"][l].rearrange("(k p) e -> p k e", p=P), m + "tab")
                ld(lower, tab["lower"], m + "tab")
                ld(iota, tab["iota"], m + "tab")
                pool.wait_ge(*at(f"o{l}.x_out", 16 * T))
                pool.wait_ge(*at(f"o{l}.xn_out", 16 * T))
                pool.wait_ge(*at(m + "affT", 3))
                pool.dma_start(aftd, affT).then_inc(s(m + "aft_out"), 16)
                pool.wait_ge(*at(m + "aft_out", 16))

                def broadcast(e, ee):
                    pool.dma_start(bc[ee].rearrange("p (o t) -> p o t", o=1), aftd[e:e + 1, :].partition_broadcast(P) if isinstance(e, int)
                                   else aftd[bass.ds(e, 1), :].partition_broadcast(P)).then_inc(s(m + f"bc{ee}"), 16)

                def gather(ee):
                    pool.sem_inc(s("e.pool_turn"), 1)
                    pool.indirect_dma_start(
                        out=xs[ee], out_offset=None, in_=xn_d,
                        in_offset=bass.IndirectOffsetOnAxis(ap=idx[:, ee, 0:1], axis=0)).then_inc(s(m + f"xs{ee}"), 16)
                    pool.indirect_dma_start(
                        out=xsc[ee], out_offset=None, in_=xn_d,
                        in_offset=bass.IndirectOffsetOnAxis(ap=idx[0:CAPC, ee, 1:2], axis=0)).then_inc(s(m + f"xs{ee}"), 16)

                broadcast(0, 0)
                broadcast(1, 1)
                pool.wait_ge(*at(m + "idx", 2))
                gather(0)

                def pair(i, last):
                    for ee in range(2):
                        if not last:
                            pool.wait_ge(*at(m + "ranked", 2 * i + ee + 1))
                            broadcast(2 * i + ee + 2, ee)
                        if not (last and ee):
                            pool.wait_ge(*at(m + "idx", 4 * i + 2 * ee + 4))
                            gather(1 - ee)
                        pool.wait_ge(*at(m + "rows", 4 * i + 2 * ee + 2))
                        pool.sem_inc(s("e.pool_turn"), 1)
                        pool.indirect_dma_start(
                            out=xd, out_offset=bass.IndirectOffsetOnAxis(ap=idx[:, ee, 0:1], axis=0), in_=orow[ee],
                            in_offset=None, compute_op=ALU.add).then_inc(s(m + "added"), 16)
                        pool.indirect_dma_start(
                            out=xd, out_offset=bass.IndirectOffsetOnAxis(ap=idx[0:CAPC, ee, 1:2], axis=0),
                            in_=orowc[ee], in_offset=None, compute_op=ALU.add).then_inc(s(m + "added"), 16)
                        pool.wait_ge(*at(m + "added", 64 * i + 32 * ee + 32))
                        pool.sem_inc(s(m + "scattered"), 1)
                each_expert_pair(pool, [], [], pair)

            after_mixer(0)
            experts(0)
            load_x(xd, xd[LAT:NT, :], 1)
            ld(misc[:, 0:2048].rearrange("p (a n) -> p a n", a=2), tab["rope"], "a.rope")
            pool.wait_ge(*at("q.mm", 34))
            ld(cv, a["cache_v"][0, 0].rearrange("t h d -> t (h d)"), "a.cv")
            ld(eb[:, 0, 0, 0:1024], a["cache_k"][0, 0].rearrange("t h d -> t (h d)"), "a.ck")
            pool.wait_ge(*at("q.ev", 34))
            pool.dma_start(out[4][0, 0].rearrange("t h d -> t (h d)"), va[:, 8, :]).then_inc(s("out"), 16)
            pool.wait_ge(*at("a.kctx", 2))
            pool.dma_start(out[3][0, 0].rearrange("t h d -> t (h d)"), eb[:, 1, 0, 0:1024]).then_inc(s("a.kctx_out"), 16)
            pool.wait_ge(*at("a.kctx_out", 16))
            after_mixer(1)
            experts(1)
            load_x(xd, xd[LAT:NT, :], 1)
            ld(misc[:, 0:1024].rearrange("p (o d) -> p o d", o=1), a["final_g"].rearrange("(o d) -> o d", o=1).partition_broadcast(P), "z.g")
            for t in range(T):
                pool.wait_ge(*at("z.y", t + 1))
                dst = out[1][0, t * P:(t + 1) * P, :] if t < 8 else out[0][0]
                pool.dma_start(dst, XN[:, t, :]).then_inc(s("out"), 16)
            pool.wait_ge(*at("r.sctx_out", 32))
            pool.wait_ge(*at("out", 16 + 16 * T))

        even_jobs = ([(even_units[0], "T", c) for c in range(4)] + [(even_units[1], "T", c) for c in range(4)]
                     + [(even_units[2], "N", t) for t in range(T)] + [(even_units[3], "N", t) for t in range(T)]
                     + [(even_units[4 + c // 4], "T", c % 4) for c in range(12)])
        odd_jobs = ([(odd_units[c // 4], "T", c % 4) for c in range(16)]
                    + [(odd_units[4 + u], "N", t) for u in range(2) for t in range(T)])
        steps = [(h, q) for h in range(AH) for q in range(T)]
        tev_of, tot = [], 0
        for h, q in steps:
            tot += 3 if q < 8 else 1
            if q == 8:
                tev_of.append((tot, tot + 3))
                tot += 3
            else:
                tev_of.append((tot, tot))

        @block.tensor
        def _(pe):
            pe.sem_inc(s("e.to"), ahead["e.to"])
            mm = nc.tensor.matmul
            tr = nc.tensor.transpose

            pe.wait_ge(*at("c.rows", 16 * 9))
            pe.wait_ge(*at("c.ident", 16))
            tr(ps[:, 0, 0:P], big[:, 0:P], ident[:, :]).then_inc(s("c.colT"), 1)
            tr(ps[:, 1, 0:73], big[0:73, P:2 * P], ident[0:73, 0:73]).then_inc(s("c.colT"), 1)

            pe.wait_ge(*at("c.cols", 2))
            pe.wait_ge(*at("f.in", 16 * 9))
            for g in range(3):
                i = mm(ps[0:64, g, 0:384], f1w, featT[:, g * 384:(g + 1) * 384], start=True, stop=True)
            i.then_inc(s("f.h12"), 1)
            pe.wait_ge(*at("f.sin", 1))
            for g in range(3):
                i = mm(ps[0:64, 3 + g, 0:384], f2w, harg[:, g * 384:(g + 1) * 384], start=True, stop=True)
            i.then_inc(s("f.h12"), 1)
            pe.wait_ge(*at("f.sin", 2))
            pe.wait_ge(*at("f.dft", 32))
            for o in range(2):
                for t in range(T):
                    for d in range(2):
                        j = 2 * t + d
                        if j >= 4 or o:
                            pe.wait_ge(*at("f.taps", max(18 * o + j - 3, 18 * o)))
                        if o and j == 0:
                            pe.wait_ge(*at("f.spec", 5 * o))
                        mm(ps[:, j % 4, :], h2T[:, t * P:(t + 1) * P], f3w[:, (2 * o + d) * HW:(2 * o + d + 1) * HW],
                           start=True, stop=True).then_inc(s("f.h3"), 1)
                pe.wait_ge(*at("f.taps", 18 * (o + 1)))
                pe.wait_ge(*at("f.ones", 1))
                for g in range(2):
                    i = mm(ps[:, 4 + g, :], ones, facc[:, g, :], start=True, stop=True)
                i.then_inc(s("f.sum"), 1)
                pe.wait_ge(*at("f.fold", o + 1))
                for kt in range(4):
                    if kt >= 2:
                        pe.wait_ge(*at("f.spec", 5 * o + kt - 1))
                    b = 4 * (kt % 2)
                    for f, (m, half) in enumerate(((fwd_c, 0), (fwd_c, 1), (fwd_s, 0), (fwd_s, 1))):
                        for n in range(4):
                            i = mm(ps[:, b + f, :], m[:, 4 * half + n, kt * P:(kt + 1) * P],
                                   FS[:, 4 * half + n, f // 2, :], start=n == 0, stop=n == 3)
                    i.then_inc(s("f.dftmm"), 1)
                pe.wait_ge(*at("f.spec", 5 * o + 3))
                for f in range(2):
                    i = mm(ps[:, f, :], cdft[:, f, :], FS[:, 8, f, :], start=True, stop=True)
                i.then_inc(s("f.dftmm"), 1)

            def modulation(l):
                for u, n in enumerate(mod_units[l]):
                    landed(pe, n)
                    w = slot(n).rearrange("p (k n) -> p k n", k=DK)
                    for j in range(4):
                        o = (4 * u + j) * 2
                        for k in range(DK):
                            i = mm(ps[:, 0, o:o + 2], w[:, k, j * P:(j + 1) * P], scond[:, k, :],
                                   start=k == 0, stop=k == DK - 1)
                    free(i, n)
                pe.wait_ge(*at(f"slot{n % NS}_free", n // NS + 1))

            def norm(p):
                for t in range(T):
                    pe.wait_ge(*at(p + "xn", t + 1))
                    if t >= 4:
                        pe.wait_ge(*at(p + "evA", t - 3))
                        pe.wait_ge(*at(p + "evD", t - 3))
                    for c in range(DK):
                        i = tr(ps[:, 2 * (t % 4) + c // 4, (c % 4) * P:(c % 4 + 1) * P],
                               XN[:, t, c * P:(c + 1) * P], ident[:, :])
                        if c % 4 == 3:
                            i.then_inc(s(p + ("tA", "tD")[c // 4]), 1)
                pe.wait_ge(*at(p + "evA", T))
                pe.wait_ge(*at(p + "evD", T))

            def project(p, jobs):
                for j, (n, kind, c) in enumerate(jobs):
                    landed(pe, n)
                    if j >= 2:
                        pe.wait_ge(*at(p + "ev", j - 1))
                    b = 3 * (j % 2)
                    w = slot(n).rearrange("p (k n) -> p k n", k=DK)
                    for k in range(DK):
                        if kind == "T":
                            for g in range(3):
                                i = mm(ps[:, b + g, 0:384], w[:, k, c * P:(c + 1) * P],
                                       hTv[:, k, g * 384:(g + 1) * 384], start=k == 0, stop=k == DK - 1)
                        else:
                            i = mm(ps[:, b, :], hTv[:, k, c * P:(c + 1) * P], w[:, k, :],
                                   start=k == 0, stop=k == DK - 1)
                    i.then_inc(s(p + "mm"), 1)
                    if j + 1 == len(jobs) or jobs[j + 1][0] != n:
                        pe.wait_ge(*at(p + "mm", j + 1))
                        pe.sem_inc(s(f"slot{n % NS}_free"), 1)
                pe.wait_ge(*at(p + "ev", len(jobs)))

            def retention():
                for t in range(T):
                    if t >= 2:
                        pe.wait_ge(*at("r.ktev", t - 1))
                    for h in range(RH):
                        i = tr(ps[:, 6 + t % 2, h * P:(h + 1) * P], kT[:, h, t * P:(t + 1) * P], ident[:, :])
                    i.then_inc(s("r.kt"), 1)
                pe.wait_ge(*at("r.ktev", T))

                def state(k, c):
                    pe.wait_ge(*at("r.vd", k + 1))
                    if k >= 2:
                        pe.wait_ge(*at("r.st", k - 1))
                    for h in range(RH):
                        i = mm(ps[:, k % 2, h * P:(h + 1) * P], ktok[:, c, h * P:(h + 1) * P],
                               vdec[:, k % 2, h * P:(h + 1) * P], start=True, stop=True)
                    i.then_inc(s("r.stmm"), 1)

                for k in range(7):
                    state(k, 7 - k)
                state(7, 8)
                state(8, 8)
                for c in range(T):
                    if c >= 2:
                        pe.wait_ge(*at("r.sm", c - 1))
                    for h in range(RH):
                        i = mm(ps[:, 2 + c % 2, h * P:(h + 1) * P], kT[:, h, c * P:(c + 1) * P],
                               qT[:, h, c * P:(c + 1) * P], start=True, stop=True)
                    i.then_inc(s("r.sc"), 1)
                    if c < 7:
                        state(9 + c, c)
                    pe.wait_ge(*at("r.sm", c + 1))
                    if c < 8:
                        pe.wait_ge(*at("r.qf", c + 1))
                        if c == 0:
                            pe.wait_ge(*at("r.s0", 32))
                            pe.wait_ge(*at("r.st", 9))
                        else:
                            pe.wait_ge(*at("r.st", 9 + c))
                    if c >= 2:
                        pe.wait_ge(*at("r.oev", c - 1))
                    for h in range(RH):
                        hs = slice(h * P, (h + 1) * P)
                        o = ps[:, 4 + c % 2, hs]
                        i = mm(o, sm[c % 2][:, hs], vtok[:, c, hs], start=True, stop=c == 8)
                        if c < 8:
                            mm(o, qfb[:, 0, hs], sfwd[:, hs], start=False, stop=False)
                            i = mm(o, qfb[:, 1, hs], sbwd[:, c, hs], start=False, stop=True)
                    i.then_inc(s("r.o"), 1)
                for t in range(T):
                    pe.wait_ge(*at("r.on", t + 1))
                    if t >= 2:
                        pe.wait_ge(*at("r.otev", t - 1))
                    for h in range(RH):
                        i = tr(ps[:, 6 + t % 2, h * P:(h + 1) * P], vtok[:, t, h * P:(h + 1) * P], ident[:, :])
                    i.then_inc(s("r.ot"), 1)
                pe.wait_ge(*at("r.otev", T))
                pe.wait_ge(*at("r.oev", T))

            def hyena():
                for o in range(2):
                    uc, us, _, _, ic, is_ = hy_units[o]
                    if o == 0:
                        pe.wait_ge(*at("h.u0", 16))
                    else:
                        pe.wait_ge(*at("h.z", 4))
                    for m in range(T):
                        if m >= 2:
                            pe.wait_ge(*at("h.vtev", T * o + m - 1))
                        for c in range(4):
                            if m < 8:
                                t0 = 2 * (m % 4) * P + m // 4
                                src = zT[0][:, c, t0:t0 + 2 * P - 1:2]
                            else:
                                src = zT[0][:, c, LAT:NT]
                            i = tr(ps[:, 6 + m % 2, c * P:(c + 1) * P], src, ident[:, :])
                        i.then_inc(s("h.vt"), 1)
                    pe.wait_ge(*at("h.vtev", T * (o + 1)))
                    landed(pe, uc)
                    landed(pe, us)
                    fc = slot(uc).rearrange("p (t k) -> p t k", t=8)
                    fs = slot(us).rearrange("p (t k) -> p t k", t=8)
                    for kt in range(5):
                        b = 4 * (kt % 2)
                        if kt >= 2:
                            pe.wait_ge(*at("h.xh", 5 * o + kt - 1))
                        if kt == 4:
                            for f in range(2):
                                i = mm(ps[:, f, :], cdft[:, f, :], vt[:, 8, :], start=True, stop=True)
                        else:
                            for f, (m, half) in enumerate(((fc, 0), (fc, 1), (fs, 0), (fs, 1))):
                                for n in range(4):
                                    i = mm(ps[:, b + f, :], m[:, 4 * half + n, kt * P:(kt + 1) * P],
                                           vt[:, 4 * half + n, :], start=n == 0, stop=n == 3)
                        i.then_inc(s("h.x"), 1)
                    pe.wait_ge(*at("h.x", 5 * (o + 1)))
                    pe.sem_inc(s(f"slot{uc % NS}_free"), 1)
                    pe.sem_inc(s(f"slot{us % NS}_free"), 1)
                    landed(pe, ic)
                    landed(pe, is_)
                    vc = slot(ic).rearrange("p (k t) -> p k t", k=4)
                    vs = slot(is_).rearrange("p (k t) -> p k t", k=4)
                    pe.wait_ge(*at("h.spec", 5 * (o + 1)))
                    for c in range(4):
                        if c >= 2:
                            pe.wait_ge(*at("h.z", 4 * o + c - 1))
                        b = 3 * (c % 2)
                        cs = slice(c * P, (c + 1) * P)
                        for par in range(2):
                            for kt in range(4):
                                mm(ps[:, b + par, :], spec[:, kt, 2 * par, cs], vc[:, kt, par * 512:(par + 1) * 512],
                                   start=kt == 0, stop=False)
                                mm(ps[:, b + par, :], spec[:, kt, 2 * par + 1, cs],
                                   vs[:, kt, par * 512:(par + 1) * 512], start=False, stop=kt == 3)
                        mm(ps[:, b + 2, 0:P], specc[:, 0, cs], cdft[:, 2, :], start=True, stop=False)
                        mm(ps[:, b + 2, 0:P], specc[:, 1, cs], cdft[:, 3, :], start=False, stop=True
                           ).then_inc(s("h.y"), 1)
                    pe.wait_ge(*at("h.y", 4 * (o + 1)))
                    pe.sem_inc(s(f"slot{ic % NS}_free"), 1)
                    pe.sem_inc(s(f"slot{is_ % NS}_free"), 1)
                pe.wait_ge(*at("h.z", 8))

            def out_project(l, us):
                p = f"o{l}."
                for g in range(2):
                    for half in range(2):
                        for c in range(4):
                            i = mm(ps[:, 4 + 2 * g + half, c * P:(c + 1) * P],
                                   modc[:, l, 16 + 4 * half + c, g:g + 1].to_broadcast([P, P]), ident[:, :],
                                   start=True, stop=True)
                i.then_inc(s(p + "g"), 1)
                for t in range(T):
                    for half in range(2):
                        j = 2 * t + half
                        landed(pe, us[half])
                        if j >= 4:
                            pe.wait_ge(*at(p + "x", j - 3))
                        w = slot(us[half]).rearrange("p (k n) -> p k n", k=DK)
                        for k in range(DK):
                            i = mm(ps[:, j % 4, :], yTv[:, k, t * P:(t + 1) * P], w[:, k, :],
                                   start=k == 0, stop=k == DK - 1)
                        i.then_inc(s(p + "mm"), 1)
                pe.wait_ge(*at(p + "mm", 2 * T))
                for n in us:
                    pe.sem_inc(s(f"slot{n % NS}_free"), 1)
                pe.wait_ge(*at(p + "x", 2 * T))
                pe.wait_ge(*at(p + "gev", 4))

            def experts(l):
                m = f"e{l}."
                base = exp_units[l]
                pe.wait_ge(*at(m + "tab", 48))
                for t in range(T):
                    for k in range(DK):
                        i = mm(ps[:, 0, t * NE:(t + 1) * NE], hTv[:, k, t * P:(t + 1) * P], rw[:, k, :],
                               start=k == 0, stop=k == DK - 1)
                i.then_inc(s(m + "lg"), 1)
                pe.wait_ge(*at(m + "aff", 1))
                for t in range(T):
                    i = tr(ps[0:NE, 1 + t // 4, (t % 4) * P:(t % 4 + 1) * P], aff[:, t, :], ident[:, :])
                    if t in (3, 7, 8):
                        i.then_inc(s(m + "at"), 1)
                pe.wait_ge(*at(m + "affT", 3))

                def find(b):
                    for t in range(8):
                        mm(ps[:, 7, 0:2], onehot[:, t, :], tg[:, b, t, :], start=t == 0, stop=t == 7)
                    mm(ps[0:CAPC, 7, 2:4], onehot[:, 8, 0:CAPC], tg[:, b, 8, :], start=True, stop=True
                       ).then_inc(s(m + "ix"), 1)

                def turn_in(b):
                    for c in range(DK):
                        o = (c % 3) * CAP
                        tr(ps[:, c // 3, o:o + CAPL], xs[b][:, c * P:(c + 1) * P], ident[:, :])
                        i = tr(ps[:, c // 3, o + CAPL:o + CAP], xsc[b][:, c * P:(c + 1) * P], ident[0:CAPC, 0:CAPC])
                        if c in (2, 5, 7):
                            i.then_inc(s(m + "ti"), 1)

                pe.wait_ge(*at(m + "oh", 1))
                find(0)
                pe.wait_ge(*at(m + "xs0", 32))
                turn_in(0)

                def pair(i, last):
                    for ee in range(2):
                        n0 = base + 6 * ee
                        w = [slot(n0 + j).rearrange("p (k n) -> p k n", k=DK) for j in range(6)]
                        more = not (last and ee)
                        for f in range(8):
                            ug, uu = n0 + 2 * (f // 4), n0 + 2 * (f // 4) + 1
                            if f % 4 == 0:
                                landed(pe, ug, 48 * i)
                                landed(pe, uu, 48 * i)
                            if f == 0:
                                pe.wait_ge(*at(m + "te", 6 * i + 3 * ee + 3))
                            if f < 2:
                                pe.wait_ge(*at(m + "dn", 16 * i + 8 * ee))
                            else:
                                pe.wait_ge(*at(m + "hid", 16 * i + 8 * ee + f - 1))
                            c = f % 4
                            for g, u in ((0, ug), (1, uu)):
                                for k in range(DK):
                                    last_mm = mm(ps[:, 3 + f % 2, g * CAP:(g + 1) * CAP],
                                                 w[u - n0][:, k, c * P:(c + 1) * P], xsT[ee][:, k, :],
                                                 start=k == 0, stop=k == DK - 1)
                                if c == 3 and g == 0:
                                    free(last_mm, ug)
                            last_mm.then_inc(s(m + "gu"), 1)
                            if c == 3:
                                pe.wait_ge(*at(m + "gu", 16 * i + 8 * ee + f + 1))
                                pe.sem_inc(s(f"slot{uu % NS}_free"), 1)
                        for d in range(8):
                            ud_ = n0 + 4 + d // 4
                            if d % 4 == 0:
                                landed(pe, ud_, 48 * i)
                            if d == 0:
                                pe.wait_ge(*at(m + "hid", 16 * i + 8 * ee + 8))
                            if d == 2 and more:
                                pe.wait_ge(*at(m + "oh", 2 * i + ee + 2))
                                find(1 - ee)
                            if d == 5 and more:
                                pe.wait_ge(*at(m + f"xs{1 - ee}", 32 * i + 32 * (1 + ee)))
                                pe.wait_ge(*at(m + "rows", 4 * i + 2 * ee))
                                turn_in(1 - ee)
                            if d >= 2:
                                pe.wait_ge(*at(m + "dn", 16 * i + 8 * ee + d - 1))
                            for k in range(DK):
                                last_mm = mm(ps[:, 3 + d % 2, 0:CAP], w[4 + d // 4][:, k, (d % 4) * P:(d % 4 + 1) * P],
                                             hid[:, k, :], start=k == 0, stop=k == DK - 1)
                            last_mm.then_inc(s(m + "d"), 1)
                            if d % 4 == 3:
                                pe.wait_ge(*at(m + "d", 16 * i + 8 * ee + d + 1))
                                pe.sem_inc(s(f"slot{ud_ % NS}_free"), 1)
                        pe.wait_ge(*at(m + "dn", 16 * i + 8 * ee + 8))
                        for c in range(DK):
                            t_ = tr(ps[:, 5 + c // 4, (c % 4) * P:(c % 4 + 1) * P], outT[:, c, 0:CAPL], ident[:, :])
                        t_.then_inc(s(m + "to"), 1)
                        if more:
                            pe.wait_ge(*at(m + "te", 6 * i + 3 * ee + 6))
                        for c in range(DK):
                            t_ = tr(ps[0:CAPC, c // 4, (c % 4) * P:(c % 4 + 1) * P], outT[:, c, CAPL:CAP], ident[:, :])
                        t_.then_inc(s(m + "to"), 1)
                each_expert_pair(pe, [], [], pair)
                pe.wait_ge(*at(m + "rows", 2 * NE))

            def attention():
                for h in range(AH):
                    i = tr(ps[:, 6 + h // 4, (h % 4) * P:(h % 4 + 1) * P], kTa[:, h, LAT:NT], ident[:, :])
                i.then_inc(s("a.kt"), 1)
                pe.wait_ge(*at("a.ck", 16))
                for h in range(AH):
                    i = tr(ps[:, 4 + h // 4, (h % 4) * P:(h % 4 + 1) * P], eb[:, 0, 0, h * P:(h + 1) * P], ident[:, :])
                i.then_inc(s("a.kt"), 1)
                pe.wait_ge(*at("a.kctx", 2))
                pe.wait_ge(*at("a.ckT", 2))
                pe.wait_ge(*at("a.cv", 16))
                pe.wait_ge(*at("q.rope", 16))

                def scores(n):
                    h, q = steps[n]
                    for m in range(2):
                        if n:
                            pe.wait_ge(*at("a.e", 2 * (n - 1) + m + 1))
                        r = slice(64 * m, 64 * m + 64)
                        lhs = qTa[r, h, q * P:(q + 1) * P]
                        if q < 8:
                            mm(ps[:, 3 * m, :], lhs, kTa[r, h, 0:512], start=True, stop=True)
                            mm(ps[:, 3 * m + 1, :], lhs, kTa[r, h, 512:1024], start=True, stop=True)
                            i = mm(ps[:, 3 * m + 2, 0:P], lhs, ckT[r, h, :], start=True, stop=True)
                        else:
                            i = mm(ps[:, 3 * m, 0:P], lhs, kTa[r, h, LAT:NT], start=True, stop=True)
                        i.then_inc(s("a.s"), 1)

                def turn(n, src, before, nt):
                    for g in range((nt + 3) // 4):
                        if g == 2:
                            pe.wait_ge(*at("a.tev", before + 1))
                        for t in range(4 * g, min(4 * g + 4, nt)):
                            i = tr(ps[:, 6 + g % 2, (t % 4) * P:(t % 4 + 1) * P], src(t), ident[:, :])
                        i.then_inc(s("a.t"), 1)

                scores(0)
                done = 0
                for n, (h, q) in enumerate(steps):
                    if n + 1 < len(steps):
                        scores(n + 1)
                    pe.wait_ge(*at("a.a", n + 1))
                    pe.wait_ge(*at("a.tev", done))
                    if n:
                        pe.wait_ge(*at("a.oev", n))
                    nt = 9 if q < 8 else 1
                    turn(n, lambda t: eb[:, n % 2, 0, t * P:(t + 1) * P], done, nt)
                    done = tev_of[n][0]
                    pe.wait_ge(*at("a.tev", done))
                    for t in range(nt):
                        v = cv[:, h * P:(h + 1) * P] if t == 8 else va[:, t if q < 8 else 8, h * P:(h + 1) * P]
                        i = mm(ps[:, 7, 0:P], aT[:, t * P:(t + 1) * P], v, start=t == 0, stop=t == nt - 1)
                    i.then_inc(s("a.pv"), 1)
                    if q == 8:
                        pe.wait_ge(*at("a.on", h + 1))
                        turn(n, lambda t: oh[:, t, :], done, 9)
                        done = tev_of[n][1]
                pe.wait_ge(*at("a.tev", done))

            pe.wait_ge(*at("f.spec", 10))
            pe.wait_ge(*at("c.scond", 1))
            modulation(0)
            norm("n10.")
            project("p.", even_jobs)
            retention()
            hyena()
            out_project(0, oute_units)
            norm("n20.")
            experts(0)
            modulation(1)
            norm("n11.")
            project("q.", odd_jobs)
            attention()
            out_project(1, outo_units)
            norm("n21.")
            experts(1)

        @block.scalar
        def _(act):
            act.sem_inc(s("e.dn"), ahead["e.dn"])
            A = nc.scalar.activation
            act.wait_ge(*at("c.cols", 2))
            A(scond[:, :, :].rearrange("p k g -> p g k"), colB[:, 57:73].rearrange("p (g k) -> p g k", g=2),
              ACT.Silu).then_inc(s("c.scond"), 1)
            act.wait_ge(*at("f.arg", 1))
            A(harg, harg, ACT.Sin).then_inc(s("f.sin"), 1)
            act.wait_ge(*at("f.arg", 2))
            A(h2T, harg, ACT.Sin).then_inc(s("f.sin"), 1)
            act.wait_ge(*at("r.d", 1))
            A(dk[:, 2, :], dk[:, 1, :], ACT.Exp, scale=-1.0).then_inc(s("r.da"), 1)
            act.wait_ge(*at("r.d", 2))
            A(dk[:, 3, :], dk[:, 1, :], ACT.Ln).then_inc(s("r.da"), 1)
            act.wait_ge(*at("r.d", 3))
            A(cdec[:, :], dk[:, 0, :], ACT.Exp, scale=float(P)).then_inc(s("r.da"), 1)
            A(kdec[:, :, :], kdec[:, :, :], ACT.Exp).then_inc(s("r.da"), 1)
            A(misc[:, 0:1536], misc[:, 0:1536], ACT.Exp).then_inc(s("r.da"), 1)
            A(rarg, rarg, ACT.Exp).then_inc(s("r.da"), 1)
            A(lamc[:, 2:4], lamc[:, 0:2], ACT.Exp).then_inc(s("r.da"), 1)

            def norm(p, l, n, x_ready):
                for t in range(T):
                    act.wait_ge(*x_ready(t))
                    A(XN[:, t, :], X[:, t, :], ACT.Square, accum_out=stat[:, 0, t:t + 1]).then_inc(s(p + "ssq"), 1)
                act.wait_ge(*at(p + "var", 1))
                A(stat[:, 2, :], stat[:, 1, :], ACT.Sqrt).then_inc(s(p + "std"), 1)
                if l is None:
                    return
                for t in range(T):
                    act.wait_ge(*at(p + "tA", t + 1))
                    g = int(t == 8)
                    for c in range(4):
                        i = A(hTv[:, c, t * P:(t + 1) * P], ps[:, 2 * (t % 4), c * P:(c + 1) * P], ACT.Identity,
                              scale=amul[:, l, n, c, g:g + 1], bias=modc[:, l, 24 * n + c, g:g + 1])
                    i.then_inc(s(p + "evA"), 1)

            def project_even():
                for j in range(len(even_jobs)):
                    act.wait_ge(*at("p.mm", j + 1))
                    b = 3 * (j % 2)
                    three = ps[:, b:b + 3, 0:384]
                    if j < 8:
                        dst = (qT if j < 4 else kT)[:, j % 4, :].rearrange("p (g t) -> p g t", g=3)
                        i = A(dst, three, ACT.Copy, scale=1.0 if j < 4 else float(P) ** -0.5)
                    elif j < 17:
                        i = A(vtok[:, j - 8, :], ps[:, b, :], ACT.Copy)
                    elif j < 26:
                        i = A(gtok[:, j - 17, :], ps[:, b, :], ACT.Silu)
                    else:
                        c = j - 26
                        if c >= 2:
                            act.wait_ge(*at("p.u", c - 1))
                        i = A(raw[c % 2].rearrange("p (g t) -> p g t", g=3), three, ACT.Copy)
                    i.then_inc(s("p.ev"), 1)

            def retention():
                for t in range(T):
                    act.wait_ge(*at("r.kt", t + 1))
                    A(ktok[:, t, :], ps[:, 6 + t % 2, :], ACT.Copy).then_inc(s("r.ktev"), 1)
                for c in range(T):
                    act.wait_ge(*at("r.o", c + 1))
                    act.wait_ge(*at("r.vd", min(9 + c + 1, 16)))
                    A(vtok[:, c, :], ps[:, 4 + c % 2, :], ACT.Copy).then_inc(s("r.oev"), 1)
                act.wait_ge(*at("r.var", 1))
                A(gstf[:, 108:144], gstf[:, 108:144], ACT.Sqrt).then_inc(s("r.std"), 1)
                for t in range(T):
                    act.wait_ge(*at("r.ot", t + 1))
                    A(yTv[:, 4:8, t * P:(t + 1) * P], ps[:, 6 + t % 2, :].rearrange("p (h n) -> p h n", h=RH),
                      ACT.Copy).then_inc(s("r.otev"), 1)

            def hyena():
                for o in range(2):
                    for m in range(T):
                        act.wait_ge(*at("h.vt", T * o + m + 1))
                        A(vt[:, m, :], ps[:, 6 + m % 2, :], ACT.Copy).then_inc(s("h.vtev"), 1)
                    for kt in range(5):
                        act.wait_ge(*at("h.x", 5 * o + kt + 1))
                        if 5 * o + kt:
                            act.wait_ge(*at("h.spec", 5 * o + kt))
                        b = 4 * (kt % 2)
                        nf = 4 if kt < 4 else 2
                        A(xh[:, 0:nf, :], ps[:, b:b + nf, :], ACT.Copy).then_inc(s("h.xh"), 1)

            def gate_rows(l):
                act.wait_ge(*at(f"o{l}.g", 1))
                for g in range(2):
                    for half in range(2):
                        A(grow[:, g, half * 512:(half + 1) * 512], ps[:, 4 + 2 * g + half, :], ACT.Copy
                          ).then_inc(s(f"o{l}.gev"), 1)

            def experts(l):
                m = f"e{l}."
                act.wait_ge(*at(m + "sub", 1))
                A(affm, affm, ACT.Exp).then_inc(s(m + "exp"), 1)
                for g in range(3):
                    act.wait_ge(*at(m + "at", g + 1))
                    w = 512 if g < 2 else P
                    A(affT[:, 512 * g:512 * g + w], ps[0:NE, 1 + g, 0:w], ACT.Copy).then_inc(s(m + "affT"), 1)

                def pair(i, last):
                    for ee in range(2):
                        for f in range(8):
                            act.wait_ge(*at(m + "gu", 16 * i + 8 * ee + f + 1))
                            if f < 2:
                                act.wait_ge(*at(m + "hid", 16 * i + 8 * ee))
                            else:
                                act.wait_ge(*at(m + "hid", 16 * i + 8 * ee + f - 1))
                            A(sg[f % 2], ps[:, 3 + f % 2, 0:CAP], ACT.Silu).then_inc(s(m + "sg"), 1)
                        act.wait_ge(*at(m + "to", 4 * i + 2 * ee))
                        for d in range(8):
                            act.wait_ge(*at(m + "d", 16 * i + 8 * ee + d + 1))
                            A(outT[:, d, 0:CAPL], ps[:, 3 + d % 2, 0:CAPL], ACT.Copy,
                              scale=modc[:, l, 40 + d, 0:1])
                            A(outT[:, d, CAPL:CAP], ps[:, 3 + d % 2, CAPL:CAP], ACT.Copy,
                              scale=modc[:, l, 40 + d, 1:2]).then_inc(s(m + "dn"), 1)
                each_expert_pair(act, [], [], pair)

            def project_odd():
                for j in range(len(odd_jobs)):
                    act.wait_ge(*at("q.mm", j + 1))
                    b = 3 * (j % 2)
                    if j < 16:
                        dst = (qTa if j < 8 else kTa)[:, j % 8, :].rearrange("p (g t) -> p g t", g=3)
                        i = A(dst, ps[:, b:b + 3, 0:384], ACT.Copy)
                    else:
                        if j == 16:
                            act.wait_ge(*at("q.rope", 16))
                        u, t = (j - 16) // T, (j - 16) % T
                        i = A(va[:, t, u * 512:(u + 1) * 512], ps[:, b, :], ACT.Copy)
                    i.then_inc(s("q.ev"), 1)

            def attention():
                act.wait_ge(*at("a.kt", 1))
                for g in range(2):
                    A(eb[:, 1, 0, g * 512:(g + 1) * 512], ps[:, 6 + g, :], ACT.Copy).then_inc(s("a.kctx"), 1)
                act.wait_ge(*at("a.kt", 2))
                for g in range(2):
                    A(ckT[:, 4 * g:4 * g + 4, :], ps[:, 4 + g, :].rearrange("p (h n) -> p h n", h=4), ACT.Copy
                      ).then_inc(s("a.ckT"), 1)
                act.wait_ge(*at("a.kctx_out", 16))
                act.wait_ge(*at("a.ckT", 2))

                def exps(n):
                    h, q = steps[n]
                    w = NT if q < 8 else P
                    if n >= 2:
                        act.wait_ge(*at("a.tev", tev_of[n - 2][0]))
                    for m in range(2):
                        act.wait_ge(*at("a.nm", 2 * n + m + 1))
                        c = (n % 4) * 8
                        A(eb[:, n % 2, m, 0:w], bank(3 * m, 3)[:, 0:w], ACT.Exp, scale=0.125,
                          bias=gstf[:, c + 2 + m:c + 3 + m], accum_out=gstf[:, c + 4 + m:c + 5 + m]
                          ).then_inc(s("a.e"), 1)

                def evacuate(dst, before, nt, **kw):
                    for g in range((nt + 3) // 4):
                        w = min(512, nt * P - 512 * g)
                        act.wait_ge(*at("a.t", before + g + 1))
                        A(dst(512 * g, w), ps[:, 6 + g % 2, 0:w], ACT.Copy, **kw).then_inc(s("a.tev"), 1)

                exps(0)
                done = 0
                for n, (h, q) in enumerate(steps):
                    if n:
                        act.wait_ge(*at("a.pv", n))
                    evacuate(lambda o, w: aT[:, o:o + w], done, 9 if q < 8 else 1)
                    done = tev_of[n][0]
                    if n + 1 < len(steps):
                        exps(n + 1)
                    if q == 8:
                        act.wait_ge(*at("a.var", h + 1))
                        A(gstf[:, 48:57], gstf[:, 48:57], ACT.Sqrt).then_inc(s("a.std"), 1)
                        evacuate(lambda o, w: yTv[:, h, o:o + w], done, 9, scale=lamc[:, 6:7])
                        done = tev_of[n][1]

            norm("n10.", 0, 0, lambda t: at(f"x{t}.landed", 16))
            project_even()
            retention()
            hyena()
            gate_rows(0)
            norm("n20.", 0, 1, lambda t: at("o0.x", 2 * t + 2))
            experts(0)
            norm("n11.", 1, 0, lambda t: at(f"x{t}.landed", 48))
            project_odd()
            attention()
            gate_rows(1)
            norm("n21.", 1, 1, lambda t: at("o1.x", 2 * t + 2))
            experts(1)
            norm("z.", None, 0, lambda t: at(f"x{t}.landed", 80))

        @block.vector
        def _(dve):
            ts, tt, stt = nc.vector.tensor_scalar, nc.vector.tensor_tensor, nc.vector.scalar_tensor_tensor
            cp, rec, ms = nc.vector.tensor_copy, nc.vector.reciprocal, nc.vector.memset
            ch = Chain(dve, "dve.chain")
            dve.sem_inc(s("e.rows"), ahead["e.rows"])
            dve.sem_inc(s("e.hid"), ahead["e.hid"])

            ms(ones, 1.0).then_inc(s("f.ones"), 1)
            dve.wait_ge(*at("c.colT", 2))
            cp(colA[:, :], ps[:, 0, 0:P]).then_inc(s("c.cols"), 1)
            cp(colB[:, 0:73], ps[:, 1, 0:73]).then_inc(s("c.cols"), 1)

            dve.wait_ge(*at("f.in", 16 * 9))
            for i in range(2):
                dve.wait_ge(*at("f.h12", i + 1))
                src = ps[0:64, 3 * i:3 * i + 3, 0:384]
                v3 = harg.rearrange("p (g t) -> p g t", g=3)
                ch(ts(v3, src, fcol[:, 2 * i:2 * i + 1], fcol[:, 2 * i + 1:2 * i + 2], ALU.add, ALU.mult))
                ch(ts(hrnd, harg, 1.0 / (2 * math.pi), MAGIC, ALU.mult, ALU.add))
                ch(ts(hrnd, hrnd, -MAGIC, None, ALU.add))
                ch(stt(harg, hrnd, -6.28125, harg, ALU.mult, ALU.add))
                ch(stt(harg, hrnd, -(2 * math.pi - 6.28125), harg, ALU.mult, ALU.add))
                ts(harg, harg, 3.1415925, -3.1415925, ALU.min, ALU.max).then_inc(s("f.arg"), 1)
            for o in range(2):
                ch(ms(facc, 0.0))
                if o:
                    dve.wait_ge(*at("f.spec_out", 64))
                    dve.wait_ge(*at("f.specc_out", 16))
                for t in range(T):
                    for d in range(2):
                        dve.wait_ge(*at("f.h3", 18 * o + 2 * t + d + 1))
                        tt(FH[:, t, d, :], ps[:, (2 * t + d) % 4, :], win[:, t, :], ALU.mult).then_inc(s("f.h3r"), 1)
                        dve.wait_ge(*at("f.h3r", 18 * o + 2 * t + d + 1))
                        g = int(t == 8)
                        ch(stt(hrow, FH[:, t, d, :], -1.0, FH[:, t, d, :], ALU.mult, ALU.max))
                        tt(facc[:, g, :], hrow, facc[:, g, :], ALU.add).then_inc(s("f.taps"), 1)
                        dve.wait_ge(*at("f.taps", 18 * o + 2 * t + d + 1))
                ms(FH[0:1, 0, 1, :], 0.0)
                ch(ms(FH[0:1, 8, 1, :], 0.0))
                for t in range(T):
                    tt(FS[:, t, 0, :], FH[:, t, 0, :], FH[:, t, 1, :], ALU.add)
                    tt(FS[:, t, 1, :], FH[:, t, 0, :], FH[:, t, 1, :], ALU.subtract)
                dve.wait_ge(*at("f.sum", o + 1))
                ch(ts(facc, ps[:, 4:6, :], EPS, None, ALU.add))
                rec(facc, facc).then_inc(s("f.fold"), 1)
                dve.wait_ge(*at("f.fold", o + 1))
                for kt in range(5):
                    dve.wait_ge(*at("f.dftmm", 5 * o + kt + 1))
                    if kt == 4:
                        for f in range(2):
                            i = tt(fstagec[:, f, :], ps[:, f, :], facc[:, 1, :], ALU.mult)
                        i.then_inc(s("f.spec"), 1)
                        dve.wait_ge(*at("f.spec", 5 * o + 5))
                        continue
                    b = 4 * (kt % 2)
                    for f in range(4):
                        i = tt(ftmp[:, f, :], ps[:, b + f, :], facc[:, 0, :], ALU.mult)
                    ch(i)
                    if kt >= 2:
                        dve.wait_ge(*at("f.spec_out", 16 * (4 * o + kt - 1)))
                    st = fstage[:, kt % 2]
                    tt(st[:, 0, :], ftmp[:, 0, :], ftmp[:, 1, :], ALU.add)
                    tt(st[:, 1, :], ftmp[:, 2, :], ftmp[:, 3, :], ALU.add)
                    tt(st[:, 2, :], ftmp[:, 0, :], ftmp[:, 1, :], ALU.subtract)
                    tt(st[:, 3, :], ftmp[:, 2, :], ftmp[:, 3, :], ALU.subtract).then_inc(s("f.spec"), 1)
                    dve.wait_ge(*at("f.spec", 5 * o + kt + 1))

            dve.wait_ge(*at("r.tab", 16 * 6))
            dve.wait_ge(*at("c.small", 32))
            for i in range(2):
                ch(nc.vector.tensor_tensor_reduce(rarg[:, 0:64], lamv[:, 2 * i, :], lamv[:, 2 * i + 1, :], 1.0, 0.0,
                                                  ALU.mult, ALU.add, lamc[:, i:i + 1]))
            stt(dk[:, 1, :], dk[:, 0, :], -1.0, dk[:, 0, :], ALU.mult, ALU.max).then_inc(s("r.d"), 1)
            dve.wait_ge(*at("r.da", 1))
            ch(ts(dk[:, 1, :], dk[:, 2, :], 1.0, None, ALU.add))
            ts(dk[:, 4, :], dk[:, 1, :], -1.0, None, ALU.add).then_inc(s("r.d"), 1)
            dve.wait_ge(*at("r.d", 2))
            dve.wait_ge(*at("r.da", 2))
            ch(ts(dk[:, 1, :], dk[:, 4, :], 1e-30, None, ALU.max))
            ch(rec(dk[:, 1, :], dk[:, 1, :]))
            ch(tt(dk[:, 3, :], dk[:, 3, :], dk[:, 1, :], ALU.mult))
            ch(stt(dk[:, 1, :], dk[:, 4, :], 0.0, dk[:, 3, :], ALU.is_equal, ALU.add))
            ch(tt(dk[:, 1, :], dk[:, 1, :], dk[:, 2, :], ALU.mult))
            ch(stt(dk[:, 0, :], dk[:, 0, :], 0.0, dk[:, 1, :], ALU.min, ALU.subtract))
            for d in range(2):
                ts(kdec[:, d, :], dk[:, 0, 4 * d:4 * d + 4], small[:, d:d + 1], None, ALU.mult)
                for h in range(RH):
                    lg = dk[:, 0, 4 * d + h:4 * d + h + 1]
                    dst = (rmask if d == 0 else rarg)[:, h * P:(h + 1) * P]
                    ts(dst, rtab[:, d, :], lg, None, ALU.mult)
                    i = ts(qdec[:, d, h * P:(h + 1) * P], rtab[:, 4 + d, :], lg, None, ALU.mult)
            i.then_inc(s("r.d"), 1)
            dve.wait_ge(*at("r.da", 7))
            heads = lambda x: x.rearrange("p (h n) -> p h n", h=RH)
            over = lambda x: x.rearrange("p (o n) -> p o n", o=1).to_broadcast([P, RH, P])
            tt(heads(rmask), heads(rmask), over(rtab[:, 2, :]), ALU.mult)
            ch(tt(heads(rarg), heads(rarg), over(rtab[:, 3, :]), ALU.mult))
            ch(tt(rmask, rmask, rarg, ALU.add))
            ch(tt(lamc[:, 4:5], lamc[:, 3:4], lamc[:, 2:3], ALU.subtract))
            ch(ts(lamc[:, 4:5], lamc[:, 4:5], -LAM_INIT, None, ALU.add))
            ch(ts(lamc[:, 6:7], colB[:, 56:57], 1.0 - LAM_INIT, None, ALU.mult))

            def modulation(l):
                n = mod_units[l][-1]
                dve.wait_ge(*at(f"slot{n % NS}_free", n // NS + 1))
                bm = colA[:, 48 * l:48 * l + 48].rearrange("p (j o) -> p j o", o=1).to_broadcast([P, 48, 2])
                ch(tt(modc[:, l, :, :], ps[:, 0, 0:96].rearrange("p (j g) -> p j g", g=2), bm, ALU.add))
                for i in range(2):
                    g = colA[:, 96 + 16 * i + 8 * l:104 + 16 * i + 8 * l].rearrange("p (j o) -> p j o", o=1)
                    ch(stt(amul[:, l, i, :, :], modc[:, l, 8 + 24 * i:16 + 24 * i, :], 1.0,
                           g.to_broadcast([P, 8, 2]), ALU.add, ALU.mult))

            def rstd(p):
                dve.wait_ge(*at(p + "ssq", T))
                ts(stat[:, 1, :], stat[:, 0, :], 1.0 / D, EPS, ALU.mult, ALU.add).then_inc(s(p + "var"), 1)
                dve.wait_ge(*at(p + "std", 1))
                ch(rec(stat[:, 1, :], stat[:, 2, :]))

            def norm(p, l, n):
                rstd(p)
                for t in range(T):
                    ts(XN[:, t, :], X[:, t, :], stat[:, 1, t:t + 1], None, ALU.mult).then_inc(s(p + "xn"), 1)
                for t in range(T):
                    dve.wait_ge(*at(p + "tD", t + 1))
                    g = int(t == 8)
                    for c in range(4, 8):
                        i = ts(hTv[:, c, t * P:(t + 1) * P], ps[:, 2 * (t % 4) + 1, (c - 4) * P:(c - 3) * P],
                               amul[:, l, n, c, g:g + 1], modc[:, l, 24 * n + c, g:g + 1], ALU.mult, ALU.add)
                    i.then_inc(s(p + "evD"), 1)

            def short_conv():
                for c in range(12):
                    dve.wait_ge(*at("p.ev", 26 + c + 1))
                    if c >= 2:
                        dve.wait_ge(*at(f"p.u_out{c % 2}", 16 * (c // 2)))
                    r, u = raw[c % 2], ubuf[c % 2]
                    w = [colB[:, 12 * i + c:12 * i + c + 1] for i in range(3)]
                    ch(ts(u, r, w[1], colB[:, 36 + c:37 + c], ALU.mult, ALU.add))
                    for lo, hi in ((0, LAT), (LAT, NT)):
                        i = stt(u[:, lo + 1:hi], r[:, lo:hi - 1], w[0], u[:, lo + 1:hi], ALU.mult, ALU.add)
                    ch(i)
                    for lo, hi in ((0, LAT), (LAT, NT)):
                        i = stt(u[:, lo:hi - 1], r[:, lo + 1:hi], w[2], u[:, lo:hi - 1], ALU.mult, ALU.add)
                    i.then_inc(s("p.u"), 1)

            def retention():
                for b in range(2):
                    dve.wait_ge(*at(f"p.u_out{b}", 16 * 6))
                dve.wait_ge(*at("r.s0", 32))
                tile_of = [7, 6, 5, 4, 3, 2, 1, 8, 8, 0, 1, 2, 3, 4, 5, 6]
                dir_of = [1] * 7 + [1, 0] + [0] * 7

                def decay_values(k):
                    kd_ = kdec[:, dir_of[k], :].rearrange("p (h o) -> p h o", o=1).to_broadcast([P, RH, P])
                    tt(heads(vdec[:, k % 2, :]), heads(vtok[:, tile_of[k], :]), kd_, ALU.mult).then_inc(s("r.vd"), 1)

                decay_values(0)
                decay_values(1)
                for k in range(7):
                    dve.wait_ge(*at("r.stmm", k + 1))
                    c = 7 - k
                    for h in range(RH):
                        hs = slice(h * P, (h + 1) * P)
                        i = stt(sbwd[:, c - 1, hs], sbwd[:, c, hs], cdec[:, 4 + h:5 + h], ps[:, k % 2, hs],
                                ALU.mult, ALU.add)
                    i.then_inc(s("r.st"), 1)
                    dve.wait_ge(*at("r.st", k + 1))
                    decay_values(k + 2)
                for k in (7, 8):
                    dve.wait_ge(*at("r.stmm", k + 1))
                    d = dir_of[k]
                    cp(sctx[:, d, :], ps[:, k % 2, :]).then_inc(s("r.st"), 1)
                    decay_values(k + 2)
                for c in range(T):
                    dve.wait_ge(*at("r.sc", c + 1))
                    if c >= 2:
                        dve.wait_ge(*at("r.o", c - 1))
                    tt(sm[c % 2], ps[:, 2 + c % 2, :], rmask, ALU.mult).then_inc(s("r.sm"), 1)
                    if c < 8:
                        if c >= 1:
                            dve.wait_ge(*at("r.o", c))
                        for d in range(2):
                            i = tt(heads(qfb[:, d, :]), qT[:, :, c * P:(c + 1) * P], heads(qdec[:, d, :]), ALU.mult)
                        i.then_inc(s("r.qf"), 1)
                    if c < 7:
                        k = 9 + c
                        dve.wait_ge(*at("r.stmm", k + 1))
                        dve.wait_ge(*at("r.o", c + 1))
                        for h in range(RH):
                            hs = slice(h * P, (h + 1) * P)
                            i = stt(sfwd[:, hs], sfwd[:, hs], cdec[:, h:h + 1], ps[:, k % 2, hs], ALU.mult, ALU.add)
                        i.then_inc(s("r.st"), 1)
                        dve.wait_ge(*at("r.st", k + 1))
                        if k + 2 < 16:
                            decay_values(k + 2)
                for t in range(T):
                    dve.wait_ge(*at("r.oev", t + 1))
                    for h in range(RH):
                        i = nc.vector.bn_stats(bnb[:, 4 * t + h, :], vtok[:, t, h * P:(h + 1) * P])
                    ch(i)
                    for h in range(RH):
                        i = nc.vector.bn_aggr(gmv[:, 4 * t + h, :], bnb[:, 4 * t + h:4 * t + h + 1, :])
                ch(i)
                ts(gstf[:, 108:144], gmv[:, :, 1], EPS, None, ALU.add).then_inc(s("r.var"), 1)
                dve.wait_ge(*at("r.std", 1))
                ch(rec(gstf[:, 72:108], gstf[:, 108:144]))
                for t in range(T):
                    for h in range(RH):
                        j = 4 * t + h
                        v = vtok[:, t, h * P:(h + 1) * P]
                        i = ts(v, v, gmv[:, j, 0:1], gstf[:, 72 + j:73 + j], ALU.subtract, ALU.mult)
                    ch(i)
                    tt(vtok[:, t, :], vtok[:, t, :], gtok[:, t, :], ALU.mult).then_inc(s("r.on"), 1)

            def hyena():
                dve.wait_ge(*at("h.kctx", 16))
                dve.wait_ge(*at("r.sctx_out", 32))
                for o in range(2):
                    xq3 = xq.rearrange("p (q f) c -> p q f c", q=2)
                    A2 = xh[:, 0:2, :]
                    B2 = xh[:, 2:4, :]
                    for kt in range(4):
                        n = hy_units[o][2 + kt // 2]
                        dve.wait_ge(*at("h.xh", 5 * o + kt + 1))
                        xf = xh.rearrange("p (f e) c -> p f e c", f=2)
                        tt(xq3[:, 0, :, :], xf[:, :, 0, :], xf[:, :, 1, :], ALU.add)
                        ch(tt(xq3[:, 1, :, :], xf[:, :, 0, :], xf[:, :, 1, :], ALU.subtract))
                        if kt % 2 == 0:
                            landed(dve, n)
                        K = slot(n).rearrange("p (b q f c) -> p b q f c", b=2, q=2, f=2)[:, kt % 2]
                        xr, xs_, kr, ks = xq3[:, :, 0, :], xq3[:, :, 1, :], K[:, :, 0, :], K[:, :, 1, :]
                        tt(A2, xr, kr, ALU.mult)
                        ch(tt(B2, xs_, ks, ALU.mult))
                        ch(tt(A2, A2, B2, ALU.subtract))
                        tt(B2, xr, ks, ALU.mult)
                        ch(tt(xs_, xs_, kr, ALU.mult))
                        if kt % 2 == 1:
                            dve.sem_inc(s(f"slot{n % NS}_free"), 1)
                        ch(tt(B2, B2, xs_, ALU.add))
                        if o and kt == 0:
                            dve.wait_ge(*at("h.y", 4))
                        tt(spec[:, kt, 0, :], xh[:, 0, :], xh[:, 1, :], ALU.add)
                        tt(spec[:, kt, 1, :], xh[:, 2, :], xh[:, 3, :], ALU.add)
                        tt(spec[:, kt, 2, :], xh[:, 0, :], xh[:, 1, :], ALU.subtract)
                        tt(spec[:, kt, 3, :], xh[:, 2, :], xh[:, 3, :], ALU.subtract).then_inc(s("h.spec"), 1)
                    dve.wait_ge(*at("h.xh", 5 * o + 5))
                    kr, ks = kctx[:, o, 0, :], kctx[:, o, 1, :]
                    tt(xq[:, 0, :], xh[:, 0, :], kr, ALU.mult)
                    tt(xq[:, 1, :], xh[:, 1, :], ks, ALU.mult)
                    tt(xq[:, 2, :], xh[:, 0, :], ks, ALU.mult)
                    ch(tt(xq[:, 3, :], xh[:, 1, :], kr, ALU.mult))
                    tt(specc[:, 0, :], xq[:, 0, :], xq[:, 1, :], ALU.subtract)
                    tt(specc[:, 1, :], xq[:, 2, :], xq[:, 3, :], ALU.add).then_inc(s("h.spec"), 1)
                    dve.wait_ge(*at(f"h.u{o + 1}", 16))
                    for c in range(4):
                        dve.wait_ge(*at("h.y", 4 * o + c + 1))
                        z = zT[0][:, c, :]
                        hb = colB[:, 48 + 4 * o + c:49 + 4 * o + c]
                        b = 3 * (c % 2)
                        stt(z[:, 0:LAT:2], z[:, 0:LAT:2], hb, ps[:, b, :], ALU.mult, ALU.add)
                        stt(z[:, 1:LAT:2], z[:, 1:LAT:2], hb, ps[:, b + 1, :], ALU.mult, ALU.add)
                        ch(stt(z[:, LAT:NT], z[:, LAT:NT], hb, ps[:, b + 2, 0:P], ALU.mult, ALU.add))
                        dst = z if o == 0 else yTv[:, c, :]
                        tt(dst, z, zT[1 + o][:, c, :], ALU.mult).then_inc(s("h.z"), 1)

            def out_project(l):
                p = f"o{l}."
                dve.wait_ge(*at(p + "gev", 4))
                for t in range(T):
                    g = int(t == 8)
                    dve.wait_ge(*at(f"x{t}.landed", 16 * (2 + 2 * l)))
                    for half in range(2):
                        hs = slice(512 * half, 512 * half + 512)
                        dve.wait_ge(*at(p + "mm", 2 * t + half + 1))
                        ch(tt(XN[:, t, hs], ps[:, (2 * t + half) % 4, :], grow[:, g, hs], ALU.mult))
                        tt(X[:, t, hs], X[:, t, hs], XN[:, t, hs], ALU.add).then_inc(s(p + "x"), 1)

            def experts(l, per):
                m = f"e{l}."
                dve.wait_ge(*at(m + "tab", 48))
                dve.wait_ge(*at(m + "lg", 1))
                lg = ps[:, 0, 0:144].rearrange("p (t e) -> p t e", t=T)
                wide = lambda x: x.rearrange("p (t o) -> p t o", o=1).to_broadcast([P, T, NE])
                ch(nc.vector.tensor_reduce(rowmax[:, 0, :], lg, AX.X, ALU.max))
                tt(affm, lg, wide(rowmax[:, 0, :]), ALU.subtract).then_inc(s(m + "sub"), 1)
                dve.wait_ge(*at(m + "exp", 1))
                ch(nc.vector.tensor_reduce(rowmax[:, 1, :], affm, AX.X, ALU.add))
                ch(rec(rowmax[:, 1, :], rowmax[:, 1, :]))
                tt(aff, affm, wide(rowmax[:, 1, :]), ALU.mult).then_inc(s(m + "aff"), 1)
                dve.wait_ge(*at(m + "aff", 1))
                for b in range(2):
                    cp(tg[:, b, :, 0], small[:, 2:11])
                dve.wait_ge(*at(f"o{l}.xn_out", 16 * T))
                dve.wait_ge(*at(f"o{l}.x_out", 16 * T))
                ch(ms(cnt, 0.0))

                def column(b, e):
                    src = aff[:, :, e:e + 1] if isinstance(e, int) else aff[:, :, bass.ds(e, 1)]
                    ch(cp(tg[:, b, :, 1:2], src))

                def rank_tile(b, t):
                    mine = tg[:, b, t, 1:2]
                    lo, hi = (0, LAT) if t < 8 else (LAT, NT)
                    t0 = P * t
                    if t0 > lo:
                        ch(ts(junk[:, 0:t0 - lo], bc[b][:, lo:t0], mine, 0.0, ALU.is_ge, ALU.add,
                              accum_out=cnt[:, t, 0:1]))
                    ch(ts(junk[:, 0:hi - t0], bc[b][:, t0:hi], mine, 0.0, ALU.is_gt, ALU.add,
                          accum_out=cnt[:, t, 1:2]))
                    ch(stt(junk[:, 0:P], bc[b][:, t0:t0 + P], mine, lower, ALU.is_equal, ALU.mult,
                           accum_out=cnt[:, t, 2:3]))

                def finish_rank(b, n):
                    rank_tile(b, 8)
                    nc.vector.tensor_reduce(rank, cnt, AX.X, ALU.add).then_inc(s(m + "ranked"), 1)
                    dve.wait_ge(*at(m + "ranked", n + 1))
                    for t in range(T):
                        i = ts(onehot[:, t, :], iota, rank[:, t:t + 1], None, ALU.is_equal)
                    i.then_inc(s(m + "oh"), 1)

                def found(b, n):
                    cp(gate[:, b, 0:1], ps[:, 7, 1:2])
                    cp(gate[0:CAPC, b, 1:2], ps[0:CAPC, 7, 3:4])
                    cp(idx[:, b, 0:1], ps[:, 7, 0:1]).then_inc(s(m + "idx"), 1)
                    cp(idx[0:CAPC, b, 1:2], ps[0:CAPC, 7, 2:3]).then_inc(s(m + "idx"), 1)

                def columns_in(b, n):
                    for bk, cs in enumerate(((0, 1, 2), (3, 4, 5), (6, 7))):
                        dve.wait_ge(*at(m + "ti", n + bk + 1))
                        for c in cs:
                            o = (c % 3) * CAP
                            for g, (lo, hi) in enumerate(((0, CAPL), (CAPL, CAP))):
                                i = ts(xsT[b][:, c, lo:hi], ps[:, bk, o + lo:o + hi], amul[:, l, 1, c, g:g + 1],
                                       modc[:, l, 24 + c, g:g + 1], ALU.mult, ALU.add)
                        i.then_inc(s(m + "te"), 1)

                dve.wait_ge(*at(m + "bc0", 16))
                column(0, 0)
                for t in range(8):
                    rank_tile(0, t)
                finish_rank(0, 0)
                dve.wait_ge(*at(m + "ix", 1))
                found(0, 0)
                columns_in(0, 0)

                def pair(i, last):
                    for ee in range(2):
                        more = not (last and ee)
                        b = 1 - ee
                        if more:
                            dve.wait_ge(*at(m + f"bc{b}", 16 * i + 16 * (1 + ee)))
                            column(b, 2 * i + ee + 1)
                        for f in range(8):
                            dve.wait_ge(*at(m + "sg", 16 * i + 8 * ee + f + 1))
                            tt(hid[:, f, :], sg[f % 2], ps[:, 3 + f % 2, CAP:2 * CAP], ALU.mult
                               ).then_inc(s(m + "hid"), 1)
                            if more:
                                rank_tile(b, f)
                        if more:
                            finish_rank(b, 2 * i + ee + 1)
                            dve.wait_ge(*at(m + "ix", 2 * i + ee + 2))
                            dve.wait_ge(*at(m + "scattered", 2 * i + ee))
                            found(b, 0)
                            columns_in(b, 6 * i + 3 * ee + 3)
                        else:
                            dve.wait_ge(*at(m + "scattered", 2 * i + ee))
                        for g in range(2):
                            dve.wait_ge(*at(m + "to", 4 * i + 2 * ee + g + 1))
                            n = CAPL if g == 0 else CAPC
                            dst = orow[ee] if g == 0 else orowc[ee]
                            b0 = 5 if g == 0 else 0
                            ts(dst, bank(b0, 2)[0:n, :], gate[0:n, ee, g:g + 1], None, ALU.mult
                               ).then_inc(s(m + "rows"), 1)
                each_expert_pair(dve, [ch], [per], pair)

            def rope():
                tmp = va[:, 0, :]
                swap = [(i + 16) % 32 for i in range(32)]
                dve.wait_ge(*at("a.rope", 16))
                for j in range(16):
                    dve.wait_ge(*at("q.ev", j + 1))
                    v = (qTa if j < 8 else kTa)[:, j % 8, 0:LAT]
                    ch(nc.vector.stream_shuffle(tmp, v, swap))
                    tt(tmp, tmp, sinT, ALU.mult)
                    ch(tt(v, v, cosT, ALU.mult))
                    tt(v, v, tmp, ALU.add).then_inc(s("q.rope"), 1)
                    dve.wait_ge(*at("q.rope", j + 1))

            def attention():
                def maxima(n):
                    h, q = steps[n]
                    w = NT if q < 8 else P
                    c = (n % 4) * 8
                    for m in range(2):
                        dve.wait_ge(*at("a.s", 2 * n + m + 1))
                        ch(nc.vector.tensor_reduce(gstf[:, c + m:c + m + 1], bank(3 * m, 3)[:, 0:w], AX.X, ALU.max))
                        ts(gstf[:, c + 2 + m:c + 3 + m], gstf[:, c + m:c + m + 1], -0.125, None, ALU.mult
                           ).then_inc(s("a.nm"), 1)

                maxima(0)
                for n, (h, q) in enumerate(steps):
                    w = NT if q < 8 else P
                    c = (n % 4) * 8
                    dve.wait_ge(*at("a.e", 2 * n + 2))
                    ch(rec(gstf[:, c + 6:c + 8], gstf[:, c + 4:c + 6]))
                    ch(tt(gstf[:, c + 7:c + 8], gstf[:, c + 7:c + 8], lamc[:, 4:5], ALU.mult))
                    e0, e1 = eb[:, n % 2, 0, 0:w], eb[:, n % 2, 1, 0:w]
                    ch(ts(e0, e0, gstf[:, c + 6:c + 7], None, ALU.mult))
                    stt(e0, e1, gstf[:, c + 7:c + 8], e0, ALU.mult, ALU.add).then_inc(s("a.a"), 1)
                    if n + 1 < len(steps):
                        maxima(n + 1)
                    dve.wait_ge(*at("a.pv", n + 1))
                    if q == 0 and h:
                        dve.wait_ge(*at("a.tev", tev_of[n - 1][1]))
                    cp(oh[:, q, :], ps[:, 7, 0:P]).then_inc(s("a.oev"), 1)
                    dve.wait_ge(*at("a.oev", n + 1))
                    i = stt(junk2, oh[:, q, :], 1.0, oh[:, q, :], ALU.mult, ALU.mult, accum_out=gstf[:, 36 + q:37 + q])
                    if q == 8:
                        ch(i)
                        ts(gstf[:, 48:57], gstf[:, 36:45], 1.0 / P, EPS, ALU.mult, ALU.add).then_inc(s("a.var"), 1)
                        dve.wait_ge(*at("a.std", h + 1))
                        ch(rec(gstf[:, 60:69], gstf[:, 48:57]))
                        for t in range(T):
                            i = ts(oh[:, t, :], oh[:, t, :], gstf[:, 60 + t:61 + t], None, ALU.mult)
                        i.then_inc(s("a.on"), 1)
                dve.wait_ge(*at("a.on", AH))
                dve.sem_inc(s("m1.big_free"), 1)

            modulation(0)
            norm("n10.", 0, 0)
            short_conv()
            retention()
            hyena()
            dve.wait_ge(*at("h.z", 8))
            dve.sem_inc(s("m0.big_free"), 1)
            out_project(0)
            norm("n20.", 0, 1)
            experts(0, 52)
            modulation(1)
            norm("n11.", 1, 0)
            rope()
            attention()
            out_project(1)
            norm("n21.", 1, 1)
            experts(1, 52)
            rstd("z.")
            dve.wait_ge(*at("z.g", 16))
            for t in range(T):
                stt(XN[:, t, :], X[:, t, :], stat[:, 1, t:t + 1], misc[:, 0:1024], ALU.mult, ALU.mult
                    ).then_inc(s("z.y"), 1)


_OUTS = [(1, CTX, D), (1, LAT, D), (1, 1, 2, RH, P, P), (1, 1, CTX, AH, P), (1, 1, CTX, AH, P)]


def kernel(**inputs):
    import concourse.bacc as bacc
    from concourse.bass_utils import run_bass_kernel_spmd

    nc = bacc.Bacc("TRN2", target_bir_lowering=False, num_devices=1, dynamic_dma_scratch_size=SCRATCH)
    arrays, a, tab = {}, {}, {}
    for name, v in inputs.items():
        arrays["in_" + name] = np.ascontiguousarray(v)
        a[name] = nc.dram_tensor("in_" + name, v.shape, F32, kind="ExternalInput").ap()
    for name, v in tables().items():
        arrays["tab_" + name] = v
        tab[name] = nc.dram_tensor("tab_" + name, v.shape, F32, kind="ExternalInput").ap()
    out = [nc.dram_tensor(f"out_{i}", shape, F32, kind="ExternalOutput").ap() for i, shape in enumerate(_OUTS)]
    build(nc, a, out, tab)
    r = run_bass_kernel_spmd(nc, [arrays], core_ids=[0])
    return tuple(r.results[0][f"out_{i}"] for i in range(len(_OUTS)))
```

```python
from contextlib import ExitStack
import math

import numpy as np

import concourse.bass as bass
from concourse import mybir

ALU = mybir.AluOpType
ACT = mybir.ActivationFunctionType
AX = mybir.AxisListType
F32 = mybir.dt.float32
U32 = mybir.dt.uint32

P = 128
D = 1024
DK = D // P
LAT, CTX = 1024, 128
NT = LAT + CTX
T = NT // P
HW = 512
RH = 4
AH = 8
NE = 16
CAPL, CAPC = 2 * LAT // NE, 2 * CTX // NE
CAP = CAPL + CAPC
EPS = 1e-6
NS = 4
U = 4096
LAM_INIT = 0.8 - 0.6 * math.exp(-0.3)
SCRATCH = 2048
MAGIC = 12582912.0


def tables():
    def order(L):
        return np.concatenate([np.arange(0, L, 2), np.arange(1, L, 2)])
    t = {}
    n = order(LAT).astype(np.float64)
    w = 2 * np.pi * (np.arange(512) + 0.5) / (2 * LAT)
    for name, f in (("cos", np.cos), ("sin", np.sin)):
        m = f(n[:, None] * w[None, :])
        t["fwd_" + name] = m.reshape(8, P, 512).transpose(1, 0, 2)
        t["inv_" + name] = (m.T / LAT).reshape(4, P, LAT).transpose(1, 0, 2)
    nc_ = np.arange(CTX, dtype=np.float64)
    wc = 2 * np.pi * (np.arange(CTX) + 0.5) / (2 * CTX)
    a = nc_[:, None] * wc[None, :]
    t["ctx_dft"] = np.stack([np.cos(a), np.sin(a), np.cos(a).T / CTX, np.sin(a).T / CTX], 1)

    feats, wins = [], []
    for L in (LAT, CTX):
        pos = np.arange(L, dtype=np.float32)
        tt = pos / np.float32(L - 1)
        ww = np.float32(2.0 * math.pi) * pos / np.float32(L)
        f = np.linspace(1e-4, 15, 16, dtype=np.float32)
        wf = ww[:, None] * f[None, :]
        ft = np.concatenate([tt[:, None], np.cos(wf), -np.sin(wf)], -1)
        dl = np.linspace(math.log(1e-2) / 1.5, math.log(1e-2) / 0.3, HW, dtype=np.float32)
        wn = np.exp(-tt[:, None] * np.abs(dl)[None, :])
        o = order(L) if L == LAT else np.arange(L)
        feats.append(ft[o])
        wins.append(wn[o])
    t["feat"] = np.concatenate(feats, 0).T
    t["window"] = np.concatenate(wins, 0).reshape(T, P, HW).transpose(1, 0, 2)

    i = np.arange(P, dtype=np.float64)
    dji = i[None, :] - i[:, None]
    t["decay"] = np.stack([np.maximum(dji, 0), np.maximum(-dji, 0), dji >= 0, dji <= 0,
                           np.broadcast_to(i[None, :] + 1, (P, P)), np.broadcast_to(P - i[None, :], (P, P))], 1)
    small = np.zeros((P, 16))
    small[:, 0] = P - 1 - i
    small[:, 1] = i
    small[:, 12] = i % 32 == 0
    small[:, 13] = i % 32 == 1
    small[:, 2:11] = i[:, None] + P * np.arange(T)[None, :]
    t["small"] = small
    t["ident"] = np.eye(P)
    t["pick"] = i[:, None] % 32 == np.arange(NE)[None, :]
    t["lower"] = (dji < 0)
    t["iota"] = np.broadcast_to(i[None, :], (P, P))

    fr = (10000.0 ** (-np.arange(16, dtype=np.float32) / np.float32(16))).astype(np.float32)
    tok = np.arange(LAT)
    d = np.arange(P) % 64
    where = np.where((d // 32)[:, None] == 0, (tok // 64)[None, :], (tok % 64)[None, :]).astype(np.float32)
    ang = where * fr[d % 16][:, None]
    sign = np.where((d % 32) < 16, -1.0, 1.0)[:, None]
    t["rope"] = np.stack([np.cos(ang), np.sin(ang) * sign], 1)
    for h in range(2):
        t[f"fwd{h}"] = np.stack([np.reshape(t["fwd_" + f], (P, 8, 512))[:, :, 256 * h:256 * h + 256]
                                 for f in ("cos", "sin")], 1).reshape(P, U)
        t[f"inv{h}"] = np.stack([np.reshape(t["inv_" + f], (P, 4, 1024))[:, 2 * h:2 * h + 2]
                                 for f in ("cos", "sin")], 1).reshape(P, U)
    del t["inv_cos"], t["inv_sin"]
    return {k: np.ascontiguousarray(v.astype(np.float32)) for k, v in t.items()}


def build(nc, a, out, tab):
    with ExitStack() as ctx:
        def sb(name, shape, dt=F32):
            return ctx.enter_context(nc.sbuf_tensor(name, shape, dt))

        made = {}

        shared = {"n10.": ("n.", 0), "n20.": ("n.", 1), "n11.": ("n.", 2), "n21.": ("n.", 3), "z.": ("n.", 4),
                  "o0.": ("o.", 0), "o1.": ("o.", 1), "e0.": ("e.", 0), "e1.": ("e.", 1),
                  "m0.": ("m.", 0), "m1.": ("m.", 1)}
        adds = {"n.ssq": T, "n.var": 3, "n.std": 3, "n.xn": T, "n.tA": T, "n.tD": T, "n.evA": T, "n.evD": T,
                "n.y": 0, "n.g": 0,
                "o.g": 1, "o.gev": 4, "o.mm": 2 * T, "o.x": 2 * T, "o.x_out": 16 * T, "o.xn_out": 16 * T,
                "m.big_free": 1,
                "e.tab": 64, "e.lg": 4, "e.lpart": 3, "e.sub": 1, "e.exp": 1, "e.aff": 1, "e.at": 3, "e.affT": 3,
                "e.aft_out": 16, "e.bc0": 8 * NE, "e.bc1": 8 * NE, "e.oh": NE, "e.ranked": NE, "e.ix": NE,
                "e.idx": 2 * NE, "e.xs0": 16 * NE, "e.xs1": 16 * NE, "e.ti": 3 * NE, "e.te": 3 * NE,
                "e.gu": 8 * NE, "e.sg": 8 * NE, "e.hid": 8 * NE, "e.d": 8 * NE, "e.dn": 8 * NE,
                "e.to": 2 * NE, "e.rows": 2 * NE, "e.added": 32 * NE, "e.scattered": NE}

        def common(name):
            head, _, tail = name.partition(".")
            pre, k = shared.get(head + ".", (head + ".", 0))
            return (pre + tail if _ else name), k

        def s(name):
            name = common(name)[0]
            if name not in made:
                made[name] = ctx.enter_context(nc.semaphore(name))
            return made[name]

        ahead = {"e.dn": 1, "e.to": 1, "e.rows": 1, "e.hid": 1, "e.scattered": 1}

        def at(name, value):
            base, k = common(name)
            value = value + (k * adds[base] if k else 0)
            return s(name), (value + ahead[base] if base in ahead else value)

        ring = sb("ring", [P, NS, U])
        hT = sb("hT", [P, DK * NT])
        yT = sb("yT", [P, DK * NT])
        big = sb("big", [P, 2 * T * D])
        misc = sb("misc", [P, 2048])
        ident = sb("ident_sb", [P, P])
        colA = sb("colA", [P, P])
        colB = sb("colB", [P, 80])
        modc = sb("modc", [P, 2, 48, 2])
        amul = sb("amul", [P, 2, 2, 8, 2])
        scond = sb("scond", [P, 8, 2])
        tmp16 = sb("tmp16", [P, 8, 2])
        small = sb("small_sb", [P, 16])
        stat = sb("stat", [P, 3, T])
        cdft = sb("cdft", [P, 4, P])
        fcol = sb("fcol", [64, 4])
        dk = sb("dk", [P, 5, 8])
        kdec = sb("kdec", [P, 2, 4])
        cdec = sb("cdec", [P, 8])
        gst = sb("gst", [P, 3, T * 8])
        lamc = sb("lamc", [P, 8])
        gstf = gst[:, :, :].rearrange("p a t -> p (a t)")
        ones = gstf[:, 0:P]
        gmv = gstf[:, 0:72].rearrange("p (j c) -> p j c", c=2)
        ps = ctx.enter_context(nc.psum_tensor("ps", [P, 8, 512], F32))

        def bank(b, n=1):
            return ps[:, b:b + n, :].rearrange("p b n -> p (b n)")

        xd = nc.dram_tensor("x_res", [NT, D], F32, kind="Internal").ap()
        xn_d = nc.dram_tensor("x_normed", [NT, D], F32, kind="Internal").ap()
        ud = nc.dram_tensor("hy_u", [12, P, NT], F32, kind="Internal").ap()
        kd = nc.dram_tensor("hy_spec", [2, 2, P, U], F32, kind="Internal").ap()
        kcd = nc.dram_tensor("hy_spec_ctx", [P, 2, 2, HW], F32, kind="Internal").ap()
        aftd = nc.dram_tensor("aff_t", [NE, NT], F32, kind="Internal").ap()

        units = []

        def unit(src, ready=None):
            units.append((src, ready))
            return len(units) - 1

        def w_units(w, cols):
            return [unit(w[:, c:c + 512].rearrange("(k p) n -> p k n", p=P)) for c in cols]

        mod_units = w_units(a["w_mod"][0], range(0, 6144, 512)) + w_units(a["w_mod"][1], range(0, 6144, 512))
        even_units = w_units(a["w_in_even"][0], [1536, 2048, 2560, 3072, 0, 512, 1024])
        hy_units = []
        for o in range(2):
            hy_units.append([unit(tab["fwd0"]), unit(tab["fwd1"]),
                             unit(kd[o, 0], ("f.spec_out", 16 * 4 * (o + 1))), unit(kd[o, 1], None),
                             unit(tab["inv0"]), unit(tab["inv1"])])
        oute_units = w_units(a["w_out_even"][0], [0, 512])
        exp_units = {}

        def expert_src(l, e, j):
            w = a[("moe_wg", "moe_wu", "moe_wg", "moe_wu", "moe_wd", "moe_wd")[j]]
            c = (0, 0, 512, 512, 0, 512)[j]
            return w[l, e, :, c:c + 512]

        exp_units[0] = len(units)
        units += [None] * (6 * NE)
        odd_units = w_units(a["w_in_odd"][0], range(0, 3072, 512))
        outo_units = w_units(a["w_out_odd"][0], [0, 512])
        exp_units[1] = len(units)
        units += [None] * (6 * NE)

        def slot(n):
            return ring[:, n % NS, :]

        def landed(eng, n, more=0):
            eng.wait_ge(*at(f"slot{n % NS}_landed", 16 * (n // NS + 1) + more))

        def free(ins, n):
            ins.then_inc(s(f"slot{n % NS}_free"), 1)

        hTv = hT[:, :].rearrange("p (k t) -> p k t", k=DK)
        yTv = yT[:, :].rearrange("p (k t) -> p k t", k=DK)
        X = big[:, 0:T * D].rearrange("p (t d) -> p t d", t=T)
        XN = big[:, T * D:2 * T * D].rearrange("p (t d) -> p t d", t=T)
        FH = big[:, 0:9216].rearrange("p (t d c) -> p t d c", t=T, d=2)
        FS = big[:, 9216:18432].rearrange("p (t d c) -> p t d c", t=T, d=2)
        fwd_c = hT[:, 0:4096].rearrange("p (t k) -> p t k", t=8)
        fwd_s = hT[:, 4096:8192].rearrange("p (t k) -> p t k", t=8)
        facc = hT[:, 8192:9216].rearrange("p (g c) -> p g c", g=2)
        win = yT[:, 0:4608].rearrange("p (t c) -> p t c", t=T)
        featT = yT[0:33, 4608:4608 + NT]
        harg = yT[0:64, 5760:5760 + NT]
        hrnd = yT[0:64, 6912:6912 + NT]
        h2T = yT[0:64, 8064:8064 + NT]
        f1w = big[0:33, 256:320]
        f2w = big[0:64, 320:384]
        fstage = big[:, 0:4096].rearrange("p (b f c) -> p b f c", b=2, f=4)
        fstagec = big[:, 4096:5120].rearrange("p (f c) -> p f c", f=2)
        ftmp = big[:, 5120:7168].rearrange("p (f c) -> p f c", f=4)
        f3w = misc[0:64, :]
        habs = [big[:, 9216 + 512 * i:9728 + 512 * i] for i in range(2)]
        mrow = [yT[:, 4608 + 512 * i:5120 + 512 * i] for i in range(2)]
        qT = big[:, 0:4608].rearrange("p (h t) -> p h t", h=4)
        kT = big[:, 4608:9216].rearrange("p (h t) -> p h t", h=4)
        vtok = big[:, 9216:13824].rearrange("p (t c) -> p t c", t=T)
        gtok = big[:, 13824:18432].rearrange("p (t c) -> p t c", t=T)
        ktok = hT[:, 0:4608].rearrange("p (t c) -> p t c", t=T)
        sbwd = hT[:, 4608:8704].rearrange("p (c n) -> p c n", c=8)
        sfwd = hT[:, 8704:9216]
        raw = [yT[:, i * NT:(i + 1) * NT] for i in range(2)]
        ubuf = [yT[:, (2 + i) * NT:(3 + i) * NT] for i in range(2)]
        rtab = yT[:, 6912:7680].rearrange("p (a n) -> p a n", a=6)
        lamv = yT[:, 7680:7936].rearrange("p (a n) -> p a n", a=4)
        rarg = yT[:, 5760:6272]
        rmask = misc[:, 0:512]
        qdec = misc[:, 512:1536].rearrange("p (d n) -> p d n", d=2)
        sm = [yT[:, i * 512:(i + 1) * 512] for i in range(2)]
        qfb = [yT[:, i:i + 1024].rearrange("p (d n) -> p d n", d=2) for i in (1024, 3072)]
        vdec = yT[:, 2048:3072].rearrange("p (d n) -> p d n", d=2)
        sctx = yT[:, 3072:4096].rearrange("p (d n) -> p d n", d=2)
        bnb = yT[:, 4096:4312].rearrange("p (j c) -> p j c", c=6)
        zT = [big[:, i * 4608:(i + 1) * 4608].rearrange("p (c t) -> p c t", c=4) for i in range(3)]
        vt = big[:, 13824:18432].rearrange("p (t c) -> p t c", t=T)
        spec = hT[:, 0:8192].rearrange("p (k f c) -> p k f c", k=4, f=4)
        specc = hT[:, 8192:9216].rearrange("p (f c) -> p f c", f=2)
        xh = yT[:, 0:2048].rearrange("p (f c) -> p f c", f=4)
        xq = yT[:, 2048:4096].rearrange("p (f c) -> p f c", f=4)
        kctx = misc[:, :].rearrange("p (o f c) -> p o f c", o=2, f=2)
        grow = misc[:, :].rearrange("p (g d) -> p g d", g=2)
        kTa = big[:, 0:9216].rearrange("p (h t) -> p h t", h=AH)
        va = big[:, 9216:18432].rearrange("p (t d) -> p t d", t=T)
        qTa = yTv
        cosT = misc[:, 0:1024]
        sinT = misc[:, 1024:2048]
        eb = hT[:, 0:4608].rearrange("p (b m k) -> p b m k", b=2, m=2)
        aT = hT[:, 4608:5760]
        oh = hT[:, 5760:6912].rearrange("p (t d) -> p t d", t=T)
        cv = hT[:, 6912:7936]
        ckT = hT[:, 7936:8960].rearrange("p (h t) -> p h t", h=AH)
        ohs = [oh, misc[:, 0:1152].rearrange("p (t d) -> p t d", t=T)]
        qz = misc[:, 1152:1664].rearrange("p (b m t) -> p b m t", b=2, m=2)
        junk2 = misc[:, 1664:1792]
        ckrow = misc[:, 0:1024]
        xs = [big[:, i * D:(i + 1) * D] for i in range(2)]
        xsc = [big[0:CAPC, (2 + i) * D:(3 + i) * D] for i in range(2)]
        xsT = [big[:, 4096 + i * 1152:4096 + (i + 1) * 1152].rearrange("p (k c) -> p k c", k=8) for i in range(2)]
        hid = big[:, 6400:7552].rearrange("p (k c) -> p k c", k=8)
        sg = [big[:, 7552 + i * CAP:7552 + (i + 1) * CAP] for i in range(3)]
        outT = big[:, 8064:9216].rearrange("p (k c) -> p k c", k=8)
        orow = [big[:, 9216 + i * D:9216 + (i + 1) * D] for i in range(2)]
        orowc = [big[0:CAPC, 11264 + i * D:11264 + (i + 1) * D] for i in range(2)]
        bc = [big[:, 13312 + i * NT:13312 + (i + 1) * NT] for i in range(2)]
        onehot = big[:, 15616:16768].rearrange("p (t n) -> p t n", t=T)
        junk = big[:, 16768:17920]
        aff = yT[:, 0:144].rearrange("p (t e) -> p t e", t=T)
        affm = yT[:, 144:288].rearrange("p (t e) -> p t e", t=T)
        affT = yT[0:NE, 512:512 + NT]
        tg = yT[:, 1664:1664 + 36].rearrange("p (b t c) -> p b t c", b=2, t=T)
        cnt = yT[:, 1700:1727].rearrange("p (t c) -> p t c", t=T)
        rank = yT[:, 1727:1736]
        rowmax = yT[:, 1736:1754].rearrange("p (c t) -> p c t", c=2)
        gate = yT[:, 1754:1762].rearrange("p (b c) -> p b c", b=2)
        idx = yT[:, 1762:1770].bitcast(U32).rearrange("p (b c) -> p b c", b=2)
        lower = yT[:, 1792:1920]
        iota = yT[:, 1920:2048]
        rw = yT[:, 2048:2176]
        pick = yT[:, 2176:2192]
        lpart = yT[:, 2304:2304 + NT]

        by_three = ((0, 1, 2), (3, 4, 5), (6, 7, 8))
        at_first = ((6, 7, 8), (0, 1, 2), (3, 4, 5))

        mods = iter(range(len(mod_units)))
        start_plan = []
        for i in range(2):
            start_plan += [("sine", i, 0), ("mod", next(mods), 0)]
        for o in range(2):
            for j in range(2 * T):
                start_plan.append(("tap", o, j))
                if j % 3 == 2:
                    start_plan.append(("mod", next(mods), 0))
            start_plan.append(("sum", o, 0))
            for j in range(9):
                start_plan.append(("dft", o, j))
                if j % 4 < (3, 2)[o] and j < 8:
                    start_plan.append(("mod", next(mods), 0))
        assert next(mods, None) is None

        even_jobs = ([(even_units[0], "T", c) for c in range(4)] + [(even_units[1], "T", c) for c in range(4)]
                     + [(even_units[2], "N", t) for t in range(T)] + [(even_units[3], "N", t) for t in range(T)]
                     + [(even_units[4 + c // 4], "T", c % 4) for c in range(12)])
        odd_jobs = ([(odd_units[c // 4], "T", c % 4) for c in range(16)]
                    + [(odd_units[4 + u], "N", t) for u in range(2) for t in range(T)])
        steps = [(h, q) for h in range(AH) for q in range(T)]
        head_step = 2
        tev_of, head_tev, tot = [], [], 0
        for h, q in steps:
            tot += 3 if q < 8 else 1
            tev_of.append(tot)
            if q == head_step and h:
                tot += 3
                head_tev.append(tot)
        head_tev.append(tot + 3)
        block = ctx.enter_context(nc.Block())

        class Chain:

            def __init__(self, eng, name):
                self.eng, self.sem, self.n, self.off = eng, s(name), 0, 0

            def raised(self, ins):
                ins.then_inc(self.sem, 1)
                self.n += 1

            def __call__(self, ins):
                self.raised(ins)
                self.eng.wait_ge(self.sem, self.off + self.n)

        def each_expert_pair(eng, chains, per, body):
            start = [c.n for c in chains]
            with eng.Fori(0, 7) as i:
                for c, n in zip(chains, per):
                    c.off = i * n
                body(i, False)
            for c, n, n0 in zip(chains, per, start):
                assert c.n - n0 == n, (c.n - n0, n)
                c.off, c.n = 0, n0 + 7 * n
            body(7, True)

        @block.sync
        def _(sp):
            def first(dst, src, name):
                sp.dma_start(dst, src).then_inc(s(name), 16)

            def load(n):
                src, ready = units[n]
                if ready:
                    sp.wait_ge(*at(ready[0], ready[1]))
                if n >= NS:
                    sp.wait_ge(*at(f"slot{n % NS}_free", n // NS))
                dst = slot(n) if len(src.shape) == 2 else slot(n).rearrange("p (k n) -> p k n", k=src.shape[1])
                sp.dma_start(dst, src).then_inc(s(f"slot{n % NS}_landed"), 16)

            def experts(l):
                base = exp_units[l]

                def pair(i, last):
                    for ee in range(2):
                        for j in range(6):
                            n = base + 6 * ee + j
                            sp.wait_ge(*at(f"slot{n % NS}_free", n // NS + 3 * i))
                            sp.dma_start(slot(n).rearrange("p (k n) -> p k n", k=DK),
                                         expert_src(l, 2 * i + ee, j).rearrange("(k p) n -> p k n", p=P)
                                         ).then_inc(s(f"slot{n % NS}_landed"), 16)
                each_expert_pair(sp, [], [], pair)

            r0 = 0
            for name, n in (("b_mod", 96), ("norm1_g", 16), ("norm2_g", 16)):
                v = a[name].rearrange("l (r c) -> (l r) c", c=P)
                first(big[r0:r0 + n, 0:P], v, "c.rows")
                r0 += n
            r0 = 0
            for v, n in ((a["hy_short_w"][0].rearrange("s (r c) -> (s r) c", c=P), 36),
                         (a["hy_short_b"][0].rearrange("(r c) -> r c", c=P), 12),
                         (a["hy_bias"][0].rearrange("o (r c) -> (o r) c", c=P), 8),
                         (a["subln_g"], 1),
                         (a["c"].rearrange("o (r c) -> (o r) c", c=P), 8),
                         (a["c_ctx"].rearrange("(r c) -> r c", c=P), 8)):
                first(big[r0:r0 + n, P:2 * P], v, "c.rows")
                r0 += n
            first(ident[:, :], tab["ident"], "c.ident")
            first(featT, tab["feat"], "f.in")
            for i, name in enumerate(("hy_f1_b", "hy_freq1", "hy_f2_b", "hy_freq2")):
                first(fcol[:, i:i + 1], a[name][0].rearrange("(p o) -> p o", o=1), "f.in")
            first(big[0:33, 256:320], a["hy_f1_w"][0], "f.in")
            first(big[0:64, 320:384], a["hy_f2_w"][0], "f.in")
            first(f3w, a["hy_f3_w"][0], "f.in")
            load(0)
            first(win, tab["window"], "f.win")

            for n in range(1, exp_units[0]):
                load(n)
            experts(0)
            for n in range(exp_units[0] + 6 * NE, exp_units[1]):
                load(n)
            experts(1)

        @block.gpsimd
        def _(pool):
            def ld(dst, src, name):
                pool.dma_start(dst, src).then_inc(s(name), 16)

            pool.sem_inc(s("e.scattered"), ahead["e.scattered"])
            ld(small[:, :], tab["small"], "c.small")
            ld(cdft[:, :, :], tab["ctx_dft"], "c.small")
            pool.wait_ge(*at("c.rows", 16 * 9))
            pool.wait_ge(*at("f.in", 16 * 8))
            ld(fwd_c, tab["fwd_cos"], "f.dft")
            ld(fwd_s, tab["fwd_sin"], "f.dft")

            def load_x(src_l, src_c, tiles=range(T)):
                for t in tiles:
                    src = src_l[t * P:(t + 1) * P, :] if t < 8 else src_c
                    ld(X[:, t, :], src, f"x{t}.landed")

            for o in range(2):
                if o == 1:
                    pool.wait_ge(*at("f.fold", 2))
                    load_x(a["x_sample"][0], a["x_prompt"][0], (8, 7))
                for kt in range(4):
                    pool.wait_ge(*at("f.spec", 9 * o + 2 * kt + 2))
                    pool.dma_start(kd[o, kt // 2, :, (kt % 2) * 2048:(kt % 2 + 1) * 2048],
                                   fstage[:, kt % 2].rearrange("p f c -> p (f c)")).then_inc(s("f.spec_out"), 16)
                    pool.wait_ge(*at("f.spec_out", 16 * (4 * o + kt + 1)))
                pool.wait_ge(*at("f.spec", 9 * (o + 1)))
                pool.dma_start(kcd[:, o, :, :], fstagec).then_inc(s("f.specc_out"), 16)
                if o == 1:
                    load_x(a["x_sample"][0], a["x_prompt"][0], (6, 5, 0, 1, 2, 3))
                pool.wait_ge(*at("f.specc_out", 16 * (o + 1)))
            load_x(a["x_sample"][0], a["x_prompt"][0], (4,))
            ld(rtab, tab["decay"], "r.tab")
            ld(dk[:, 0:1, :], a["ret_decay"].rearrange("o d h -> o (d h)").partition_broadcast(P), "r.tab")
            for i, name in enumerate(("lam_q1", "lam_k1", "lam_q2", "lam_k2")):
                ld(lamv[:, i:i + 1, :], a[name].partition_broadcast(P), "r.tab")
            for j in range(12):
                pool.wait_ge(*at("p.u", j + 1))
                pool.dma_start(ud[j], ubuf[j % 2]).then_inc(s(f"p.u_out{j % 2}"), 16)
            for b in range(2):
                pool.wait_ge(*at(f"p.u_out{b}", 16 * 6))
            pool.wait_ge(*at("p.ev", 4 + 4 + 9 + 9 + 12))
            pool.wait_ge(*at("p.mm", 4 + 4 + 9 + 9 + 12))
            for d, dst in ((0, sfwd), (1, sbwd[:, 7, :])):
                ld(dst.rearrange("p (h n) -> p h n", h=RH),
                   a["state_ret"][0, 0, d].rearrange("h p n -> p h n"), "r.s0")
            pool.wait_ge(*at("r.st", 9))
            for d in range(2):
                pool.dma_start(out[2][0, 0, d].rearrange("h p n -> p h n"),
                               sctx[:, d, :].rearrange("p (h n) -> p h n", h=RH)).then_inc(s("r.sctx_out"), 16)
            pool.wait_ge(*at("r.o", T))
            for i in range(3):
                if i == 2:
                    pool.wait_ge(*at("r.otev", T))
                ld(zT[i], ud[4 * i:4 * i + 4].rearrange("c p t -> p c t"), f"h.u{i}")
            ld(kctx, kcd, "h.kctx")

            def after_mixer(l):
                pool.wait_ge(*at(f"m{l}.big_free", 1))
                if l == 0:
                    load_x(a["x_sample"][0], a["x_prompt"][0])
                else:
                    load_x(xd, xd[LAT:NT, :])
                for tiles in by_three:
                    for t in tiles:
                        pool.wait_ge(*at(f"o{l}.x", 2 * (t + 1)))
                        pool.dma_start(xd[t * P:(t + 1) * P, :], X[:, t, :]).then_inc(s(f"o{l}.x_out"), 16)
                    if tiles[0] == 6:
                        pool.wait_ge(*at(f"o{l}.mm", 18))
                        m = f"e{l}."
                        ld(rw.rearrange("p (k e) -> p k e", k=DK),
                           a["moe_router"][l].rearrange("(k p) e -> p k e", p=P), m + "tab")
                        ld(pick, tab["pick"], m + "tab")
                        ld(lower, tab["lower"], m + "tab")
                        ld(iota, tab["iota"], m + "tab")
                    for t in tiles:
                        pool.wait_ge(*at(f"n2{l}.xn", t + 1))
                        pool.dma_start(xn_d[t * P:(t + 1) * P, :], XN[:, t, :]).then_inc(s(f"o{l}.xn_out"), 16)

            def experts(l):
                m = f"e{l}."
                pool.wait_ge(*at(f"o{l}.x_out", 16 * T))
                pool.wait_ge(*at(f"o{l}.xn_out", 16 * T))
                pool.wait_ge(*at(m + "affT", 3))
                pool.dma_start(aftd, affT).then_inc(s(m + "aft_out"), 16)
                pool.wait_ge(*at(m + "aft_out", 16))

                def broadcast(e, ee):
                    row = aftd[e:e + 1, :] if isinstance(e, int) else aftd[bass.ds(e, 1), :]
                    pool.dma_start(bc[ee].rearrange("p (o t) -> p o t", o=1), row.partition_broadcast(P)
                                   ).then_inc(s(m + f"bc{ee}"), 16)

                def gather(ee):
                    pool.sem_inc(s("e.pool_turn"), 1)
                    pool.indirect_dma_start(
                        out=xs[ee], out_offset=None, in_=xn_d,
                        in_offset=bass.IndirectOffsetOnAxis(ap=idx[:, ee, 0:1], axis=0)).then_inc(s(m + f"xs{ee}"), 16)
                    pool.indirect_dma_start(
                        out=xsc[ee], out_offset=None, in_=xn_d,
                        in_offset=bass.IndirectOffsetOnAxis(ap=idx[0:CAPC, ee, 1:2], axis=0)).then_inc(s(m + f"xs{ee}"), 16)

                broadcast(0, 0)
                broadcast(1, 1)
                pool.wait_ge(*at(m + "idx", 2))
                gather(0)

                def pair(i, last):
                    for ee in range(2):
                        if not last:
                            pool.wait_ge(*at(m + "ranked", 2 * i + ee + 1))
                            broadcast(2 * i + ee + 2, ee)
                        if not (last and ee):
                            pool.wait_ge(*at(m + "idx", 4 * i + 2 * ee + 4))
                            gather(1 - ee)
                        pool.wait_ge(*at(m + "rows", 4 * i + 2 * ee + 2))
                        pool.sem_inc(s("e.pool_turn"), 1)
                        pool.indirect_dma_start(
                            out=xd, out_offset=bass.IndirectOffsetOnAxis(ap=idx[:, ee, 0:1], axis=0), in_=orow[ee],
                            in_offset=None, compute_op=ALU.add).then_inc(s(m + "added"), 16)
                        pool.indirect_dma_start(
                            out=xd, out_offset=bass.IndirectOffsetOnAxis(ap=idx[0:CAPC, ee, 1:2], axis=0),
                            in_=orowc[ee], in_offset=None, compute_op=ALU.add).then_inc(s(m + "added"), 16)
                        pool.wait_ge(*at(m + "added", 64 * i + 32 * ee + 32))
                        pool.sem_inc(s(m + "scattered"), 1)
                each_expert_pair(pool, [], [], pair)

            after_mixer(0)
            experts(0)
            load_x(xd, xd[LAT:NT, :])
            ld(misc[:, 0:2048].rearrange("p (a n) -> p a n", a=2), tab["rope"], "a.rope")
            def queries(n):
                h, q = steps[n]
                if n >= 2:
                    pool.wait_ge(*at("a.s", 2 * n - 2))
                for m in range(2):
                    r = slice(64 * m, 64 * m + 64)
                    i = nc.gpsimd.tensor_copy(qz[r, n % 2, m, :], qTa[r, h, q * P:(q + 1) * P])
                i.then_inc(s("a.qz"), 1)

            pool.wait_ge(*at("q.rope", 16))
            ld(ckrow, a["cache_k"][0, 0].rearrange("t h d -> t (h d)"), "a.ck")
            nc.gpsimd.memset(qz, 0.0).then_inc(s("a.qz0"), 1)
            pool.wait_ge(*at("a.qz0", 1))
            queries(0)
            queries(1)
            pool.wait_ge(*at("q.mm", 34))
            ld(cv, a["cache_v"][0, 0].rearrange("t h d -> t (h d)"), "a.cv")
            pool.wait_ge(*at("a.kctx", 2))
            pool.dma_start(out[3][0, 0].rearrange("t h d -> t (h d)"), eb[:, 1, 0, 0:1024]).then_inc(s("a.kctx_out"), 16)
            pool.wait_ge(*at("q.ev", 34))
            pool.dma_start(out[4][0, 0].rearrange("t h d -> t (h d)"), va[:, 8, :]).then_inc(s("out"), 16)
            pool.wait_ge(*at("a.kctx_out", 16))
            for n in range(2, len(steps)):
                queries(n)
            after_mixer(1)
            experts(1)
            ld(misc[:, 0:1024].rearrange("p (o d) -> p o d", o=1),
               a["final_g"].rearrange("(o d) -> o d", o=1).partition_broadcast(P), "z.g")
            load_x(xd, xd[LAT:NT, :])
            for t in range(T):
                pool.wait_ge(*at("z.y", t + 1))
                dst = out[1][0, t * P:(t + 1) * P, :] if t < 8 else out[0][0]
                pool.dma_start(dst, XN[:, t, :]).then_inc(s("out"), 16)
            pool.wait_ge(*at("r.sctx_out", 32))
            pool.wait_ge(*at("out", 16 + 16 * T))


        @block.tensor
        def _(pe):
            pe.sem_inc(s("e.to"), ahead["e.to"])
            mm = nc.tensor.matmul
            tr = nc.tensor.transpose

            pe.wait_ge(*at("c.rows", 16 * 9))
            pe.wait_ge(*at("c.ident", 16))
            tr(ps[:, 0, 0:P], big[:, 0:P], ident[:, :]).then_inc(s("c.colT"), 1)
            tr(ps[:, 1, 0:73], big[0:73, P:2 * P], ident[0:73, 0:73]).then_inc(s("c.colT"), 1)

            pe.wait_ge(*at("c.cols", 2))
            pe.wait_ge(*at("f.in", 16 * 8))

            def sine_layer(n):
                if n:
                    pe.wait_ge(*at("f.sin", n))
                w, src = ((f1w, featT), (f2w, harg))[n]
                for g in range(3):
                    i = mm(ps[0:64, 3 * n + g, 0:384], w, src[:, g * 384:(g + 1) * 384], start=True, stop=True)
                i.then_inc(s("f.h12"), 1)

            pe.wait_ge(*at("c.scond", 1))
            pe.wait_ge(*at("c.small", 32))
            pe.wait_ge(*at("mod.zero", 1))
            sel = small[:, 12:14].rearrange("p (o c) -> p o c", o=1).to_broadcast([P, 48, 2])

            def mod_rows(n):
                landed(pe, mod_units[n])
                if n:
                    pe.wait_ge(*at("mod.rowev", n))
                w = slot(mod_units[n]).rearrange("p (k n) -> p k n", k=DK)
                for k in range(DK):
                    g = k % 4
                    i = mm(ps[32 * g:32 * g + 2, 6, :], scond[:, k, :], w[:, k, :],
                           start=k < 4, stop=k >= 4, tile_position=(0, 32 * g))
                i.then_inc(s("mod.rows"), 1)

            def mod_cols(n):
                pe.wait_ge(*at("mod.rowev", n + 1))
                if n:
                    pe.wait_ge(*at("mod.colev", n))
                for j in range(4):
                    i = mm(ps[:, 7, 96 * j:96 * j + 96], mrow[n % 2][:, j * P:(j + 1) * P], sel, start=True, stop=True)
                i.then_inc(s("mod.cols"), 1)

            for kind, o, j in start_plan:
                if kind == "sine":
                    sine_layer(o)
                elif kind == "tap":
                    if j == 0 and o == 0:
                        pe.wait_ge(*at("f.sin", 2))
                    if j >= 4 or o:
                        pe.wait_ge(*at("f.taps", max(18 * o + j - 3, 18 * o)))
                    if o and j == 0:
                        pe.wait_ge(*at("f.spec", 9))
                    t, d = j // 2, j % 2
                    mm(ps[:, j % 4, :], h2T[:, t * P:(t + 1) * P], f3w[:, (2 * o + d) * HW:(2 * o + d + 1) * HW],
                       start=True, stop=True).then_inc(s("f.h3"), 1)
                elif kind == "mod":
                    if o:
                        mod_cols(o - 1)
                    mod_rows(o)
                elif kind == "sum":
                    pe.wait_ge(*at("f.acc", 18 * (o + 1)))
                    for g in range(2):
                        i = mm(ps[:, 4 + g, :], ones, facc[:, g, :], start=True, stop=True)
                    i.then_inc(s("f.sum"), 1)
                    pe.wait_ge(*at("f.fold", o + 1))
                else:
                    if j == 0 and o == 0:
                        pe.wait_ge(*at("f.dft", 32))
                    if j >= 3:
                        pe.wait_ge(*at("f.spec", 9 * o + j - 2))
                    b = 2 * (j % 3)
                    kt, f = j // 2, j % 2
                    for half in range(2):
                        if j == 8:
                            i = mm(ps[:, b + half, :], cdft[:, half, :], FS[:, 8, half, :], start=True, stop=True)
                            continue
                        for n in range(4):
                            i = mm(ps[:, b + half, :], (fwd_c, fwd_s)[f][:, 4 * half + n, kt * P:(kt + 1) * P],
                                   FS[:, 4 * half + n, f, :], start=n == 0, stop=n == 3)
                    i.then_inc(s("f.dftmm"), 1)
            mod_cols(len(mod_units) - 1)

            def norm(p, groups=by_three):
                for j, t in enumerate(sum(groups, ())):
                    pe.wait_ge(*at(p + "xn", j + 1))
                    if j >= 4:
                        pe.wait_ge(*at(p + "evA", j - 3))
                        pe.wait_ge(*at(p + "evD", j - 3))
                    for c in range(DK):
                        i = tr(ps[:, 2 * (j % 4) + c // 4, (c % 4) * P:(c % 4 + 1) * P],
                               XN[:, t, c * P:(c + 1) * P], ident[:, :])
                        if c % 4 == 3:
                            i.then_inc(s(p + ("tA", "tD")[c // 4]), 1)
                pe.wait_ge(*at(p + "evA", T))
                pe.wait_ge(*at(p + "evD", T))

            def project(p, jobs):
                for j, (n, kind, c) in enumerate(jobs):
                    landed(pe, n)
                    if j >= 2:
                        pe.wait_ge(*at(p + "ev", j - 1))
                    b = 3 * (j % 2)
                    w = slot(n).rearrange("p (k n) -> p k n", k=DK)
                    for k in range(DK):
                        if kind == "T":
                            for g in range(3):
                                i = mm(ps[:, b + g, 0:384], w[:, k, c * P:(c + 1) * P],
                                       hTv[:, k, g * 384:(g + 1) * 384], start=k == 0, stop=k == DK - 1)
                        else:
                            i = mm(ps[:, b, :], hTv[:, k, c * P:(c + 1) * P], w[:, k, :],
                                   start=k == 0, stop=k == DK - 1)
                    i.then_inc(s(p + "mm"), 1)
                pe.wait_ge(*at(p + "ev", len(jobs)))

            def retention():
                for t in range(T):
                    if t >= 2:
                        pe.wait_ge(*at("r.ktev", t - 1))
                    for h in range(RH):
                        i = tr(ps[:, 6 + t % 2, h * P:(h + 1) * P], kT[:, h, t * P:(t + 1) * P], ident[:, :])
                    i.then_inc(s("r.kt"), 1)
                pe.wait_ge(*at("r.ktev", T))

                def state(k, c):
                    pe.wait_ge(*at("r.vd", k + 1))
                    if k >= 2:
                        pe.wait_ge(*at("r.st", k - 1))
                    for h in range(RH):
                        i = mm(ps[:, k % 2, h * P:(h + 1) * P], ktok[:, c, h * P:(h + 1) * P],
                               vdec[:, k % 2, h * P:(h + 1) * P], start=True, stop=True)
                    i.then_inc(s("r.stmm"), 1)

                for k in range(7):
                    state(k, 7 - k)
                state(7, 8)
                state(8, 8)
                def scores(c):
                    if c >= 2:
                        pe.wait_ge(*at("r.sm", c - 1))
                    for h in range(RH):
                        i = mm(ps[:, 2 + c % 2, h * P:(h + 1) * P], kT[:, h, c * P:(c + 1) * P],
                               qT[:, h, c * P:(c + 1) * P], start=True, stop=True)
                    i.then_inc(s("r.sc"), 1)

                scores(0)
                for c in range(T):
                    if c + 1 < T:
                        scores(c + 1)
                    if c < 7:
                        state(9 + c, c)
                    pe.wait_ge(*at("r.sm", c + 1))
                    if c < 8:
                        pe.wait_ge(*at("r.qf", c + 1))
                        if c == 0:
                            pe.wait_ge(*at("r.s0", 32))
                            pe.wait_ge(*at("r.st", 9))
                        else:
                            pe.wait_ge(*at("r.st", 9 + c))
                    if c >= 2:
                        pe.wait_ge(*at("r.oev", c - 1))
                    for h in range(RH):
                        hs = slice(h * P, (h + 1) * P)
                        o = ps[:, 4 + c % 2, hs]
                        i = mm(o, sm[c % 2][:, hs], vtok[:, c, hs], start=True, stop=c == 8)
                        if c < 8:
                            mm(o, qfb[c % 2][:, 0, hs], sfwd[:, hs], start=False, stop=False)
                            i = mm(o, qfb[c % 2][:, 1, hs], sbwd[:, c, hs], start=False, stop=True)
                    i.then_inc(s("r.o"), 1)
                for t in range(T):
                    pe.wait_ge(*at("r.on", t + 1))
                    if t >= 2:
                        pe.wait_ge(*at("r.otev", t - 1))
                    for h in range(RH):
                        i = tr(ps[:, 6 + t % 2, h * P:(h + 1) * P], vtok[:, t, h * P:(h + 1) * P], ident[:, :])
                    i.then_inc(s("r.ot"), 1)
                pe.wait_ge(*at("r.otev", T))
                pe.wait_ge(*at("r.oev", T))

            def hyena():
                for o in range(2):
                    fwd0, fwd1, _, _, inv0, inv1 = hy_units[o]
                    if o == 0:
                        pe.wait_ge(*at("h.u0", 16))
                    else:
                        pe.wait_ge(*at("h.z", 4))
                    for m in range(T):
                        if m >= 2:
                            pe.wait_ge(*at("h.vtev", T * o + m - 1))
                        for c in range(4):
                            if m < 8:
                                t0 = 2 * (m % 4) * P + m // 4
                                src = zT[0][:, c, t0:t0 + 2 * P - 1:2]
                            else:
                                src = zT[0][:, c, LAT:NT]
                            i = tr(ps[:, 6 + m % 2, c * P:(c + 1) * P], src, ident[:, :])
                        i.then_inc(s("h.vt"), 1)
                    pe.wait_ge(*at("h.vtev", T * (o + 1)))
                    fwd = [slot(n).rearrange("p (f t k) -> p f t k", f=2, t=8) for n in (fwd0, fwd1)]
                    inv = [slot(n).rearrange("p (f k t) -> p f k t", f=2, k=2) for n in (inv0, inv1)]
                    for j, kt in enumerate((4, 0, 1, 2, 3)):
                        b = 4 * (j % 2)
                        if j >= 2:
                            pe.wait_ge(*at("h.xh", 5 * o + j - 1))
                        if kt == 4:
                            for f in range(2):
                                i = mm(ps[:, f, :], cdft[:, f, :], vt[:, 8, :], start=True, stop=True)
                        else:
                            if kt % 2 == 0:
                                landed(pe, (fwd0, fwd1)[kt // 2])
                            for f in range(4):
                                for n in range(4):
                                    tt_, ks = 4 * (f % 2) + n, slice((kt % 2) * P, (kt % 2 + 1) * P)
                                    i = mm(ps[:, b + f, :], fwd[kt // 2][:, f // 2, tt_, ks], vt[:, tt_, :],
                                           start=n == 0, stop=n == 3)
                        i.then_inc(s("h.x"), 1)
                        if kt == 1:
                            pe.wait_ge(*at("h.x", 5 * o + 3))
                            pe.sem_inc(s(f"slot{fwd0 % NS}_free"), 1)
                    pe.wait_ge(*at("h.x", 5 * (o + 1)))
                    pe.sem_inc(s(f"slot{fwd1 % NS}_free"), 1)

                    def back(c, kts):
                        b = 4 + 2 * (c % 2)
                        cs = slice(c * P, (c + 1) * P)
                        for par in range(2):
                            for kt in kts:
                                for f in range(2):
                                    mm(ps[:, b + par, :], spec[:, kt, 2 * par + f, cs],
                                       inv[kt // 2][:, f, kt % 2, par * 512:(par + 1) * 512],
                                       start=kt == 0 and f == 0, stop=kt == 3 and f == 1)

                    def back_context(c):
                        cs = slice(c * P, (c + 1) * P)
                        mm(ps[:, c % 2, 0:P], specc[:, 0, cs], cdft[:, 2, :], start=True, stop=False)
                        mm(ps[:, c % 2, 0:P], specc[:, 1, cs], cdft[:, 3, :], start=False, stop=True
                           ).then_inc(s("h.y"), 1)

                    pe.wait_ge(*at("h.xh", 5 * o + 4))
                    pe.wait_ge(*at("h.spec", 5 * o + 3))
                    landed(pe, inv0)
                    back(0, range(2))
                    back(1, range(2))
                    pe.wait_ge(*at("h.spec", 5 * o + 4))
                    landed(pe, inv1)
                    back(0, (2,))
                    back(1, (2,))
                    pe.wait_ge(*at("h.spec", 5 * (o + 1)))
                    for c in range(4):
                        if c >= 2:
                            pe.wait_ge(*at("h.z", 4 * o + c - 1))
                        back(c, range(4) if c >= 2 else (3,))
                        back_context(c)
                    pe.wait_ge(*at("h.y", 4 * (o + 1)))
                    pe.sem_inc(s(f"slot{inv0 % NS}_free"), 1)
                    pe.sem_inc(s(f"slot{inv1 % NS}_free"), 1)
                pe.wait_ge(*at("h.z", 8))

            def out_project(l, us):
                p = f"o{l}."
                for g in range(2):
                    for half in range(2):
                        for c in range(4):
                            i = mm(ps[:, 4 + 2 * g + half, c * P:(c + 1) * P],
                                   modc[:, l, 16 + 4 * half + c, g:g + 1].to_broadcast([P, P]), ident[:, :],
                                   start=True, stop=True)
                i.then_inc(s(p + "g"), 1)
                for t in range(T):
                    for half in range(2):
                        j = 2 * t + half
                        landed(pe, us[half])
                        if j >= 4:
                            pe.wait_ge(*at(p + "x", j - 3))
                        w = slot(us[half]).rearrange("p (k n) -> p k n", k=DK)
                        for k in range(DK):
                            i = mm(ps[:, j % 4, :], yTv[:, k, t * P:(t + 1) * P], w[:, k, :],
                                   start=k == 0, stop=k == DK - 1)
                        i.then_inc(s(p + "mm"), 1)
                pe.wait_ge(*at(p + "mm", 2 * T))
                for n in us:
                    pe.sem_inc(s(f"slot{n % NS}_free"), 1)
                pe.wait_ge(*at(p + "x", 2 * T))
                pe.wait_ge(*at(p + "gev", 4))

            def experts(l):
                m = f"e{l}."
                base = exp_units[l]
                pe.wait_ge(*at(m + "tab", 64))
                for j in range(3):
                    for k in range(DK):
                        g, wide = k % 4, 32 if k < 4 else NE
                        i = mm(ps[32 * g:32 * g + wide, j, 0:384], rw[:, NE * k:NE * k + wide],
                               hTv[:, k, 384 * j:384 * (j + 1)], start=k < 4, stop=k >= 4, tile_position=(0, 32 * g))
                    i.then_inc(s(m + "lg"), 1)
                pe.wait_ge(*at(m + "lpart", 3))
                for t in range(T):
                    i = mm(ps[:, 3 + t // 4, (t % 4) * P:(t % 4 + 1) * P], lpart[:, t * P:(t + 1) * P],
                           pick.rearrange("p (o e) -> p o e", o=1).to_broadcast([P, 8, NE]), start=True, stop=True)
                i.then_inc(s(m + "lg"), 1)
                pe.wait_ge(*at(m + "aff", 1))
                for t in range(T):
                    i = tr(ps[0:NE, 1 + t // 4, (t % 4) * P:(t % 4 + 1) * P], aff[:, t, :], ident[:, :])
                    if t in (3, 7, 8):
                        i.then_inc(s(m + "at"), 1)
                pe.wait_ge(*at(m + "affT", 3))

                def find(b):
                    wide = lambda t: tg[:, b, t:t + 1, :].to_broadcast([P, 48, 2])
                    for t in range(8):
                        mm(ps[:, 7, 0:96], onehot[:, t, :], wide(t), start=t == 0, stop=t == 7)
                    mm(ps[0:CAPC, 7, 96:192], onehot[:, 8, 0:CAPC], wide(8), start=True, stop=True
                       ).then_inc(s(m + "ix"), 1)

                def turn_in(b):
                    for c in range(DK):
                        o = (c % 3) * CAP
                        tr(ps[:, c // 3, o:o + CAPL], xs[b][:, c * P:(c + 1) * P], ident[:, :])
                        i = tr(ps[:, c // 3, o + CAPL:o + CAP], xsc[b][:, c * P:(c + 1) * P], ident[0:CAPC, 0:CAPC])
                        if c in (2, 5, 7):
                            i.then_inc(s(m + "ti"), 1)

                pe.wait_ge(*at(m + "oh", 1))
                find(0)
                pe.wait_ge(*at(m + "xs0", 32))
                turn_in(0)

                def pair(i, last):
                    for ee in range(2):
                        n0 = base + 6 * ee
                        w = [slot(n0 + j).rearrange("p (k n) -> p k n", k=DK) for j in range(6)]
                        more = not (last and ee)
                        for f in range(8):
                            ug, uu = n0 + 2 * (f // 4), n0 + 2 * (f // 4) + 1
                            if f % 4 == 0:
                                landed(pe, ug, 48 * i)
                                landed(pe, uu, 48 * i)
                            if f == 0:
                                pe.wait_ge(*at(m + "te", 6 * i + 3 * ee + 3))
                            if f < 2:
                                pe.wait_ge(*at(m + "dn", 16 * i + 8 * ee))
                            else:
                                pe.wait_ge(*at(m + "hid", 16 * i + 8 * ee + f - 1))
                            if f == 7 and more:
                                pe.wait_ge(*at(m + "oh", 2 * i + ee + 2))
                                find(1 - ee)
                            c = f % 4
                            for g, u in ((0, ug), (1, uu)):
                                for k in range(DK):
                                    last_mm = mm(ps[:, 3 + f % 2, g * CAP:(g + 1) * CAP],
                                                 w[u - n0][:, k, c * P:(c + 1) * P], xsT[ee][:, k, :],
                                                 start=k == 0, stop=k == DK - 1)
                            last_mm.then_inc(s(m + "gu"), 1)
                        for d in range(8):
                            ud_ = n0 + 4 + d // 4
                            if d % 4 == 0:
                                landed(pe, ud_, 48 * i)
                            if d == 0:
                                pe.wait_ge(*at(m + "hid", 16 * i + 8 * ee + 7))
                            if d == 6 and more:
                                pe.wait_ge(*at(m + f"xs{1 - ee}", 32 * i + 32 * (1 + ee)))
                                pe.wait_ge(*at(m + "rows", 4 * i + 2 * ee))
                                turn_in(1 - ee)
                            if d >= 2:
                                pe.wait_ge(*at(m + "dn", 16 * i + 8 * ee + d - 1))
                            for k in range(DK):
                                if d == 0 and k == DK - 1:
                                    pe.wait_ge(*at(m + "hid", 16 * i + 8 * ee + 8))
                                last_mm = mm(ps[:, 3 + d % 2, 0:CAP], w[4 + d // 4][:, k, (d % 4) * P:(d % 4 + 1) * P],
                                             hid[:, k, :], start=k == 0, stop=k == DK - 1)
                            last_mm.then_inc(s(m + "d"), 1)
                        def turn_out(c):
                            return tr(ps[:, 5 + c // 4, (c % 4) * P:(c % 4 + 1) * P], outT[:, c, 0:CAPL], ident[:, :])

                        def turn_out_context(c):
                            return tr(ps[0:CAPC, c // 4, (c % 4) * P:(c % 4 + 1) * P], outT[:, c, CAPL:CAP], ident[:, :])

                        pe.wait_ge(*at(m + "dn", 16 * i + 8 * ee + 7))
                        for c in range(7):
                            turn_out(c)
                        if more:
                            pe.wait_ge(*at(m + "te", 6 * i + 3 * ee + 6))
                        for c in range(7):
                            turn_out_context(c)
                        pe.wait_ge(*at(m + "dn", 16 * i + 8 * ee + 8))
                        turn_out(7).then_inc(s(m + "to"), 1)
                        turn_out_context(7).then_inc(s(m + "to"), 1)
                each_expert_pair(pe, [], [], pair)
                pe.wait_ge(*at(m + "rows", 2 * NE))

            def attention():
                for h in range(AH):
                    i = tr(ps[:, 6 + h // 4, (h % 4) * P:(h % 4 + 1) * P], kTa[:, h, LAT:NT], ident[:, :])
                i.then_inc(s("a.kt"), 1)
                pe.wait_ge(*at("a.ck", 16))
                for h in range(AH):
                    i = tr(ps[:, 4 + h // 4, (h % 4) * P:(h % 4 + 1) * P], ckrow[:, h * P:(h + 1) * P], ident[:, :])
                i.then_inc(s("a.kt"), 1)
                pe.wait_ge(*at("a.kctx", 2))
                pe.wait_ge(*at("a.ckT", 2))
                pe.wait_ge(*at("q.rope", 16))

                def scores(n, m):
                    h, q = steps[n]
                    pe.wait_ge(*at("a.qz", n + 1))
                    if n:
                        pe.wait_ge(*at("a.e", 2 * (n - 1) + m + 1))
                    lhs = qz[:, n % 2, m, :]
                    if q < 8:
                        mm(ps[:, 3 * m, :], lhs, kTa[:, h, 0:512], start=True, stop=True)
                        mm(ps[:, 3 * m + 1, :], lhs, kTa[:, h, 512:1024], start=True, stop=True)
                        i = mm(ps[:, 3 * m + 2, 0:P], lhs, ckT[:, h, :], start=True, stop=True)
                    else:
                        i = mm(ps[:, 3 * m, 0:P], lhs, kTa[:, h, LAT:NT], start=True, stop=True)
                    i.then_inc(s("a.s"), 1)

                def turn(src, before, nt, first=True, ninth=True, oev=None):
                    if first:
                        pe.wait_ge(*at("a.tev", before))
                        for t in range(min(nt, 8)):
                            if t == 4 and oev:
                                pe.wait_ge(*at("a.oev", oev))
                            i = tr(ps[:, 6 + t // 4, (t % 4) * P:(t % 4 + 1) * P], src(t), ident[:, :])
                            if t % 4 == 3 or t == nt - 1:
                                i.then_inc(s("a.t"), 1)
                    if ninth and nt == 9:
                        pe.wait_ge(*at("a.tev", before + 1))
                        tr(ps[:, 6, 0:P], src(8), ident[:, :]).then_inc(s("a.t"), 1)

                for n in range(2):
                    for m in range(2):
                        scores(n, m)
                done = 0
                for n, (h, q) in enumerate(steps):
                    nt = 9 if q < 8 else 1
                    if n + 2 < len(steps):
                        scores(n + 2, 0)
                    pe.wait_ge(*at("a.a", n + 1))
                    if n:
                        pe.wait_ge(*at("a.oev", n))
                    probs = lambda t: eb[:, n % 2, 0, t * P:(t + 1) * P]
                    turn(probs, done, nt, ninth=False)
                    if n + 2 < len(steps):
                        scores(n + 2, 1)
                    turn(probs, done, nt, first=False)
                    done = tev_of[n]
                    pe.wait_ge(*at("a.tev", done - (nt == 9)))
                    if n == 0:
                        pe.wait_ge(*at("a.cv", 16))
                    for t in range(nt):
                        if t == 8:
                            pe.wait_ge(*at("a.tev", done))
                        v = cv[:, h * P:(h + 1) * P] if t == 8 else va[:, t if q < 8 else 8, h * P:(h + 1) * P]
                        i = mm(ps[:, 7, 0:P], aT[:, t * P:(t + 1) * P], v, start=t == 0, stop=t == nt - 1)
                    i.then_inc(s("a.pv"), 1)
                    if q == head_step and h:
                        pe.wait_ge(*at("a.on", h))
                        turn(lambda t: ohs[(h - 1) % 2][:, t, :], done, 9, oev=n + 1)
                        done = head_tev[h - 1]
                pe.wait_ge(*at("a.on", AH))
                pe.wait_ge(*at("a.oev", len(steps)))
                turn(lambda t: ohs[(AH - 1) % 2][:, t, :], done, 9)
                pe.wait_ge(*at("a.tev", head_tev[-1]))

            pe.wait_ge(*at("f.spec", 18))
            pe.wait_ge(*at("mod.colev", len(mod_units)))
            norm("n10.", at_first)
            project("p.", even_jobs)
            retention()
            hyena()
            out_project(0, oute_units)
            norm("n20.")
            experts(0)
            norm("n11.")
            project("q.", odd_jobs)
            attention()
            out_project(1, outo_units)
            norm("n21.")
            experts(1)

        @block.scalar
        def _(act):
            act.sem_inc(s("e.dn"), ahead["e.dn"])
            A = nc.scalar.activation

            def give_back(n):
                act.sem_inc(s(f"slot{n % NS}_free"), 1)
            act.wait_ge(*at("c.cols", 2))
            A(scond[:, :, :].rearrange("p k g -> p g k"), colB[:, 57:73].rearrange("p (g k) -> p g k", g=2),
              ACT.Silu).then_inc(s("c.scond"), 1)
            for kind, o, j in start_plan:
                if kind == "sine":
                    act.wait_ge(*at("f.arg", o + 1))
                    A((harg, h2T)[o], harg, ACT.Sin).then_inc(s("f.sin"), 1)
                elif kind == "tap":
                    act.wait_ge(*at("f.taps", 18 * o + j + 1))
                    if j >= 2:
                        act.wait_ge(*at("f.acc", 18 * o + j - 1))
                    A(habs[j % 2], FH[:, j // 2, j % 2, :], ACT.Abs).then_inc(s("f.abs"), 1)
                elif kind == "mod":
                    act.wait_ge(*at("mod.rows", o + 1))
                    give_back(mod_units[o])
                    if o >= 2:
                        act.wait_ge(*at("mod.cols", o - 1))
                    A(mrow[o % 2], ps[:, 6, :], ACT.Copy).then_inc(s("mod.rowev"), 1)
            def norm(p, l, n, x_ready, groups=by_three):
                def columns(js):
                    for j in js:
                        t = groups[j // 3][j % 3]
                        act.wait_ge(*at(p + "tA", j + 1))
                        g = int(t == 8)
                        for c in range(4):
                            i = A(hTv[:, c, t * P:(t + 1) * P], ps[:, 2 * (j % 4), c * P:(c + 1) * P], ACT.Identity,
                                  scale=amul[:, l, n, c, g:g + 1], bias=modc[:, l, 24 * n + c, g:g + 1])
                        i.then_inc(s(p + "evA"), 1)

                for k, tiles in enumerate(groups):
                    for t in tiles:
                        act.wait_ge(*x_ready(t))
                        A(XN[:, t, :], X[:, t, :], ACT.Square, accum_out=stat[:, 0, t:t + 1]).then_inc(s(p + "ssq"), 1)
                    if k == 2 and l is not None:
                        columns(range(3))
                    act.wait_ge(*at(p + "var", k + 1))
                    A(stat[:, 2, tiles[0]:tiles[0] + 3], stat[:, 1, tiles[0]:tiles[0] + 3], ACT.Sqrt
                      ).then_inc(s(p + "std"), 1)
                if l is not None:
                    columns(range(3, T))

            def decays():
                act.wait_ge(*at("r.d", 1))
                A(dk[:, 2, :], dk[:, 1, :], ACT.Exp, scale=-1.0).then_inc(s("r.da"), 1)
                act.wait_ge(*at("r.d", 2))
                A(dk[:, 3, :], dk[:, 1, :], ACT.Ln).then_inc(s("r.da"), 1)
                act.wait_ge(*at("r.d", 3))
                A(cdec[:, :], dk[:, 0, :], ACT.Exp, scale=float(P)).then_inc(s("r.da"), 1)
                A(kdec[:, :, :], kdec[:, :, :], ACT.Exp).then_inc(s("r.da"), 1)
                A(misc[:, 0:1536], misc[:, 0:1536], ACT.Exp).then_inc(s("r.da"), 1)
                A(rarg, rarg, ACT.Exp).then_inc(s("r.da"), 1)
                A(lamc[:, 2:4], lamc[:, 0:2], ACT.Exp).then_inc(s("r.da"), 1)

            def project_even():
                for j in range(len(even_jobs)):
                    act.wait_ge(*at("p.mm", j + 1))
                    if j + 1 == len(even_jobs) or even_jobs[j + 1][0] != even_jobs[j][0]:
                        give_back(even_jobs[j][0])
                    b = 3 * (j % 2)
                    three = ps[:, b:b + 3, 0:384]
                    if j < 8:
                        dst = (qT if j < 4 else kT)[:, j % 4, :].rearrange("p (g t) -> p g t", g=3)
                        i = A(dst, three, ACT.Copy, scale=1.0 if j < 4 else float(P) ** -0.5)
                    elif j < 17:
                        i = A(vtok[:, j - 8, :], ps[:, b, :], ACT.Copy)
                    elif j < 26:
                        i = A(gtok[:, j - 17, :], ps[:, b, :], ACT.Silu)
                    else:
                        c = j - 26
                        if c >= 2:
                            act.wait_ge(*at("p.u", c - 1))
                        i = A(raw[c % 2].rearrange("p (g t) -> p g t", g=3), three, ACT.Copy)
                    i.then_inc(s("p.ev"), 1)

            def retention():
                for t in range(T):
                    act.wait_ge(*at("r.kt", t + 1))
                    A(ktok[:, t, :], ps[:, 6 + t % 2, :], ACT.Copy).then_inc(s("r.ktev"), 1)
                for c in range(T):
                    act.wait_ge(*at("r.o", c + 1))
                    act.wait_ge(*at("r.vd", min(9 + c + 1, 16)))
                    A(vtok[:, c, :], ps[:, 4 + c % 2, :], ACT.Copy).then_inc(s("r.oev"), 1)
                act.wait_ge(*at("r.var", 1))
                A(gstf[:, 108:144], gstf[:, 108:144], ACT.Sqrt).then_inc(s("r.std"), 1)
                for t in range(T):
                    act.wait_ge(*at("r.ot", t + 1))
                    A(yTv[:, 4:8, t * P:(t + 1) * P], ps[:, 6 + t % 2, :].rearrange("p (h n) -> p h n", h=RH),
                      ACT.Copy).then_inc(s("r.otev"), 1)

            def hyena():
                for o in range(2):
                    for m in range(T):
                        act.wait_ge(*at("h.vt", T * o + m + 1))
                        A(vt[:, m, :], ps[:, 6 + m % 2, :], ACT.Copy).then_inc(s("h.vtev"), 1)
                    for j in range(5):
                        act.wait_ge(*at("h.x", 5 * o + j + 1))
                        if 5 * o + j:
                            act.wait_ge(*at("h.spec", 5 * o + j))
                        b = 4 * (j % 2)
                        nf = 4 if j else 2
                        A(xh[:, 0:nf, :], ps[:, b:b + nf, :], ACT.Copy).then_inc(s("h.xh"), 1)

            def gate_rows(l):
                act.wait_ge(*at(f"o{l}.g", 1))
                for g in range(2):
                    for half in range(2):
                        A(grow[:, g, half * 512:(half + 1) * 512], ps[:, 4 + 2 * g + half, :], ACT.Copy
                          ).then_inc(s(f"o{l}.gev"), 1)

            def experts(l):
                m = f"e{l}."
                base = exp_units[l]
                for j in range(3):
                    act.wait_ge(*at(m + "lg", j + 1))
                    A(lpart[:, 384 * j:384 * (j + 1)], ps[:, j, 0:384], ACT.Copy).then_inc(s(m + "lpart"), 1)
                act.wait_ge(*at(m + "sub", 1))
                A(affm, affm, ACT.Exp).then_inc(s(m + "exp"), 1)
                for g in range(3):
                    act.wait_ge(*at(m + "at", g + 1))
                    w = 512 if g < 2 else P
                    A(affT[:, 512 * g:512 * g + w], ps[0:NE, 1 + g, 0:w], ACT.Copy).then_inc(s(m + "affT"), 1)

                def pair(i, last):
                    for ee in range(2):
                        for f in range(8):
                            act.wait_ge(*at(m + "gu", 16 * i + 8 * ee + f + 1))
                            if f % 4 == 3:
                                give_back(base + 6 * ee + f // 4 * 2)
                                give_back(base + 6 * ee + f // 4 * 2 + 1)
                            if f < 2:
                                act.wait_ge(*at(m + "hid", 16 * i + 8 * ee))
                            else:
                                act.wait_ge(*at(m + "hid", 16 * i + 8 * ee + f - 1))
                            A(sg[f % 2], ps[:, 3 + f % 2, 0:CAP], ACT.Silu).then_inc(s(m + "sg"), 1)
                        act.wait_ge(*at(m + "to", 4 * i + 2 * ee))
                        for d in range(8):
                            act.wait_ge(*at(m + "d", 16 * i + 8 * ee + d + 1))
                            if d % 4 == 3:
                                give_back(base + 6 * ee + 4 + d // 4)
                            A(outT[:, d, 0:CAPL], ps[:, 3 + d % 2, 0:CAPL], ACT.Copy,
                              scale=modc[:, l, 40 + d, 0:1])
                            A(outT[:, d, CAPL:CAP], ps[:, 3 + d % 2, CAPL:CAP], ACT.Copy,
                              scale=modc[:, l, 40 + d, 1:2]).then_inc(s(m + "dn"), 1)
                each_expert_pair(act, [], [], pair)

            def project_odd():
                for j in range(len(odd_jobs)):
                    act.wait_ge(*at("q.mm", j + 1))
                    if j + 1 == len(odd_jobs) or odd_jobs[j + 1][0] != odd_jobs[j][0]:
                        give_back(odd_jobs[j][0])
                    b = 3 * (j % 2)
                    if j < 16:
                        dst = (qTa if j < 8 else kTa)[:, j % 8, :].rearrange("p (g t) -> p g t", g=3)
                        i = A(dst, ps[:, b:b + 3, 0:384], ACT.Copy)
                    else:
                        if j == 16:
                            act.wait_ge(*at("q.rope", 16))
                        u, t = (j - 16) // T, (j - 16) % T
                        i = A(va[:, t, u * 512:(u + 1) * 512], ps[:, b, :], ACT.Copy)
                    i.then_inc(s("q.ev"), 1)

            def attention():
                act.wait_ge(*at("a.kt", 1))
                for g in range(2):
                    A(eb[:, 1, 0, g * 512:(g + 1) * 512], ps[:, 6 + g, :], ACT.Copy).then_inc(s("a.kctx"), 1)
                act.wait_ge(*at("a.kt", 2))
                for g in range(2):
                    A(ckT[:, 4 * g:4 * g + 4, :], ps[:, 4 + g, :].rearrange("p (h n) -> p h n", h=4), ACT.Copy
                      ).then_inc(s("a.ckT"), 1)
                act.wait_ge(*at("a.ckT", 2))

                def exps(n):
                    h, q = steps[n]
                    w = NT if q < 8 else P
                    if n >= 2:
                        act.wait_ge(*at("a.tev", tev_of[n - 2]))
                    for m in range(2):
                        act.wait_ge(*at("a.nm", 2 * n + m + 1))
                        c = (n % 4) * 8
                        A(eb[:, n % 2, m, 0:w], bank(3 * m, 3)[:, 0:w], ACT.Exp, scale=0.125,
                          bias=gstf[:, c + 2 + m:c + 3 + m], accum_out=gstf[:, c + 4 + m:c + 5 + m]
                          ).then_inc(s("a.e"), 1)

                def evacuate(dst, before, nt, **kw):
                    for g in range((nt + 3) // 4):
                        w = min(512, nt * P - 512 * g)
                        act.wait_ge(*at("a.t", before + g + 1))
                        A(dst(512 * g, w), ps[:, 6 + g % 2, 0:w], ACT.Copy, **kw).then_inc(s("a.tev"), 1)

                def deviations(h):
                    act.wait_ge(*at("a.var", h + 1))
                    A(gstf[:, 48:57], gstf[:, 48:57], ACT.Sqrt).then_inc(s("a.std"), 1)

                exps(0)
                act.wait_ge(*at("a.kctx_out", 16))
                exps(1)
                done = 0
                for n, (h, q) in enumerate(steps):
                    if n:
                        act.wait_ge(*at("a.pv", n))
                    evacuate(lambda o, w: aT[:, o:o + w], done, 9 if q < 8 else 1)
                    done = tev_of[n]
                    if q == head_step - 1 and h:
                        deviations(h - 1)
                    if n + 2 < len(steps):
                        exps(n + 2)
                    if q == head_step and h:
                        evacuate(lambda o, w: yTv[:, h - 1, o:o + w], done, 9, scale=lamc[:, 6:7])
                        done = head_tev[h - 1]
                deviations(AH - 1)
                evacuate(lambda o, w: yTv[:, AH - 1, o:o + w], done, 9, scale=lamc[:, 6:7])

            norm("n10.", 0, 0, lambda t: at(f"x{t}.landed", 16), at_first)
            decays()
            project_even()
            retention()
            hyena()
            gate_rows(0)
            norm("n20.", 0, 1, lambda t: at("o0.x", 2 * t + 2))
            experts(0)
            norm("n11.", 1, 0, lambda t: at(f"x{t}.landed", 48))
            project_odd()
            attention()
            gate_rows(1)
            norm("n21.", 1, 1, lambda t: at("o1.x", 2 * t + 2))
            experts(1)
            norm("z.", None, 0, lambda t: at(f"x{t}.landed", 80))

        @block.vector
        def _(dve):
            ts, tt, stt = nc.vector.tensor_scalar, nc.vector.tensor_tensor, nc.vector.scalar_tensor_tensor
            cp, rec, ms = nc.vector.tensor_copy, nc.vector.reciprocal, nc.vector.memset
            ch = Chain(dve, "dve.chain")
            dve.sem_inc(s("e.rows"), ahead["e.rows"])
            dve.sem_inc(s("e.hid"), ahead["e.hid"])

            ms(ones, 1.0).then_inc(s("f.ones"), 1)
            ms(ps[:, 6, :], 0.0).then_inc(s("mod.zero"), 1)
            dve.wait_ge(*at("c.colT", 2))
            cp(colA[:, :], ps[:, 0, 0:P]).then_inc(s("c.cols"), 1)
            cp(colB[:, 0:73], ps[:, 1, 0:73]).then_inc(s("c.cols"), 1)

            dve.wait_ge(*at("f.in", 16 * 8))
            def sine_layer(i):
                dve.wait_ge(*at("f.h12", i + 1))
                src = ps[0:64, 3 * i:3 * i + 3, 0:384]
                v3 = harg.rearrange("p (g t) -> p g t", g=3)
                ch(ts(v3, src, fcol[:, 2 * i:2 * i + 1], fcol[:, 2 * i + 1:2 * i + 2], ALU.add, ALU.mult))
                ch(ts(hrnd, harg, 1.0 / (2 * math.pi), MAGIC, ALU.mult, ALU.add))
                ch(ts(hrnd, hrnd, -MAGIC, None, ALU.add))
                ch(stt(harg, hrnd, -6.28125, harg, ALU.mult, ALU.add))
                ch(stt(harg, hrnd, -(2 * math.pi - 6.28125), harg, ALU.mult, ALU.add))
                ts(harg, harg, 3.1415925, -3.1415925, ALU.min, ALU.max).then_inc(s("f.arg"), 1)

            def add_taps(o, j):
                dve.wait_ge(*at("f.abs", 18 * o + j + 1))
                g = int(j >= 16)
                tt(facc[:, g, :], habs[j % 2], facc[:, g, :], ALU.add).then_inc(s("f.acc"), 1)
                dve.wait_ge(*at("f.acc", 18 * o + j + 1))

            def sum_taps(t):
                tt(FS[:, t, 0, :], FH[:, t, 0, :], FH[:, t, 1, :], ALU.add)
                tt(FS[:, t, 1, :], FH[:, t, 0, :], FH[:, t, 1, :], ALU.subtract)

            def mod_columns(n):
                l, u = n // 12, n % 12
                dve.wait_ge(*at("mod.cols", n + 1))
                bm = colA[:, 48 * l + 4 * u:48 * l + 4 * u + 4].rearrange("p (j o) -> p j o", o=1)
                tt(modc[:, l, 4 * u:4 * u + 4, :], ps[:, 7, 0:384].rearrange("p (j c) -> p j c", j=4)[:, :, 0:2],
                   bm.to_broadcast([P, 4, 2]), ALU.add).then_inc(s("mod.colev"), 1)

            for kind, o, j in start_plan:
                if kind == "sine":
                    sine_layer(o)
                elif kind == "mod":
                    if o:
                        mod_columns(o - 1)
                elif kind == "tap":
                    if j == 0:
                        dve.wait_ge(*at("f.win", 16))
                        ch(ms(facc, 0.0))
                        if o:
                            dve.wait_ge(*at("f.spec_out", 64))
                            dve.wait_ge(*at("f.specc_out", 16))
                    dve.wait_ge(*at("f.h3", 18 * o + j + 1))
                    tt(FH[:, j // 2, j % 2, :], ps[:, j % 4, :], win[:, j // 2, :], ALU.mult).then_inc(s("f.taps"), 1)
                    if j:
                        add_taps(o, j - 1)
                    if j > 3 and j % 2 == 0:
                        sum_taps(j // 2 - 1)
                elif kind == "sum":
                    add_taps(o, 17)
                    for t in (0, 8):
                        ch(ms(FH[0:1, t, 1, :], 0.0))
                        sum_taps(t)
                    dve.wait_ge(*at("f.sum", o + 1))
                    ch(ts(facc, ps[:, 4:6, :], EPS, None, ALU.add))
                    rec(facc, facc).then_inc(s("f.fold"), 1)
                    dve.wait_ge(*at("f.fold", o + 1))
                else:
                    dve.wait_ge(*at("f.dftmm", 9 * o + j + 1))
                    kt, f = j // 2, j % 2
                    b = 2 * (j % 3)
                    if j == 8:
                        for h in range(2):
                            i = tt(fstagec[:, h, :], ps[:, b + h, :], facc[:, 1, :], ALU.mult)
                        i.then_inc(s("f.spec"), 1)
                        dve.wait_ge(*at("f.spec", 9 * o + 9))
                        continue
                    for h in range(2):
                        i = tt(ftmp[:, h, :], ps[:, b + h, :], facc[:, 0, :], ALU.mult)
                    ch(i)
                    if kt >= 2 and f == 0:
                        dve.wait_ge(*at("f.spec_out", 16 * (4 * o + kt - 1)))
                    st = fstage[:, kt % 2]
                    tt(st[:, f, :], ftmp[:, 0, :], ftmp[:, 1, :], ALU.add)
                    tt(st[:, 2 + f, :], ftmp[:, 0, :], ftmp[:, 1, :], ALU.subtract).then_inc(s("f.spec"), 1)
                    dve.wait_ge(*at("f.spec", 9 * o + j + 1))
            mod_columns(len(mod_units) - 1)
            dve.wait_ge(*at("mod.colev", len(mod_units)))
            for l in range(2):
                for i in range(2):
                    g = colA[:, 96 + 16 * i + 8 * l:104 + 16 * i + 8 * l].rearrange("p (j o) -> p j o", o=1)
                    ch(stt(amul[:, l, i, :, :], modc[:, l, 8 + 24 * i:16 + 24 * i, :], 1.0,
                           g.to_broadcast([P, 8, 2]), ALU.add, ALU.mult))

            def rstd(p, k, tiles):
                sl = slice(tiles[0], tiles[0] + 3)
                dve.wait_ge(*at(p + "ssq", 3 * (k + 1)))
                ts(stat[:, 1, sl], stat[:, 0, sl], 1.0 / D, EPS, ALU.mult, ALU.add).then_inc(s(p + "var"), 1)
                dve.wait_ge(*at(p + "std", k + 1))
                ch(rec(stat[:, 1, sl], stat[:, 2, sl]))

            def normed(p, k, tiles):
                rstd(p, k, tiles)
                for t in tiles:
                    ts(XN[:, t, :], X[:, t, :], stat[:, 1, t:t + 1], None, ALU.mult).then_inc(s(p + "xn"), 1)

            def norm(p, l, n, groups=by_three, begin=0):
                def columns(js):
                    for j in js:
                        t = groups[j // 3][j % 3]
                        dve.wait_ge(*at(p + "tD", j + 1))
                        g = int(t == 8)
                        for c in range(4, 8):
                            i = ts(hTv[:, c, t * P:(t + 1) * P], ps[:, 2 * (j % 4) + 1, (c - 4) * P:(c - 3) * P],
                                   amul[:, l, n, c, g:g + 1], modc[:, l, 24 * n + c, g:g + 1], ALU.mult, ALU.add)
                        i.then_inc(s(p + "evD"), 1)

                for k in range(begin, 2):
                    normed(p, k, groups[k])
                columns(range(3))
                normed(p, 2, groups[2])
                columns(range(3, T))

            heads = lambda x: x.rearrange("p (h n) -> p h n", h=RH)

            def decays():
                dve.wait_ge(*at("r.tab", 16 * 6))
                dve.wait_ge(*at("c.small", 32))
                for i in range(2):
                    ch(nc.vector.tensor_tensor_reduce(rarg[:, 0:64], lamv[:, 2 * i, :], lamv[:, 2 * i + 1, :], 1.0, 0.0,
                                                      ALU.mult, ALU.add, lamc[:, i:i + 1]))
                stt(dk[:, 1, :], dk[:, 0, :], -1.0, dk[:, 0, :], ALU.mult, ALU.max).then_inc(s("r.d"), 1)
                dve.wait_ge(*at("r.da", 1))
                ch(ts(dk[:, 1, :], dk[:, 2, :], 1.0, None, ALU.add))
                ts(dk[:, 4, :], dk[:, 1, :], -1.0, None, ALU.add).then_inc(s("r.d"), 1)
                dve.wait_ge(*at("r.d", 2))
                dve.wait_ge(*at("r.da", 2))
                ch(ts(dk[:, 1, :], dk[:, 4, :], 1e-30, None, ALU.max))
                ch(rec(dk[:, 1, :], dk[:, 1, :]))
                ch(tt(dk[:, 3, :], dk[:, 3, :], dk[:, 1, :], ALU.mult))
                ch(stt(dk[:, 1, :], dk[:, 4, :], 0.0, dk[:, 3, :], ALU.is_equal, ALU.add))
                ch(tt(dk[:, 1, :], dk[:, 1, :], dk[:, 2, :], ALU.mult))
                ch(stt(dk[:, 0, :], dk[:, 0, :], 0.0, dk[:, 1, :], ALU.min, ALU.subtract))
                for d in range(2):
                    ts(kdec[:, d, :], dk[:, 0, 4 * d:4 * d + 4], small[:, d:d + 1], None, ALU.mult)
                    for h in range(RH):
                        lg = dk[:, 0, 4 * d + h:4 * d + h + 1]
                        dst = (rmask if d == 0 else rarg)[:, h * P:(h + 1) * P]
                        ts(dst, rtab[:, d, :], lg, None, ALU.mult)
                        i = ts(qdec[:, d, h * P:(h + 1) * P], rtab[:, 4 + d, :], lg, None, ALU.mult)
                i.then_inc(s("r.d"), 1)
                dve.wait_ge(*at("r.da", 7))
                over = lambda x: x.rearrange("p (o n) -> p o n", o=1).to_broadcast([P, RH, P])
                tt(heads(rmask), heads(rmask), over(rtab[:, 2, :]), ALU.mult)
                ch(tt(heads(rarg), heads(rarg), over(rtab[:, 3, :]), ALU.mult))
                ch(tt(rmask, rmask, rarg, ALU.add))
                ch(tt(lamc[:, 4:5], lamc[:, 3:4], lamc[:, 2:3], ALU.subtract))
                ch(ts(lamc[:, 4:5], lamc[:, 4:5], -LAM_INIT, None, ALU.add))
                ch(ts(lamc[:, 6:7], colB[:, 56:57], 1.0 - LAM_INIT, None, ALU.mult))

            def short_conv():
                for c in range(12):
                    dve.wait_ge(*at("p.ev", 26 + c + 1))
                    if c >= 2:
                        dve.wait_ge(*at(f"p.u_out{c % 2}", 16 * (c // 2)))
                    r, u = raw[c % 2], ubuf[c % 2]
                    w = [colB[:, 12 * i + c:12 * i + c + 1] for i in range(3)]
                    ch(ts(u, r, w[1], colB[:, 36 + c:37 + c], ALU.mult, ALU.add))
                    for lo, hi in ((0, LAT), (LAT, NT)):
                        i = stt(u[:, lo + 1:hi], r[:, lo:hi - 1], w[0], u[:, lo + 1:hi], ALU.mult, ALU.add)
                    ch(i)
                    for lo, hi in ((0, LAT), (LAT, NT)):
                        i = stt(u[:, lo:hi - 1], r[:, lo + 1:hi], w[2], u[:, lo:hi - 1], ALU.mult, ALU.add)
                    i.then_inc(s("p.u"), 1)

            def retention():
                for b in range(2):
                    dve.wait_ge(*at(f"p.u_out{b}", 16 * 6))
                dve.wait_ge(*at("r.s0", 32))
                tile_of = [7, 6, 5, 4, 3, 2, 1, 8, 8, 0, 1, 2, 3, 4, 5, 6]
                dir_of = [1] * 7 + [1, 0] + [0] * 7

                def decay_values(k):
                    kd_ = kdec[:, dir_of[k], :].rearrange("p (h o) -> p h o", o=1).to_broadcast([P, RH, P])
                    tt(heads(vdec[:, k % 2, :]), heads(vtok[:, tile_of[k], :]), kd_, ALU.mult).then_inc(s("r.vd"), 1)

                decay_values(0)
                decay_values(1)
                for k in range(7):
                    dve.wait_ge(*at("r.stmm", k + 1))
                    c = 7 - k
                    for h in range(RH):
                        hs = slice(h * P, (h + 1) * P)
                        i = stt(sbwd[:, c - 1, hs], sbwd[:, c, hs], cdec[:, 4 + h:5 + h], ps[:, k % 2, hs],
                                ALU.mult, ALU.add)
                    i.then_inc(s("r.st"), 1)
                    dve.wait_ge(*at("r.st", k + 1))
                    decay_values(k + 2)
                for k in (7, 8):
                    dve.wait_ge(*at("r.stmm", k + 1))
                    d = dir_of[k]
                    cp(sctx[:, d, :], ps[:, k % 2, :]).then_inc(s("r.st"), 1)
                    decay_values(k + 2)
                def weigh(c):
                    dve.wait_ge(*at("r.sc", c + 1))
                    if c >= 2:
                        dve.wait_ge(*at("r.o", c - 1))
                    tt(sm[c % 2], ps[:, 2 + c % 2, :], rmask, ALU.mult).then_inc(s("r.sm"), 1)
                    if c == 1:
                        dve.wait_ge(*at("r.sctx_out", 32))
                    if c < 8:
                        for d in range(2):
                            i = tt(heads(qfb[c % 2][:, d, :]), qT[:, :, c * P:(c + 1) * P], heads(qdec[:, d, :]),
                                   ALU.mult)
                        i.then_inc(s("r.qf"), 1)

                def moments(t):
                    dve.wait_ge(*at("r.oev", t + 1))
                    for h in range(RH):
                        i = nc.vector.bn_stats(bnb[:, 4 * t + h, :], vtok[:, t, h * P:(h + 1) * P])
                    ch(i)
                    for h in range(RH):
                        i = nc.vector.bn_aggr(gmv[:, 4 * t + h, :], bnb[:, 4 * t + h:4 * t + h + 1, :])
                    return i

                weigh(0)
                for c in range(T):
                    if c + 1 < T:
                        weigh(c + 1)
                    if c < 7:
                        k = 9 + c
                        dve.wait_ge(*at("r.stmm", k + 1))
                        dve.wait_ge(*at("r.o", c + 1))
                        for h in range(RH):
                            hs = slice(h * P, (h + 1) * P)
                            i = stt(sfwd[:, hs], sfwd[:, hs], cdec[:, h:h + 1], ps[:, k % 2, hs], ALU.mult, ALU.add)
                        i.then_inc(s("r.st"), 1)
                        dve.wait_ge(*at("r.st", k + 1))
                        if k + 2 < 16:
                            decay_values(k + 2)
                    if c:
                        moments(c - 1)
                ch(moments(T - 1))
                ts(gstf[:, 108:144], gmv[:, :, 1], EPS, None, ALU.add).then_inc(s("r.var"), 1)
                dve.wait_ge(*at("r.std", 1))
                ch(rec(gstf[:, 72:108], gstf[:, 108:144]))
                for t in range(T):
                    for h in range(RH):
                        j = 4 * t + h
                        v = vtok[:, t, h * P:(h + 1) * P]
                        i = ts(v, v, gmv[:, j, 0:1], gstf[:, 72 + j:73 + j], ALU.subtract, ALU.mult)
                    ch(i)
                    tt(vtok[:, t, :], vtok[:, t, :], gtok[:, t, :], ALU.mult).then_inc(s("r.on"), 1)

            def hyena():
                dve.wait_ge(*at("h.kctx", 16))
                dve.wait_ge(*at("r.sctx_out", 32))
                for o in range(2):
                    xq3 = xq.rearrange("p (q f) c -> p q f c", q=2)
                    A2 = xh[:, 0:2, :]
                    B2 = xh[:, 2:4, :]
                    dve.wait_ge(*at("h.xh", 5 * o + 1))
                    kr, ks = kctx[:, o, 0, :], kctx[:, o, 1, :]
                    tt(xq[:, 0, :], xh[:, 0, :], kr, ALU.mult)
                    tt(xq[:, 1, :], xh[:, 1, :], ks, ALU.mult)
                    tt(xq[:, 2, :], xh[:, 0, :], ks, ALU.mult)
                    ch(tt(xq[:, 3, :], xh[:, 1, :], kr, ALU.mult))
                    if o:
                        dve.wait_ge(*at("h.y", 4))
                    tt(specc[:, 0, :], xq[:, 0, :], xq[:, 1, :], ALU.subtract)
                    tt(specc[:, 1, :], xq[:, 2, :], xq[:, 3, :], ALU.add).then_inc(s("h.spec"), 1)
                    dve.wait_ge(*at("h.spec", 5 * o + 1))
                    for kt in range(4):
                        n = hy_units[o][2 + kt // 2]
                        dve.wait_ge(*at("h.xh", 5 * o + kt + 2))
                        xf = xh.rearrange("p (f e) c -> p f e c", f=2)
                        tt(xq3[:, 0, :, :], xf[:, :, 0, :], xf[:, :, 1, :], ALU.add)
                        ch(tt(xq3[:, 1, :, :], xf[:, :, 0, :], xf[:, :, 1, :], ALU.subtract))
                        if kt % 2 == 0:
                            landed(dve, n)
                        K = slot(n).rearrange("p (b q f c) -> p b q f c", b=2, q=2, f=2)[:, kt % 2]
                        xr, xs_, kr, ks = xq3[:, :, 0, :], xq3[:, :, 1, :], K[:, :, 0, :], K[:, :, 1, :]
                        tt(A2, xr, kr, ALU.mult)
                        ch(tt(B2, xs_, ks, ALU.mult))
                        ch(tt(A2, A2, B2, ALU.subtract))
                        tt(B2, xr, ks, ALU.mult)
                        ch(tt(xs_, xs_, kr, ALU.mult))
                        if kt % 2 == 1:
                            dve.sem_inc(s(f"slot{n % NS}_free"), 1)
                        ch(tt(B2, B2, xs_, ALU.add))
                        tt(spec[:, kt, 0, :], xh[:, 0, :], xh[:, 1, :], ALU.add)
                        tt(spec[:, kt, 1, :], xh[:, 2, :], xh[:, 3, :], ALU.add)
                        tt(spec[:, kt, 2, :], xh[:, 0, :], xh[:, 1, :], ALU.subtract)
                        tt(spec[:, kt, 3, :], xh[:, 2, :], xh[:, 3, :], ALU.subtract).then_inc(s("h.spec"), 1)
                    dve.wait_ge(*at(f"h.u{o + 1}", 16))
                    for c in range(4):
                        dve.wait_ge(*at("h.y", 4 * o + c + 1))
                        z = zT[0][:, c, :]
                        hb = colB[:, 48 + 4 * o + c:49 + 4 * o + c]
                        b = 4 + 2 * (c % 2)
                        stt(z[:, 0:LAT:2], z[:, 0:LAT:2], hb, ps[:, b, :], ALU.mult, ALU.add)
                        stt(z[:, 1:LAT:2], z[:, 1:LAT:2], hb, ps[:, b + 1, :], ALU.mult, ALU.add)
                        ch(stt(z[:, LAT:NT], z[:, LAT:NT], hb, ps[:, c % 2, 0:P], ALU.mult, ALU.add))
                        dst = z if o == 0 else yTv[:, c, :]
                        tt(dst, z, zT[1 + o][:, c, :], ALU.mult).then_inc(s("h.z"), 1)

            def out_project(l):
                p = f"o{l}."
                dve.wait_ge(*at(p + "gev", 4))
                for t in range(T):
                    g = int(t == 8)
                    dve.wait_ge(*at(f"x{t}.landed", 16 * (2 + 2 * l)))
                    for half in range(2):
                        hs = slice(512 * half, 512 * half + 512)
                        dve.wait_ge(*at(p + "mm", 2 * t + half + 1))
                        ch(tt(XN[:, t, hs], ps[:, (2 * t + half) % 4, :], grow[:, g, hs], ALU.mult))
                        tt(X[:, t, hs], X[:, t, hs], XN[:, t, hs], ALU.add).then_inc(s(p + "x"), 1)
                    if t in (3, 6):
                        normed(f"n2{l}.", t // 3 - 1, by_three[t // 3 - 1])

            def experts(l, per):
                m = f"e{l}."
                dve.wait_ge(*at(m + "tab", 64))
                dve.wait_ge(*at(m + "lg", 4))
                lg = bank(3, 3).rearrange("p (t e) -> p t e", e=P)[:, 0:T, 0:NE]
                wide = lambda x: x.rearrange("p (t o) -> p t o", o=1).to_broadcast([P, T, NE])
                ch(nc.vector.tensor_reduce(rowmax[:, 0, :], lg, AX.X, ALU.max))
                tt(affm, lg, wide(rowmax[:, 0, :]), ALU.subtract).then_inc(s(m + "sub"), 1)
                dve.wait_ge(*at(m + "exp", 1))
                ch(nc.vector.tensor_reduce(rowmax[:, 1, :], affm, AX.X, ALU.add))
                ch(rec(rowmax[:, 1, :], rowmax[:, 1, :]))
                tt(aff, affm, wide(rowmax[:, 1, :]), ALU.mult).then_inc(s(m + "aff"), 1)
                dve.wait_ge(*at(m + "aff", 1))
                for b in range(2):
                    cp(tg[:, b, :, 0], small[:, 2:11])
                dve.wait_ge(*at(f"o{l}.xn_out", 16 * T))
                dve.wait_ge(*at(f"o{l}.x_out", 16 * T))
                ch(ms(cnt, 0.0))

                def column(b, e):
                    src = aff[:, :, e:e + 1] if isinstance(e, int) else aff[:, :, bass.ds(e, 1)]
                    ch(cp(tg[:, b, :, 1:2], src))

                def rank_tile(b, t):
                    mine = tg[:, b, t, 1:2]
                    lo, hi = (0, LAT) if t < 8 else (LAT, NT)
                    t0 = P * t
                    if t0 > lo:
                        ch.raised(ts(junk[:, 0:t0 - lo], bc[b][:, lo:t0], mine, 0.0, ALU.is_ge, ALU.add,
                                     accum_out=cnt[:, t, 0:1]))
                    ch.raised(ts(junk[:, t0 - lo:hi - lo], bc[b][:, t0:hi], mine, 0.0, ALU.is_gt, ALU.add,
                                 accum_out=cnt[:, t, 1:2]))
                    ch(stt(junk[:, LAT:LAT + P], bc[b][:, t0:t0 + P], mine, lower, ALU.is_equal, ALU.mult,
                           accum_out=cnt[:, t, 2:3]))

                def finish_rank(n):
                    nc.vector.tensor_reduce(rank, cnt, AX.X, ALU.add).then_inc(s(m + "ranked"), 1)
                    dve.wait_ge(*at(m + "ranked", n + 1))
                    for t in range(T):
                        i = ts(onehot[:, t, :], iota, rank[:, t:t + 1], None, ALU.is_equal)
                    i.then_inc(s(m + "oh"), 1)

                def found(b, n):
                    cp(gate[:, b, 0:1], ps[:, 7, 1:2])
                    cp(gate[0:CAPC, b, 1:2], ps[0:CAPC, 7, 97:98])
                    cp(idx[:, b, 0:1], ps[:, 7, 0:1]).then_inc(s(m + "idx"), 1)
                    cp(idx[0:CAPC, b, 1:2], ps[0:CAPC, 7, 96:97]).then_inc(s(m + "idx"), 1)

                def columns_in(b, n):
                    for bk, cs in enumerate(((0, 1, 2), (3, 4, 5), (6, 7))):
                        dve.wait_ge(*at(m + "ti", n + bk + 1))
                        for c in cs:
                            o = (c % 3) * CAP
                            for g, (lo, hi) in enumerate(((0, CAPL), (CAPL, CAP))):
                                i = ts(xsT[b][:, c, lo:hi], ps[:, bk, o + lo:o + hi], amul[:, l, 1, c, g:g + 1],
                                       modc[:, l, 24 + c, g:g + 1], ALU.mult, ALU.add)
                        i.then_inc(s(m + "te"), 1)

                dve.wait_ge(*at(m + "bc0", 16))
                column(0, 0)
                for t in range(T):
                    rank_tile(0, t)
                finish_rank(0)
                dve.wait_ge(*at(m + "ix", 1))
                found(0, 0)
                columns_in(0, 0)

                def pair(i, last):
                    for ee in range(2):
                        more = not (last and ee)
                        b = 1 - ee
                        if more:
                            dve.wait_ge(*at(m + f"bc{b}", 16 * i + 16 * (1 + ee)))
                            column(b, 2 * i + ee + 1)
                        for f in range(8):
                            dve.wait_ge(*at(m + "sg", 16 * i + 8 * ee + f + 1))
                            tt(hid[:, f, :], sg[f % 2], ps[:, 3 + f % 2, CAP:2 * CAP], ALU.mult
                               ).then_inc(s(m + "hid"), 1)
                            if more:
                                for t in ((0, 8), (1, 2), (3, 4), (5, 6), (7,), (), (), ())[f]:
                                    rank_tile(b, t)
                                if f == 5:
                                    finish_rank(2 * i + ee + 1)
                                if f == 6:
                                    dve.wait_ge(*at(m + "ix", 2 * i + ee + 2))
                                    dve.wait_ge(*at(m + "scattered", 2 * i + ee))
                                    found(b, 0)
                        if more:
                            columns_in(b, 6 * i + 3 * ee + 3)
                        else:
                            dve.wait_ge(*at(m + "scattered", 2 * i + ee))
                        for g in range(2):
                            dve.wait_ge(*at(m + "to", 4 * i + 2 * ee + g + 1))
                            n = CAPL if g == 0 else CAPC
                            dst = orow[ee] if g == 0 else orowc[ee]
                            b0 = 5 if g == 0 else 0
                            ts(dst, bank(b0, 2)[0:n, :], gate[0:n, ee, g:g + 1], None, ALU.mult
                               ).then_inc(s(m + "rows"), 1)
                each_expert_pair(dve, [ch], [per], pair)

            def rope():
                tmp = va[:, 0, :]
                swap = [(i + 16) % 32 for i in range(32)]
                dve.wait_ge(*at("a.rope", 16))
                for j in range(16):
                    dve.wait_ge(*at("q.ev", j + 1))
                    v = (qTa if j < 8 else kTa)[:, j % 8, 0:LAT]
                    ch(nc.vector.stream_shuffle(tmp, v, swap))
                    tt(tmp, tmp, sinT, ALU.mult)
                    ch(tt(v, v, cosT, ALU.mult))
                    tt(v, v, tmp, ALU.add).then_inc(s("q.rope"), 1)
                    dve.wait_ge(*at("q.rope", j + 1))

            def attention():
                def maxima(n):
                    h, q = steps[n]
                    w = NT if q < 8 else P
                    c = (n % 4) * 8
                    for m in range(2):
                        dve.wait_ge(*at("a.s", 2 * n + m + 1))
                        ch(nc.vector.tensor_reduce(gstf[:, c + m:c + m + 1], bank(3 * m, 3)[:, 0:w], AX.X, ALU.max))
                        ts(gstf[:, c + 2 + m:c + 3 + m], gstf[:, c + m:c + m + 1], -0.125, None, ALU.mult
                           ).then_inc(s("a.nm"), 1)

                def norm_head(h):
                    dve.wait_ge(*at("a.std", h + 1))
                    ch(rec(gstf[:, 60:69], gstf[:, 48:57]))
                    r = gstf[:, 60:69].rearrange("p (t o) -> p t o", o=1).to_broadcast([P, T, P])
                    tt(ohs[h % 2], ohs[h % 2], r, ALU.mult).then_inc(s("a.on"), 1)
                    dve.wait_ge(*at("a.on", h + 1))

                def mix(n):
                    w = NT if steps[n][1] < 8 else P
                    c = (n % 4) * 8
                    dve.wait_ge(*at("a.e", 2 * n + 2))
                    ch(rec(gstf[:, c + 6:c + 8], gstf[:, c + 4:c + 6]))
                    ch(tt(gstf[:, c + 7:c + 8], gstf[:, c + 7:c + 8], lamc[:, 4:5], ALU.mult))
                    e0, e1 = eb[:, n % 2, 0, 0:w], eb[:, n % 2, 1, 0:w]
                    ch(ts(e0, e0, gstf[:, c + 6:c + 7], None, ALU.mult))
                    stt(e0, e1, gstf[:, c + 7:c + 8], e0, ALU.mult, ALU.add).then_inc(s("a.a"), 1)

                maxima(0)
                maxima(1)
                mix(0)
                for n, (h, q) in enumerate(steps):
                    if n + 1 < len(steps):
                        mix(n + 1)
                    if n + 2 < len(steps):
                        maxima(n + 2)
                    if q == head_step - 1 and h:
                        norm_head(h - 1)
                    dve.wait_ge(*at("a.pv", n + 1))
                    if q == 0 and h >= 2:
                        dve.wait_ge(*at("a.tev", head_tev[h - 2]))
                    o = ohs[h % 2]
                    cp(o[:, q, :], ps[:, 7, 0:P]).then_inc(s("a.oev"), 1)
                    dve.wait_ge(*at("a.oev", n + 1))
                    ch(stt(junk2, o[:, q, :], 1.0, o[:, q, :], ALU.mult, ALU.mult, accum_out=gstf[:, 36 + q:37 + q]))
                    if q == 8:
                        ts(gstf[:, 48:57], gstf[:, 36:45], 1.0 / P, EPS, ALU.mult, ALU.add).then_inc(s("a.var"), 1)
                        dve.wait_ge(*at("a.var", h + 1))
                norm_head(AH - 1)
                dve.wait_ge(*at("a.on", AH))
                dve.sem_inc(s("m1.big_free"), 1)

            norm("n10.", 0, 0, at_first)
            decays()
            short_conv()
            retention()
            hyena()
            dve.wait_ge(*at("h.z", 8))
            dve.sem_inc(s("m0.big_free"), 1)
            out_project(0)
            norm("n20.", 0, 1, begin=2)
            experts(0, 52)
            norm("n11.", 1, 0)
            rope()
            attention()
            out_project(1)
            norm("n21.", 1, 1, begin=2)
            experts(1, 52)
            dve.wait_ge(*at("z.g", 16))
            for k, tiles in enumerate(by_three):
                rstd("z.", k, tiles)
                for t in tiles:
                    stt(XN[:, t, :], X[:, t, :], stat[:, 1, t:t + 1], misc[:, 0:1024], ALU.mult, ALU.mult
                        ).then_inc(s("z.y"), 1)


_OUTS = [(1, CTX, D), (1, LAT, D), (1, 1, 2, RH, P, P), (1, 1, CTX, AH, P), (1, 1, CTX, AH, P)]


def kernel(**inputs):
    import concourse.bacc as bacc
    from concourse.bass_utils import run_bass_kernel_spmd

    nc = bacc.Bacc("TRN2", target_bir_lowering=False, num_devices=1, dynamic_dma_scratch_size=SCRATCH)
    arrays, a, tab = {}, {}, {}
    for name, v in inputs.items():
        arrays["in_" + name] = np.ascontiguousarray(v)
        a[name] = nc.dram_tensor("in_" + name, v.shape, F32, kind="ExternalInput").ap()
    for name, v in tables().items():
        arrays["tab_" + name] = v
        tab[name] = nc.dram_tensor("tab_" + name, v.shape, F32, kind="ExternalInput").ap()
    out = [nc.dram_tensor(f"out_{i}", shape, F32, kind="ExternalOutput").ap() for i, shape in enumerate(_OUTS)]
    build(nc, a, out, tab)
    r = run_bass_kernel_spmd(nc, [arrays], core_ids=[0])
    return tuple(r.results[0][f"out_{i}"] for i in range(len(_OUTS)))
```
